# Optimizing a Trainium2 kernel written in Bass

```python
import math
import jax, jax.numpy as jnp
from jax import lax
import numpy as np

D_MODEL = 1024
BATCH = 1
SEQ = 512
DEPTH = 2
DEC_BATCH = 8
DEC_SEQ = 1
PAST_LEN = 256
PAGE_SIZE = 128

N_MIXERS = 2
N_ATTN_LAYERS = (DEPTH + 1) // 2
N_CONV_LAYERS = DEPTH // 2
ATT_HEADS = 8
ATT_HD = 64
ATT_KD = 2 * ATT_HD
ATT_VD = 2 * ATT_HD
Q_BLOCK = 128
CONV_W = 3
PEER_HEADS = 8
PEER_DK = 256
N_KEYS = 128
N_EXPERTS = N_KEYS * N_KEYS
PEER_TOPK = 16
PEER_BLOCK = 128
PLE_DIM = 256
DN_ALPHA = (2 * DEPTH) ** 0.25
DN_BETA = (8 * DEPTH) ** -0.25
LN_EPS = 1e-5
SUBLN_EPS = 1e-5
NEG_INF = -1e30

kernel_name = "diffattn_shortconv_peer_hybrid_step"

def layer_norm(x, g, b):
    xf = x.astype(jnp.float32)
    mu = jnp.mean(xf, axis=-1, keepdims=True)
    var = jnp.mean(jnp.square(xf - mu), axis=-1, keepdims=True)
    return ((xf - mu) * lax.rsqrt(var + LN_EPS) * g + b).astype(x.dtype)

def alibi_slopes():
    return jnp.exp2(-8.0 * jnp.arange(1, ATT_HEADS + 1, dtype=jnp.float32) / ATT_HEADS)

def diff_logits(q, k, q_pos, k_pos):
    s = jnp.einsum('bqhcd,bkhcd->bchqk', q, k, preferred_element_type=jnp.float32)
    s = s * (ATT_HD ** -0.5)
    dist = (q_pos[:, None] - k_pos[None, :]).astype(jnp.float32)
    s = s - alibi_slopes()[:, None, None] * dist
    return jnp.where(dist >= 0, s, NEG_INF)

def diff_weights(logits, lam):
    p = jax.nn.softmax(logits, axis=-1)
    return p[:, 0] - lam * p[:, 1]

def diff_lambda(w_lam, lam_init):
    wl = w_lam.astype(jnp.float32)
    return jnp.exp(jnp.sum(wl[0] * wl[1])) - jnp.exp(jnp.sum(wl[2] * wl[3])) + lam_init

def attn_project(x, w_qkv):
    b, s, _ = x.shape
    qkv = x @ w_qkv
    w = ATT_HEADS * ATT_KD
    q = qkv[..., :w].reshape(b, s, ATT_HEADS, 2, ATT_HD)
    k = qkv[..., w:2 * w].reshape(b, s, ATT_HEADS, ATT_KD)
    v = qkv[..., 2 * w:].reshape(b, s, ATT_HEADS, ATT_VD)
    return q, k, v

def attn_finish(o, subln_g, w_o, lam_init, dtype):
    o = o * lax.rsqrt(jnp.mean(jnp.square(o), axis=-1, keepdims=True) + SUBLN_EPS)
    o = o * subln_g * (1.0 - lam_init)
    b, q = o.shape[:2]
    return o.reshape(b, q, -1).astype(dtype) @ w_o

def diff_attn_prompt(x, w_qkv, w_lam, subln_g, w_o, lam_init):
    b, s, _ = x.shape
    q, k, v = attn_project(x, w_qkv)
    k5 = k.reshape(b, s, ATT_HEADS, 2, ATT_HD)
    lam = diff_lambda(w_lam, lam_init)
    k_pos = jnp.arange(s)

    def block(i):
        start = i * Q_BLOCK
        qb = lax.dynamic_slice_in_dim(q, start, Q_BLOCK, axis=1)
        q_pos = start + jnp.arange(Q_BLOCK)
        w = diff_weights(diff_logits(qb, k5, q_pos, k_pos), lam).astype(v.dtype)
        return jnp.einsum('bhqk,bkhv->bqhv', w, v, preferred_element_type=jnp.float32)

    o = lax.map(block, jnp.arange(s // Q_BLOCK))
    o = jnp.moveaxis(o, 0, 1).reshape(b, s, ATT_HEADS, ATT_VD)
    return attn_finish(o, subln_g, w_o, lam_init, x.dtype), k, v

def diff_attn_sample(x, cache_k, cache_v, layer, page_table, w_qkv, w_lam, subln_g, w_o, lam_init):
    b, s, _ = x.shape
    q, k, v = attn_project(x, w_qkv)
    lam = diff_lambda(w_lam, lam_init)
    past = page_table.shape[1] * cache_k.shape[2]
    k_past = cache_k[layer, page_table].reshape(b, past, ATT_HEADS, 2, ATT_HD)
    v_past = cache_v[layer, page_table].reshape(b, past, ATT_HEADS, ATT_VD)
    q_pos = past + jnp.arange(s)
    logits = jnp.concatenate([
        diff_logits(q, k_past, q_pos, jnp.arange(past)),
        diff_logits(q, k.reshape(b, s, ATT_HEADS, 2, ATT_HD), q_pos, q_pos)], axis=-1)
    w = diff_weights(logits, lam).astype(x.dtype)
    o = (jnp.einsum('bhqk,bkhv->bqhv', w[..., :past], v_past, preferred_element_type=jnp.float32)
         + jnp.einsum('bhqk,bkhv->bqhv', w[..., past:], v, preferred_element_type=jnp.float32))
    return attn_finish(o, subln_g, w_o, lam_init, x.dtype), k, v

def short_conv(x, left, w_in, conv_w, w_out):
    s = x.shape[1]
    b_g, c_g, h = jnp.split(x @ w_in, 3, axis=-1)
    u = c_g * h
    u_ext = jnp.concatenate([left.astype(u.dtype), u], axis=1)
    z = conv_w[0] * u_ext[:, 0:s]
    for j in range(1, CONV_W):
        z = z + conv_w[j] * u_ext[:, j:j + s]
    return (b_g * z) @ w_out, u_ext[:, -(CONV_W - 1):]

def peer_ffn(x, w_q, keys, u_tab, v_tab):
    shp = x.shape
    x2 = x.reshape(-1, shp[-1])
    t = x2.shape[0]
    pad = (-t) % PEER_BLOCK
    x2 = jnp.pad(x2, ((0, pad), (0, 0)))
    xb = x2.reshape(-1, PEER_BLOCK, shp[-1])

    def block(xt):
        q = (xt @ w_q).reshape(PEER_BLOCK, PEER_HEADS, 2, PEER_DK // 2)
        s = jnp.einsum('thcd,hcnd->thcn', q, keys, preferred_element_type=jnp.float32)
        sv, si = lax.top_k(s, PEER_TOPK)
        cand_s = (sv[:, :, 0, :, None] + sv[:, :, 1, None, :]).reshape(PEER_BLOCK, PEER_HEADS, PEER_TOPK ** 2)
        cand_i = (si[:, :, 0, :, None] * N_KEYS + si[:, :, 1, None, :]).reshape(PEER_BLOCK, PEER_HEADS, PEER_TOPK ** 2)
        top_s, top_p = lax.top_k(cand_s, PEER_TOPK)
        idx = jnp.take_along_axis(cand_i, top_p, axis=-1)
        g = jax.nn.softmax(top_s, axis=-1)
        a = jnp.einsum('td,thkd->thk', xt, u_tab[idx], preferred_element_type=jnp.float32)
        hk = (g * jax.nn.gelu(a, approximate=False)).astype(xt.dtype)
        return jnp.einsum('thk,thkd->td', hk, v_tab[idx])

    out = lax.map(block, xb).reshape(-1, shp[-1])[:t]
    return out.reshape(shp)

def ple_add(h, p, w_gate, w_proj):
    return h + jax.nn.sigmoid(h @ w_gate) * (p @ w_proj)

def setup_inputs(seed: int = 0) -> dict:
    key = jax.random.key(seed)
    ks = jax.random.split(key, 26)
    f32 = jnp.float32
    n_pages = PAST_LEN // PAGE_SIZE
    used = DEC_BATCH * n_pages
    pool = used + max(1, used // 4)

    def nrm(k, shape, scale):
        return scale * jax.random.normal(k, shape, f32)

    hw = ATT_HEADS * ATT_KD
    qkv_scale = jnp.concatenate([jnp.ones((2 * hw,), f32), jnp.full((ATT_HEADS * ATT_VD,), DN_BETA, f32)])
    return {
        "x_prompt": nrm(ks[0], (BATCH, SEQ, D_MODEL), 1.0),
        "x_sample": nrm(ks[1], (DEC_BATCH, DEC_SEQ, D_MODEL), 1.0),
        "cache_k": nrm(ks[2], (N_ATTN_LAYERS, pool, PAGE_SIZE, ATT_HEADS, ATT_KD), 1.0),
        "cache_v": nrm(ks[3], (N_ATTN_LAYERS, pool, PAGE_SIZE, ATT_HEADS, ATT_VD), DN_BETA),
        "state_conv": nrm(ks[4], (N_CONV_LAYERS, DEC_BATCH, CONV_W - 1, D_MODEL), 1.0),
        "page_table": jax.random.permutation(ks[5], pool)[:used].reshape(DEC_BATCH, n_pages).astype(jnp.int32),
        "p_prompt": nrm(ks[6], (DEPTH, BATCH, SEQ, PLE_DIM), 1.0),
        "p_sample": nrm(ks[7], (DEPTH, DEC_BATCH, DEC_SEQ, PLE_DIM), 1.0),
        "ln_g": 1.0 + nrm(ks[8], (DEPTH, 2, D_MODEL), 0.02),
        "ln_b": nrm(ks[9], (DEPTH, 2, D_MODEL), 0.02),
        "w_attn_qkv": nrm(ks[10], (N_ATTN_LAYERS, D_MODEL, 2 * hw + ATT_HEADS * ATT_VD), D_MODEL ** -0.5) * qkv_scale,
        "w_attn_lambda": nrm(ks[11], (N_ATTN_LAYERS, 4, ATT_HD), 0.1),
        "attn_subln_g": 1.0 + nrm(ks[12], (N_ATTN_LAYERS, ATT_VD), 0.02),
        "w_attn_o": nrm(ks[13], (N_ATTN_LAYERS, ATT_HEADS * ATT_VD, D_MODEL), DN_BETA * (ATT_HEADS * ATT_VD) ** -0.5),
        "w_conv_in": nrm(ks[14], (N_CONV_LAYERS, D_MODEL, 3 * D_MODEL), D_MODEL ** -0.5),
        "conv_w": nrm(ks[15], (N_CONV_LAYERS, CONV_W, D_MODEL), CONV_W ** -0.5),
        "w_conv_out": nrm(ks[16], (N_CONV_LAYERS, D_MODEL, D_MODEL), DN_BETA * D_MODEL ** -0.5),
        "w_peer_q": nrm(ks[17], (DEPTH, D_MODEL, PEER_HEADS * PEER_DK), D_MODEL ** -0.5),
        "peer_keys": nrm(ks[18], (DEPTH, PEER_HEADS, 2, N_KEYS, PEER_DK // 2), (PEER_DK // 2) ** -0.5),
        "peer_u": nrm(ks[19], (DEPTH, N_EXPERTS, D_MODEL), D_MODEL ** -0.5),
        "peer_v": nrm(ks[20], (DEPTH, N_EXPERTS, D_MODEL), DN_BETA),
        "w_ple_gate": nrm(ks[21], (DEPTH, D_MODEL, D_MODEL), D_MODEL ** -0.5),
        "w_ple_proj": nrm(ks[22], (DEPTH, PLE_DIM, D_MODEL), PLE_DIM ** -0.5),
    }

def reference(x_prompt, x_sample, cache_k, cache_v, state_conv, page_table, p_prompt, p_sample,
              ln_g, ln_b, w_attn_qkv, w_attn_lambda, attn_subln_g, w_attn_o,
              w_conv_in, conv_w, w_conv_out, w_peer_q, peer_keys, peer_u, peer_v,
              w_ple_gate, w_ple_proj):
    hp, hs = x_prompt, x_sample
    kp_l, vp_l, ks_l, vs_l, cp_l, cs_l = [], [], [], [], [], []
    for i in range(DEPTH):
        j = i // N_MIXERS
        if i % N_MIXERS == 0:
            lam_init = 0.8 - 0.6 * math.exp(-0.3 * i)
            yp, kp, vp = diff_attn_prompt(hp, w_attn_qkv[j], w_attn_lambda[j], attn_subln_g[j], w_attn_o[j], lam_init)
            ys, kn, vn = diff_attn_sample(hs, cache_k, cache_v, j, page_table, w_attn_qkv[j], w_attn_lambda[j],
                                          attn_subln_g[j], w_attn_o[j], lam_init)
            kp_l.append(kp); vp_l.append(vp); ks_l.append(kn); vs_l.append(vn)
        else:
            zeros_left = jnp.zeros((hp.shape[0], CONV_W - 1, hp.shape[2]), hp.dtype)
            yp, cp = short_conv(hp, zeros_left, w_conv_in[j], conv_w[j], w_conv_out[j])
            ys, cs = short_conv(hs, state_conv[j], w_conv_in[j], conv_w[j], w_conv_out[j])
            cp_l.append(cp); cs_l.append(cs)
        hp = layer_norm(DN_ALPHA * hp + yp, ln_g[i, 0], ln_b[i, 0])
        hs = layer_norm(DN_ALPHA * hs + ys, ln_g[i, 0], ln_b[i, 0])
        hp = layer_norm(DN_ALPHA * hp + peer_ffn(hp, w_peer_q[i], peer_keys[i], peer_u[i], peer_v[i]), ln_g[i, 1], ln_b[i, 1])
        hs = layer_norm(DN_ALPHA * hs + peer_ffn(hs, w_peer_q[i], peer_keys[i], peer_u[i], peer_v[i]), ln_g[i, 1], ln_b[i, 1])
        hp = ple_add(hp, p_prompt[i], w_ple_gate[i], w_ple_proj[i])
        hs = ple_add(hs, p_sample[i], w_ple_gate[i], w_ple_proj[i])
    return (hp, hs, jnp.stack(kp_l), jnp.stack(vp_l), jnp.stack(ks_l), jnp.stack(vs_l),
            jnp.stack(cp_l), jnp.stack(cs_l))


_drawn_inputs = setup_inputs


def setup_inputs(seed=0):
    import zlib

    import numpy as np

    out = dict(_drawn_inputs(seed))
    spreads = {}
    factors = {}
    for name, (base, spread) in spreads.items():
        noise = np.random.default_rng([zlib.crc32(name.encode()), seed]).standard_normal(out[name].shape)
        drawn = base * np.exp(spread * noise) if base else spread * noise
        out[name] = __import__('jax').numpy.asarray(drawn.astype(out[name].dtype))
    for name, factor in factors.items():
        out[name] = (out[name] * factor).astype(out[name].dtype)
    return out
```

```python
import math
from contextlib import ExitStack

import numpy as np

import concourse.bass as bass
from concourse import mybir

ALU = mybir.AluOpType
ACT = mybir.ActivationFunctionType
F32 = mybir.dt.float32
I32 = mybir.dt.int32
U32 = mybir.dt.uint32
AX_X = mybir.AxisListType.X

P = 128
D = 1024
C = D // P
SEQ = 512
NS = 8
T = SEQ + NS
TB = SEQ // P
BLOCKS = TB + 1
HEADS = 8
HD = 64
PAGE = 128
N_PAGES = 2
PAST = PAGE * N_PAGES
POOL_PAGES = 20
TOPK = 16
KEYS = 128
EXPERTS = KEYS * KEYS
PLE = 256
DEPTH = 2
ALPHA = (2 * DEPTH) ** 0.25
LAM_INIT = 0.8 - 0.6 * math.exp(0.0)
EPS = 1e-5
NEG = -1e30
LOWEST = -3.0e38
SCALE = HD ** -0.5
SLOPES = [2.0 ** -(h + 1) for h in range(HEADS)]
RING = 8
GROUPS = TB * HEADS * 2 + 1
DIAGS = 4

PN_QK, PN_V, PN_O, PN_PQ, PN_GATE, PN_PROJ = 0, 4, 6, 8, 12, 14
PN_CONV, PN_COUT, PN_PQ1, PN_GATE1, PN_PROJ1 = 15, 23, 25, 29, 31
PANELS = 32

USES = [
    ("qk", 16), ("v", BLOCKS), ("k_rows", BLOCKS), ("q_rows", 1), ("q_spread", NS), ("s_turn", 1), ("p_turn", 1),
    ("s_out", 1), ("attn", TB * HEADS), ("subln", HEADS), ("mix0", BLOCKS), ("turn0", BLOCKS), ("pq0", 16),
    ("x_spread0", 1), ("i_spread0", 1), ("turn_a0", BLOCKS), ("ple0", 2 * BLOCKS), ("turn_b0", BLOCKS),
    ("conv", 24), ("mix1", BLOCKS), ("turn1", BLOCKS), ("pq1", 16),
    ("x_spread1", 1), ("i_spread1", 1), ("turn_a1", BLOCKS), ("ple1", 2 * BLOCKS),
]
BASE = {}
_n = 0
for _name, _count in USES:
    BASE[_name] = _n
    _n += _count

CONST = [("ident", P), ("alpha_eye", P), ("group_of", P), ("spread", P), ("kmask", TOPK), ("iota", TOPK)]
ATTN_CONST = [("dist", SEQ), ("bias_s", PAST + NS), ("pick", NS * P), ("own", NS), ("mean", P), ("second", 1)]


def columns(parts):
    at, out = 0, {}
    for name, width in parts:
        out[name] = (at, at + width)
        at += width
    return out, at


CC, N_CONST = columns(CONST)
AC, N_ATTN = columns(ATTN_CONST)


def constants():
    p = np.arange(P)
    a = np.zeros((P, N_CONST + N_ATTN), np.float32)

    def put(cols, off, v):
        a[:v.shape[0], off + cols[0]:off + cols[1]] = v

    put(CC["ident"], 0, np.eye(P))
    put(CC["alpha_eye"], 0, np.eye(P) * ALPHA)
    put(CC["group_of"], 0, (p[:, None] // TOPK == p[None, :]).astype(np.float32))
    put(CC["spread"], 0, (np.arange(NS)[:, None] == p[None, :] // TOPK).astype(np.float32))
    put(CC["kmask"], 0, (p[:, None] % TOPK == np.arange(TOPK)[None, :]).astype(np.float32))
    put(CC["iota"], 0, np.tile(np.arange(TOPK), (P, 1)))
    j = np.arange(SEQ)
    dist = p[:, None] + (SEQ - P) - j[None, :]
    put(AC["dist"], N_CONST, np.where(dist >= 0, -dist, NEG))
    slope = np.array(SLOPES)[(p // 2) % HEADS] / SCALE
    bias = np.zeros((P, PAST + NS))
    bias[:, :PAST] = -slope[:, None] * (PAST - np.arange(PAST))[None, :]
    put(AC["bias_s"], N_CONST, bias)
    pick = np.zeros((NS, NS, P))
    for b in range(NS):
        pick[b, b] = 1
    put(AC["pick"], N_CONST, pick.reshape(NS, NS * P))
    put(AC["own"], N_CONST, np.where(np.eye(NS) > 0, 0, NEG))
    put(AC["mean"], N_CONST, np.full((P, P), 1 / P))
    put(AC["second"], N_CONST, (p % 2)[:, None])
    return a


def rows(b):
    return P if b < TB else NS


def freed(n):
    return n // 2 + 1


def build(nc, h0, h0T, consts, panels, keysT, uv0, uv1, cache_k, cache_v, pages, wlam, subg, ln, convw,
          state_conv, stateT, y_p, y_s, nk_p, nv_p, nk_s, nv_s, cp, cs):
    uv_dram = [uv0, uv1]
    ctx = ExitStack()
    with ctx:
        def sb(name, shape, dt=F32):
            return ctx.enter_context(nc.sbuf_tensor(name, shape, dt))

        def sem(name):
            return ctx.enter_context(nc.semaphore(name))

        h = sb("h", [P, BLOCKS, D])
        hT = sb("hT", [P, C, T])
        QTN = 16 * T
        qT = sb("qT", [P, QTN + P - NS])
        qT3 = qT[:, 0:QTN].rearrange("p (f t) -> p f t", t=T)
        qT4 = qT[:, 0:QTN].rearrange("p (i f t) -> p i f t", f=8, t=T)
        sig = qT[:, 0:BLOCKS * D].rearrange("p (b n) -> p b n", b=BLOCKS)
        keys = sb("keys", [P, 16, KEYS])
        arena = sb("arena", [P, RING * 2 * D])
        uv = arena[:].rearrange("p (r n) -> p r n", r=RING)
        panel = sb("panel", [P, 2, C * 512])
        xcur = sb("xcur", [P, D])
        ya = sb("ya", [P, D])
        yb = sb("yb", [P, D])
        lng = sb("lng", [P, D])
        lnb = sb("lnb", [P, D])
        idx = sb("idx", [P, BLOCKS, HEADS, TOPK], I32)
        gate = sb("gate", [P, BLOCKS, HEADS, TOPK])
        diag = sb("diag", [P, DIAGS, P])
        qst = sb("qst", [P, 2 * P])
        cst = sb("cst", [P, N_CONST])
        ixst = sb("ixst", [P, 2, RING], I32)
        dots = sb("dots", [P, 2, RING])
        act_w = sb("act_w", [P, 3, 2, RING])
        small = sb("small", [P, 64])
        state = sb("state", [P, C, 2, NS])
        cw = sb("cw", [P, 3, C])

        def const(name):
            return cst[:, CC[name][0]:CC[name][1]]

        at = [0]

        def part(n):
            at[0] += n
            return arena[:, at[0] - n:at[0]]

        v_rows = part(BLOCKS * D).rearrange("p (b n) -> p b n", b=BLOCKS)
        oT = part(C * T).rearrange("p (c t) -> p c t", c=C)
        kv_pages = part(4 * D).rearrange("p (i j n) -> p i j n", i=2, j=2)
        logit = kv_pages[:, 0].rearrange("p j (c n) -> p j c n", c=2)
        wrow = kv_pages[:, 1, 0].rearrange("p (j n) -> p j n", j=2)
        wT = kv_pages[:, 1, 1].rearrange("p (j n) -> p j n", j=2)
        attn_c = part(N_ATTN)
        wl = part(4 * HD)
        s_pos = part(2 * P).rearrange("p (j n) -> p j n", j=2)
        s_new = part(P)

        def aconst(name):
            return attn_c[:, AC[name][0]:AC[name][1]]

        UW = T + 2
        uT = arena[:, 0:C * UW].rearrange("p (c t) -> p c t", c=C)
        gz = arena[:, C * UW:C * (UW + T)].rearrange("p (c t) -> p c t", c=C)
        o = C * (UW + T)
        c_st = arena[:, o:o + 2 * T].rearrange("p (j t) -> p j t", j=2)
        z = arena[:, o + 2 * T:o + 3 * T]

        r_sc = yb[:, 0:256]
        r_wk = yb[:, 256:512]
        r_eq = yb[:, 512:1024]
        r_cand = ya[:, 0:256]
        r_v = ya[:, 256:288]
        r_si = ya[:, 288:320].bitcast(U32)
        r_sif = ya[:, 320:352]
        r_tv = ya[:, 352:368]
        r_ti = ya[:, 368:384].bitcast(U32)
        r_ij = ya[:, 384:416].bitcast(U32)
        r_ijf = ya[:, 416:448]
        r_e = ya[:, 448:480]
        r_nm = ya[:, 480:481]
        r_ex = ya[:, 496:512]
        r_sum = ya[:, 512:513]
        r_inv = ya[:, 513:514]
        x_ig = yb[:, 0:256]
        x_pr = yb[:, 256:512]
        x_sel = ya[:, 640:656]

        stats = small[:, 0:12].rearrange("p (a s) -> p a s", a=2)
        mv = small[:, 12:14]
        rstd = small[:, 14:15]
        lam2 = small[:, 16:18]
        lam_e = small[:, 18:20]
        neglam = small[:, 20:21]
        coef = small[:, 21:22]
        gsub = small[:, 22:23]
        subg_sb = small[:, 23:24]
        mx = small[:, 24:28].rearrange("p (j c) -> p j c", j=2)
        nb = small[:, 28:32].rearrange("p (j c) -> p j c", j=2)
        lsum = small[:, 32:36].rearrange("p (j c) -> p j c", j=2)
        linv = small[:, 36:40].rearrange("p (j c) -> p j c", j=2)
        smx, snb, ssum, sinv = (small[:, 40 + i:41 + i] for i in range(4))
        ixs = small[:, 44:52].bitcast(I32)
        gs8 = small[:, 52:60]
        eps = small[:, 60:61]
        pg = sb("pg", [1, NS * N_PAGES], I32)

        pj = [ctx.enter_context(nc.psum_tensor(f"pj{i}", [P, 1024], F32)) for i in range(2)]
        acc = ctx.enter_context(nc.psum_tensor("acc", [P, 1024], F32))
        tp = [ctx.enter_context(nc.psum_tensor(f"tp{i}", [P, 512], F32)) for i in range(2)]

        s_const = sem("const_in")
        s_attn_c = sem("attn_const_in")
        s_h = sem("h_in")
        s_hT = sem("hT_in")
        s_keys = sem("keys_in")
        s_small = sem("small_in")
        s_pages = sem("page_ids_in")
        s_zero = sem("zeroed")
        s_panel = [sem(f"panel_in{i}") for i in range(2)]
        s_ln = sem("ln_params_in")
        s_pair = [sem(f"page_pair_in{i}") for i in range(2)]
        full = sem("proj_full")
        free = [sem(f"proj_free{i}") for i in range(2)]
        k_out = [sem(f"k_rows_stored{i}") for i in range(3)]
        v_out = sem("v_rows_stored")
        kpair_used = sem("k_pair_used")
        vpair_used = sem("v_pair_used")
        lam_sums = sem("lambda_sums")
        lam_exps = sem("lambda_exps")
        s_scores = sem("sample_scores")
        s_bias_done = sem("sample_logits")
        s_exp_done = sem("sample_exps")
        s_probs = sem("sample_probs")
        s_wT = sem("sample_weights_turned")
        a_logits = sem("logits_ready")
        a_exps = sem("exps_ready")
        a_w = sem("weights_ready")
        a_wT_ps = sem("weights_turned")
        a_wT = sem("turned_weights_ready")
        a_o = sem("attn_out_full")
        a_ofree = sem("attn_out_free")
        sq_ready = sem("squares_ready")
        o_normed = sem("attn_out_normed")
        var_ready = sem("variance_ready")
        std_ready = sem("deviation_ready")
        rms_ready = sem("rms_ready")
        ln_done = sem("ln_done")
        ple_done = sem("ple_done")
        c_ready = sem("conv_c_ready")
        c_used = sem("conv_c_used")
        gz_ready = sem("conv_out_ready")
        conv_out = sem("conv_state_stored")
        conv_copy = sem("conv_state_copied")
        q_staged = sem("q_staged")
        sc_ready = sem("key_scores_ready")
        sc_read = sem("key_scores_read")
        top_ready = sem("top_ready")
        gexp_done = sem("gate_exps")
        idx_done = sem("expert_ids")
        g_done = sem("gates_ready")
        ix_ready = sem("ids_staged")
        gathered = [sem(f"gathered{r}") for r in range(RING)]
        dot_done = sem("dots_done")
        gelu_done = sem("gelu_done")
        diag_ready = sem("diag_ready")
        slot_done = sem("slots_done")
        x_ready = sem("x_staged")
        acc_free = sem("acc_free")
        ig_ready = sem("sample_ids_rows")
        ixs_ready = sem("sample_ids_spread")
        y_out = sem("y_stored")
        turn = {e: sem(f"turn_{e}") for e in ("act", "pool", "dve")}

        SEED_SLOTS = RING
        SEED_GELU = 4

        block = ctx.enter_context(nc.Block())

        def rms_buf(hd):
            return (wrow, wT)[hd % 2].rearrange("p j n -> p (j n)")[:, 0:T]

        def all_read(eng, n):
            for p in range(2):
                eng.wait_ge(free[p], (n - p + 1) // 2 + 1)

        @block.sync
        def _(sp):
            sp.dma_start(hT[:], h0T).then_inc(s_hT, 16)
            last = {}
            for name, first, per, count in (("qk", PN_QK, 4, 4), ("pq0", PN_PQ, 4, 4), ("pq1", PN_PQ1, 4, 4),
                                            ("conv", PN_CONV, 3, 8)):
                for i in range(count):
                    last[first + i] = BASE[name] + per * (i + 1)
            for name, first in (("v", PN_V), ("mix0", PN_O), ("mix1", PN_COUT)):
                last[first] = last[first + 1] = BASE[name] + BLOCKS
            for name, first in (("ple0", PN_GATE), ("ple1", PN_GATE1)):
                last[first] = last[first + 1] = BASE[name] + BLOCKS
                last[first + 2] = BASE[name] + 2 * BLOCKS

            def load_panel(i):
                if i >= 2:
                    sp.wait_ge(full, last[i - 2])
                sp.dma_start(panel[:, i % 2, :], panels[i]).then_inc(s_panel[i % 2], 16)

            def load_ln(k):
                if k == 0:
                    for i in range(2):
                        sp.wait_ge(k_out[i], 32)
                else:
                    sp.wait_ge(ln_done, BLOCKS * k)
                sp.dma_start(lng[:], ln[k, 0:1, :].broadcast_to([P, D])).then_inc(s_ln, 16)
                sp.dma_start(lnb[:], ln[k, 1:2, :].broadcast_to([P, D])).then_inc(s_ln, 16)

            load_panel(0)
            load_panel(1)
            sp.dma_start(cst[:], consts[:, 0:N_CONST]).then_inc(s_const, 16)
            sp.dma_start(attn_c, consts[:, N_CONST:N_CONST + N_ATTN]).then_inc(s_attn_c, 16)
            sp.dma_start(wl, wlam.broadcast_to([P, 4 * HD])).then_inc(s_small, 16)
            sp.dma_start(subg_sb, subg).then_inc(s_small, 16)
            sp.dma_start(cw[:], convw).then_inc(s_small, 16)
            sp.dma_start(state[:], stateT).then_inc(s_small, 16)
            sp.dma_start(h[:, 0:TB, :], h0[0:SEQ, :].rearrange("(b p) n -> p b n", p=P)).then_inc(s_h, 16)
            sp.wait_ge(s_zero, 1)
            sp.dma_start(h[0:NS, TB, :], h0[SEQ:T, :]).then_inc(s_h, 16)
            sp.dma_start(keys[:], keysT[0]).then_inc(s_keys, 16)
            for i in range(2, PN_PQ):
                load_panel(i)
            load_ln(0)
            for i in range(PN_PQ, PN_GATE):
                load_panel(i)
            load_ln(1)
            load_panel(PN_GATE)
            load_panel(PN_GATE + 1)
            sp.wait_ge(sc_ready, HEADS * BLOCKS + 1)
            sp.dma_start(keys[:], keysT[1]).then_inc(s_keys, 16)
            load_panel(PN_PROJ)
            load_panel(PN_CONV)
            load_panel(PN_CONV + 1)
            load_ln(2)
            for i in range(PN_CONV + 2, PN_GATE1):
                load_panel(i)
            load_ln(3)
            for i in range(PN_GATE1, PANELS):
                load_panel(i)
            for b in range(BLOCKS):
                sp.wait_ge(ple_done, BLOCKS + b + 1)
                dst = y_p[b * P:(b + 1) * P, :] if b < TB else y_s
                sp.dma_start(dst, h[0:rows(b), b, :]).then_inc(y_out, 16)
            sp.wait_ge(y_out, 16 * BLOCKS)
            sp.wait_ge(v_out, 16 * BLOCKS)
            sp.wait_ge(k_out[2], 16)
            sp.wait_ge(conv_out, 16 * 2 * C)
            sp.wait_ge(conv_copy, 16)

        @block.gpsimd
        def _(pool):
            pool.dma_start(pg[:], pages).then_inc(s_pages, 16)
            nc.gpsimd.memset(h[:, TB, :], 0.0).then_inc(s_zero, 1)
            nc.gpsimd.memset(qT[:, QTN:QTN + P - NS], 0.0).then_inc(s_zero, 1)
            pool.wait_ge(s_pages, 16)

            def load_pair(i):
                cache = cache_k if i < NS else cache_v
                if i >= 2:
                    pool.wait_ge(kpair_used, min(i - 1, NS))
                    if i - 2 >= NS:
                        pool.wait_ge(vpair_used, i - 1 - NS)
                for j in range(N_PAGES):
                    k = (i % NS) * N_PAGES + j
                    page = pool.value_load(pg[0:1, k:k + 1], min_val=0, max_val=POOL_PAGES - 1)
                    pool.dma_start(kv_pages[:, i % 2, j, :], cache[bass.ds(page, 1)].rearrange("a p n -> (a p) n")) \
                        .then_inc(s_pair[i % 2], 16)

            load_pair(0)
            load_pair(1)
            for b in range(BLOCKS):
                n = BASE["v"] + b
                pool.wait_ge(free[n % 2], freed(n) + 1)
                dst = nv_p[b * P:(b + 1) * P, :] if b < TB else nv_s
                pool.dma_start(dst, v_rows[0:rows(b), b, :]).then_inc(v_out, 16)
            for b in range(BLOCKS):
                n = BASE["k_rows"] + b
                pool.wait_ge(free[n % 2], freed(n) + 1)
                dst = nk_p[b * P:(b + 1) * P, :] if b < TB else nk_s
                src = (lng, lnb)[b % 2] if b < TB else ya
                pool.dma_start(dst, src[0:rows(b), :]).then_inc(k_out[b % 2 if b < TB else 2], 16)
            for i in range(2, 2 * NS):
                load_pair(i)

            def gather_group(layer, G, first, ids, ids_ready, count):
                half = first % 2
                pool.wait_ge(ids_ready, count)
                pool.sem_inc(turn["pool"], 1)
                nc.gpsimd.tensor_copy(ixst[:, half, :], ids).then_inc(ix_ready, 1)
                for r in range(RING):
                    if r == 0:
                        pool.wait_ge(ix_ready, G + 1)
                    pool.wait_ge(slot_done, G * RING + r + 1)
                    pool.sem_inc(turn["pool"], 1)
                    nc.gpsimd.indirect_dma_start(
                        uv[:, r, :], None, uv_dram[layer],
                        bass.IndirectOffsetOnAxis(ixst[:, half, r:r + 1], 0)).then_inc(gathered[r], 16)

            ids5 = idx[:].rearrange("p b h (a r) -> p b h a r", a=2)
            for layer in range(DEPTH):
                g0 = layer * GROUPS
                if layer == 1:
                    pool.dma_start(cs[:, 0, :], state_conv[:, 1, :]).then_inc(conv_copy, 16)
                    pool.wait_ge(gz_ready, C)
                    with nc.allow_non_contiguous_dma(reason="small state"):
                        for j in range(C):
                            pool.dma_start(cp[:, j * P:(j + 1) * P].rearrange("s p -> p s"),
                                           uT[:, j, SEQ:SEQ + 2]).then_inc(conv_out, 16)
                            pool.dma_start(cs[:, 1, j * P:(j + 1) * P].rearrange("s p -> p s"),
                                           uT[:, j, SEQ + 2:SEQ + 2 + NS]).then_inc(conv_out, 16)
                    pool.wait_ge(conv_out, 16 * 2 * C)
                with pool.Fori(0, TB) as b:
                    with pool.Fori(0, HEADS) as hd:
                        for half in range(2):
                            gather_group(layer, b * 16 + hd * 2 + (half + g0), g0 + half, ids5[:, b, hd, half, :],
                                         idx_done, b * HEADS + (BLOCKS * layer + 1) * HEADS)
                gather_group(layer, g0 + GROUPS - 1, g0 + GROUPS - 1, ixs, ixs_ready, layer + 1)

        @block.scalar
        def _(act):
            act.sem_inc(slot_done, SEED_SLOTS)
            act.sem_inc(free[0], 1)
            act.sem_inc(free[1], 1)
            act.sem_inc(acc_free, 1)
            act.sem_inc(a_ofree, 2)

            def features_out(base):
                with act.Fori(0, 2) as it:
                    for f in range(8):
                        n = base + f
                        act.wait_ge(full, it * 8 + (n + 1))
                        act.sem_inc(turn["act"], 1)
                        nc.scalar.activation(qT4[:, it, f, :], pj[n % 2][:, 0:T], ACT.Copy).then_inc(free[n % 2], 1)

            def turned_out(base):
                for b in range(BLOCKS):
                    n, m = base + b, rows(b)
                    act.wait_ge(full, n + 1)
                    nc.scalar.activation(hT[:, :, b * P:b * P + m],
                                         pj[n % 2][:].rearrange("p (c t) -> p c t", c=C)[:, :, 0:m],
                                         ACT.Copy).then_inc(free[n % 2], 1)

            features_out(BASE["qk"])
            for b in range(BLOCKS):
                n, m = BASE["v"] + b, rows(b)
                act.wait_ge(full, n + 1)
                nc.scalar.activation(v_rows[0:m, b, :], pj[n % 2][0:m, :], ACT.Copy).then_inc(free[n % 2], 1)
            act.wait_ge(lam_sums, 1)
            nc.scalar.activation(lam_e, lam2, ACT.Exp).then_inc(lam_exps, 1)
            act.wait_ge(s_bias_done, 1)
            nc.scalar.activation(yb[:, 0:PAST + NS], yb[:, 0:PAST + NS], ACT.Exp, bias=snb, scale=SCALE,
                                 accum_out=ssum).then_inc(s_exp_done, 1)
            n = BASE["s_out"]
            act.wait_ge(full, n + 1)
            nc.scalar.activation(oT[:, :, SEQ:T], pj[n % 2][:, 0:HEADS * NS].rearrange("p (h b) -> p h b", h=HEADS),
                                 ACT.Copy).then_inc(free[n % 2], 1)

            units = [(hd, i) for hd in range(HEADS) for i in range(TB)]
            for u in range(len(units) + 3):
                if u < len(units):
                    n = (units[u][1] + 1) * P
                    act.wait_ge(a_logits, u + 1)
                    for c in range(2):
                        e = nc.scalar.activation(logit[:, u % 2, c, 0:n], logit[:, u % 2, c, 0:n], ACT.Exp,
                                                 bias=nb[:, u % 2, c:c + 1], scale=SCALE,
                                                 accum_out=lsum[:, u % 2, c:c + 1])
                    e.then_inc(a_exps, 1)
                if 2 <= u <= len(units) + 1:
                    v, n = u - 2, (units[u - 2][1] + 1) * P
                    act.wait_ge(a_wT_ps, v + 1)
                    if v >= 2:
                        act.wait_ge(a_o, v - 1)
                    nc.scalar.activation(wT[:, v % 2, 0:n], tp[v % 2][:, 0:n], ACT.Copy).then_inc(a_wT, 1)
                if u >= 3:
                    v = u - 3
                    hd, i = units[v]
                    act.wait_ge(a_o, v + 1)
                    nc.scalar.activation(oT[:, hd, i * P:(i + 1) * P], acc[:, (v % 2) * 512:(v % 2) * 512 + P],
                                         ACT.Copy).then_inc(a_ofree, 1)
            act.drain()
            for hd in range(HEADS + 1):
                if hd < HEADS:
                    if hd >= 2:
                        act.wait_ge(full, BASE["subln"] + hd - 1)
                    nc.scalar.activation(logit[:, hd % 2].rearrange("p c n -> p (c n)")[:, 0:T], oT[:, hd, :],
                                         ACT.Square).then_inc(sq_ready, 1)
                if hd >= 1:
                    n = BASE["subln"] + hd - 1
                    act.wait_ge(full, n + 1)
                    if hd >= 3:
                        act.wait_ge(o_normed, hd - 2)
                    nc.scalar.activation(rms_buf(hd - 1), pj[n % 2][:, 0:T], ACT.Sqrt, bias=eps)
                    act.drain()
                    act.sem_inc(rms_ready, 1)
                    act.sem_inc(free[n % 2], 1)

            def deviations(k):
                for b in range(BLOCKS):
                    m = rows(b)
                    act.wait_ge(var_ready, BLOCKS * k + b + 1)
                    nc.scalar.activation(rstd[0:m], mv[0:m, 1:2], ACT.Sqrt, bias=eps[0:m]).then_inc(std_ready, 1)

            def stage_q(layer, b, hd, b8):
                act.wait_ge(sc_ready, b8 + hd + BLOCKS * HEADS * layer)
                act.sem_inc(turn["act"], 1)
                for c in range(2):
                    a = nc.scalar.activation(qst[:, c * P:(c + 1) * P],
                                             qT[:, bass.ds(hd * 2 * T + b * P + c * T, P)], ACT.Copy)
                a.then_inc(q_staged, 1)

            def gate_exps(unit):
                act.wait_ge(top_ready, unit + 1)
                act.sem_inc(turn["act"], 1)
                nc.scalar.activation(r_ex, r_tv, ACT.Exp, bias=r_nm, accum_out=r_sum).then_inc(gexp_done, 1)

            def expert_group(G, half, gates, gates_ready, count, mask):
                act.wait_ge(gates_ready, count)
                act.sem_inc(turn["act"], 1)
                nc.scalar.activation(act_w[:, 0, half, :], gates, ACT.Copy)
                for q in range(2):
                    s = slice(4 * q, 4 * q + 4)
                    act.wait_ge(dot_done, G * RING + 4 * q + 4)
                    nc.scalar.activation(act_w[:, 1, half, s], dots[:, half, s], ACT.Gelu).then_inc(gelu_done, 1)
                    act.drain()
                    for r in range(4 * q, 4 * q + 4):
                        nc.scalar.activation(act_w[:, 2, half, r:r + 1], act_w[:, 1, half, r:r + 1], ACT.Copy,
                                             scale=act_w[:, 0, half, r:r + 1])
                    act.drain()
                    for r in range(4 * q, 4 * q + 4):
                        act.wait_ge(slot_done, G * RING + r + 1 + SEED_SLOTS - DIAGS)
                        nc.scalar.activation(diag[:, r % DIAGS, :], mask, ACT.Copy,
                                             scale=act_w[:, 2, half, r:r + 1]).then_inc(diag_ready, 1)

            gates5 = gate[:].rearrange("p b h (a r) -> p b h a r", a=2)
            for layer in range(DEPTH):
                g0 = layer * GROUPS
                u0 = layer * BLOCKS * HEADS
                if layer == 1:
                    turned_out(BASE["turn_b0"])
                    n0 = BASE["conv"]
                    with act.Fori(0, C // 2) as it:
                        for jj in range(2):
                            n = n0 + 3 * jj
                            act.wait_ge(full, it * 6 + (n + 1))
                            act.wait_ge(c_used, it * 2 + (jj + 1))
                            nc.scalar.activation(c_st[:, jj, :], pj[n % 2][:, 0:T], ACT.Copy).then_inc(c_ready, 1)
                            act.wait_ge(c_ready, it * 2 + (jj + 1))
                            act.sem_inc(free[n % 2], 1)
                deviations(2 * layer)
                turned_out(BASE[f"turn{layer}"])
                act.drain()
                if layer == 0:
                    act.wait_ge(s_zero, 2)
                features_out(BASE[f"pq{layer}"])
                act.drain()
                with act.Fori(0, HEADS) as hd:
                    stage_q(layer, 0, hd, 1)
                    gate_exps(hd + u0)
                with act.Fori(0, TB) as b:
                    with act.Fori(0, HEADS) as hd:
                        for half in range(2):
                            if half == 0:
                                stage_q(layer, b + 1, hd, b * HEADS + (HEADS + 1))
                            else:
                                gate_exps(b * HEADS + hd + (u0 + HEADS))
                            expert_group(b * 16 + hd * 2 + (half + g0), (half + g0) % 2, gates5[:, b, hd, half, :],
                                         g_done, b * HEADS + (u0 + HEADS), const("ident"))
                    act.wait_ge(slot_done, b * 16 * RING + ((g0 + 16) * RING + SEED_SLOTS))
                    act.sem_inc(turn["act"], 1)
                    nc.scalar.activation(h[:, b, :], acc[:], ACT.Copy).then_inc(acc_free, 1)
                G = g0 + GROUPS - 1
                expert_group(G, G % 2, gs8, ixs_ready, layer + 1, const("group_of"))
                act.wait_ge(slot_done, (G + 1) * RING + SEED_SLOTS)
                nc.scalar.activation(h[0:NS, TB, :], acc[0:NS, :], ACT.Copy).then_inc(acc_free, 1)
                deviations(2 * layer + 1)
                turned_out(BASE[f"turn_a{layer}"])
                for b in range(BLOCKS):
                    n, m = BASE[f"ple{layer}"] + b, rows(b)
                    act.wait_ge(full, n + 1)
                    nc.scalar.activation(sig[0:m, b, :], pj[n % 2][0:m, :], ACT.Sigmoid).then_inc(free[n % 2], 1)

        @block.vector
        def _(dve):
            V = nc.vector
            V.memset(eps, EPS)
            dve.sem_inc(gelu_done, SEED_GELU)
            dve.sem_inc(c_used, 2)
            dve.sem_inc(sc_read, 1)
            dve.sem_inc(sc_ready, 1)

            dve.wait_ge(s_small, 64)
            dve.wait_ge(s_attn_c, 16)
            w4 = wl.rearrange("p (a b d) -> p a b d", a=2, b=2)
            V.tensor_tensor(w4[:, :, 0, :], w4[:, :, 0, :], w4[:, :, 1, :], ALU.mult)
            dve.drain()
            V.tensor_reduce(lam2, w4[:, :, 0, :], AX_X, ALU.add).then_inc(lam_sums, 1)
            V.tensor_scalar(gsub, subg_sb, 1.0 - LAM_INIT, None, ALU.mult)
            for b in range(BLOCKS):
                n, m = BASE["k_rows"] + b, rows(b)
                dve.wait_ge(full, n + 1)
                if b in (2, 3):
                    dve.wait_ge(k_out[b % 2], 16)
                V.tensor_copy(((lng, lnb)[b % 2] if b < TB else ya)[0:m, :], pj[n % 2][0:m, :]).then_inc(free[n % 2], 1)
            n = BASE["q_rows"]
            dve.wait_ge(full, n + 1)
            V.tensor_copy(xcur[0:NS, :], pj[n % 2][0:NS, :]).then_inc(free[n % 2], 1)
            dve.wait_ge(lam_exps, 1)
            V.tensor_tensor(neglam, lam_e[:, 1:2], lam_e[:, 0:1], ALU.subtract)
            dve.drain()
            V.tensor_scalar(neglam, neglam, LAM_INIT, None, ALU.subtract)
            dve.drain()
            V.tensor_scalar(coef, neglam, 1.0, None, ALU.subtract)
            dve.drain()
            V.tensor_scalar(coef, coef, aconst("second"), 1.0, ALU.mult, ALU.add)
            for b in range(NS):
                n = BASE["q_spread"] + b
                dve.wait_ge(full, n + 1)
                for j in range(N_PAGES):
                    dve.wait_ge(s_pair[b % 2], 32 * (b // 2 + 1))
                    dve.drain()
                    t = V.tensor_tensor(yb[:], kv_pages[:, b % 2, j, :], pj[n % 2][:], ALU.mult)
                    if j == N_PAGES - 1:
                        t.then_inc(free[n % 2], 1)
                    dve.drain()
                    t = V.tensor_reduce(s_pos[:, j, b * 16:(b + 1) * 16], yb[:].rearrange("p (g d) -> p g d", d=HD), AX_X,
                                        ALU.add)
                    if j == N_PAGES - 1:
                        t.then_inc(kpair_used, 1)
            dve.drain()
            V.tensor_tensor(yb[0:NS, :], xcur[0:NS, :], ya[0:NS, :], ALU.mult)
            dve.drain()
            V.tensor_reduce(yb[0:NS, 0:16], yb[0:NS, :].rearrange("p (g d) -> p g d", d=HD), AX_X, ALU.add)
            dve.drain()
            V.tensor_tensor(s_new[0:NS, :].rearrange("p (b g) -> p b g", b=NS),
                            yb[0:NS, 0:16].rearrange("p (b g) -> p b g", b=1).broadcast_to([NS, NS, 16]),
                            aconst("own")[0:NS, :].rearrange("p (b g) -> p b g", g=1).broadcast_to([NS, NS, 16]),
                            ALU.add).then_inc(s_scores, 1)
            n = BASE["s_turn"]
            lg = yb[:, 0:PAST + NS]
            dve.wait_ge(full, n + 1)
            dve.drain()
            V.tensor_tensor(lg, pj[n % 2][:, 0:PAST + NS], aconst("bias_s"), ALU.add).then_inc(free[n % 2], 1)
            dve.drain()
            V.tensor_reduce(smx, lg, AX_X, ALU.max)
            dve.drain()
            V.tensor_scalar(snb, smx, -SCALE, None, ALU.mult).then_inc(s_bias_done, 1)
            dve.wait_ge(s_exp_done, 1)
            V.reciprocal(sinv, ssum)
            dve.drain()
            V.tensor_scalar(lg, lg, sinv, coef, ALU.mult, ALU.mult).then_inc(s_probs, 1)
            n = BASE["p_turn"]
            dve.wait_ge(full, n + 1)
            V.tensor_reduce(diag[:, 0, :], pj[n % 2][:, 0:PAST].rearrange("p (g c) -> p g c", c=2), AX_X, ALU.add)
            V.tensor_reduce(diag[0:NS, 1, 0:NS * HEADS],
                            pj[n % 2][0:NS, PAST:PAST + P].rearrange("p (g c) -> p g c", c=2), AX_X,
                            ALU.add).then_inc(free[n % 2], 1)

            units = [(hd, i) for hd in range(HEADS) for i in range(TB)]
            dve.wait_ge(vpair_used, NS)
            for u in range(len(units) + 1):
                if u < len(units):
                    hd, i = units[u]
                    k = (i + 1) * P
                    n = BASE["attn"] + u
                    dve.wait_ge(full, n + 1)
                    V.scalar_tensor_tensor(out=logit[:, u % 2, :, 0:k],
                                           in0=aconst("dist")[:, SEQ - k:SEQ].rearrange("p (a k) -> p a k", a=1)
                                           .broadcast_to([P, 2, k]),
                                           scalar=SLOPES[hd] / SCALE,
                                           in1=pj[n % 2][:].rearrange("p (c k) -> p c k", c=2)[:, :, 0:k],
                                           op0=ALU.mult, op1=ALU.add).then_inc(free[n % 2], 1)
                    dve.drain()
                    V.tensor_reduce(mx[:, u % 2, :], logit[:, u % 2, :, 0:k], AX_X, ALU.max)
                    dve.drain()
                    V.tensor_scalar(nb[:, u % 2, :], mx[:, u % 2, :], -SCALE, None, ALU.mult).then_inc(a_logits, 1)
                if u >= 1:
                    v = u - 1
                    k = (units[v][1] + 1) * P
                    dve.wait_ge(a_exps, v + 1)
                    V.reciprocal(linv[:, v % 2, :], lsum[:, v % 2, :])
                    dve.drain()
                    V.tensor_scalar(linv[:, v % 2, 1:2], linv[:, v % 2, 1:2], neglam, None, ALU.mult)
                    if v >= 2:
                        dve.wait_ge(a_wT_ps, v - 1)
                    V.tensor_scalar(wrow[:, v % 2, 0:k], logit[:, v % 2, 0, 0:k], linv[:, v % 2, 0:1], None, ALU.mult)
                    dve.drain()
                    V.scalar_tensor_tensor(out=wrow[:, v % 2, 0:k], in0=logit[:, v % 2, 1, 0:k],
                                           scalar=linv[:, v % 2, 1:2], in1=wrow[:, v % 2, 0:k],
                                           op0=ALU.mult, op1=ALU.add).then_inc(a_w, 1)
                    dve.drain()
            for hd in range(HEADS):
                n = BASE["subln"] + hd
                rr = rms_buf(hd)
                dve.wait_ge(rms_ready, hd + 1)
                V.reciprocal(rr, rr)
                dve.drain()
                V.scalar_tensor_tensor(out=oT[:, hd, :], in0=oT[:, hd, :], scalar=gsub, in1=rr,
                                       op0=ALU.mult, op1=ALU.mult).then_inc(o_normed, 1)
                dve.drain()

            def layer_norm(b, k):
                m = rows(b)
                x = h[0:m, b, :]
                for a in range(2):
                    V.bn_stats(stats[0:m, a, :], x[:, a * 512:(a + 1) * 512])
                dve.drain()
                V.bn_aggr(mv[0:m, :], stats[0:m].rearrange("p a s -> p (a s)"))
                dve.drain()
                dve.drain()
                dve.sem_inc(var_ready, 1)
                dve.wait_ge(s_ln, 32 * (k + 1))
                V.scalar_tensor_tensor(out=x, in0=x, scalar=mv[0:m, 0:1], in1=lng[0:m, :],
                                       op0=ALU.subtract, op1=ALU.mult)
                dve.wait_ge(std_ready, BLOCKS * k + b + 1)
                V.reciprocal(rstd[0:m], rstd[0:m])
                dve.drain()
                V.scalar_tensor_tensor(out=x, in0=x, scalar=rstd[0:m], in1=lnb[0:m, :],
                                       op0=ALU.mult, op1=ALU.add).then_inc(ln_done, 1)

            def route_keys(unit):
                dve.wait_ge(sc_ready, unit + 2)
                V.tensor_copy(r_sc, tp[0][:, 0:256]).then_inc(sc_read, 1)
                dve.drain()
                for c in range(2):
                    V.max(r_v[:, c * 16:c * 16 + 8], r_sc[:, c * P:(c + 1) * P])
                dve.drain()
                for c in range(2):
                    V.max_index(r_si[:, c * 16:c * 16 + 8], r_v[:, c * 16:c * 16 + 8], r_sc[:, c * P:(c + 1) * P])
                    V.match_replace(r_wk[:, c * P:(c + 1) * P], r_v[:, c * 16:c * 16 + 8], r_sc[:, c * P:(c + 1) * P],
                                    LOWEST)

            def route_pairs():
                dve.drain()
                for c in range(2):
                    V.max(r_v[:, c * 16 + 8:c * 16 + 16], r_wk[:, c * P:(c + 1) * P])
                dve.drain()
                for c in range(2):
                    V.max_index(r_si[:, c * 16 + 8:c * 16 + 16], r_v[:, c * 16 + 8:c * 16 + 16],
                                r_wk[:, c * P:(c + 1) * P])
                V.tensor_tensor(r_cand.rearrange("p (i j) -> p i j", j=16),
                                r_v[:, 0:16].rearrange("p (i j) -> p i j", j=1).broadcast_to([P, 16, 16]),
                                r_v[:, 16:32].rearrange("p (i j) -> p i j", i=1).broadcast_to([P, 16, 16]), ALU.add)
                dve.drain()
                V.tensor_copy(r_sif, r_si)
                V.max(r_tv[:, 0:8], r_cand)

            def route_top():
                dve.drain()
                V.max_index(r_ti[:, 0:8], r_tv[:, 0:8], r_cand)
                V.match_replace(r_wk, r_tv[:, 0:8], r_cand, LOWEST)
                dve.drain()
                V.max(r_tv[:, 8:16], r_wk)
                V.tensor_scalar(r_nm, r_tv[:, 0:1], -1.0, None, ALU.mult).then_inc(top_ready, 1)
                dve.drain()
                V.max_index(r_ti[:, 8:16], r_tv[:, 8:16], r_wk)
                dve.drain()
                V.tensor_scalar(r_ij[:, 0:16], r_ti, 4, None, ALU.logical_shift_right)
                V.tensor_scalar(r_ij[:, 16:32], r_ti, 15, None, ALU.bitwise_and)
                dve.drain()
                V.tensor_copy(r_ijf, r_ij)

            def route_ids(b, hd):
                dve.drain()
                V.tensor_tensor(r_eq.rearrange("p (k i) -> p k i", i=16),
                                r_ijf.rearrange("p (k i) -> p k i", i=1).broadcast_to([P, 32, 16]),
                                const("iota").rearrange("p (k i) -> p k i", k=1).broadcast_to([P, 32, 16]),
                                ALU.is_equal)
                dve.drain()
                eq4 = r_eq.rearrange("p (c k i) -> p c k i", c=2, i=16)
                V.tensor_tensor(eq4, eq4, r_sif.rearrange("p (c k i) -> p c k i", c=2, k=1).broadcast_to([P, 2, 16, 16]),
                                ALU.mult)
                dve.drain()
                V.tensor_reduce(r_e, r_eq.rearrange("p (k i) -> p k i", i=16), AX_X, ALU.add)
                dve.drain()
                V.scalar_tensor_tensor(out=idx[:, b, hd, :], in0=r_e[:, 0:16], scalar=float(KEYS), in1=r_e[:, 16:32],
                                       op0=ALU.mult, op1=ALU.add).then_inc(idx_done, 1)

            def gates(b, hd, unit):
                dve.wait_ge(gexp_done, unit + 1)
                V.reciprocal(r_inv, r_sum)
                dve.drain()
                V.tensor_scalar(gate[:, b, hd, :], r_ex, r_inv, None, ALU.mult).then_inc(g_done, 1)

            def dot_group(G, half, slots=range(RING)):
                for r in slots:
                    dve.wait_ge(gathered[r], G * 16 + 16)
                    if r == 0:
                        dve.wait_ge(gelu_done, G * 2 + 2)
                    V.tensor_tensor_reduce(uv[:, r, 0:D], uv[:, r, 0:D], xcur[:], 1.0, 0.0, ALU.mult, ALU.add,
                                           dots[:, half, r:r + 1]).then_inc(dot_done, 1)

            for layer in range(DEPTH):
                g0 = layer * GROUPS
                u0 = layer * BLOCKS * HEADS
                if layer == 1:
                    n0 = BASE["conv"]
                    dve.drain()
                    V.memset(uT[:, :, 0:2], 0.0)
                    with dve.Fori(0, C // 2) as it:
                        for jj in range(2):
                            j = it * 2 + jj
                            n = n0 + 3 * jj
                            dve.drain()
                            dve.wait_ge(c_ready, it * 2 + (jj + 1))
                            dve.wait_ge(full, it * 6 + (n + 2))
                            V.tensor_tensor(uT[:, j, 2:UW], c_st[:, jj, :], pj[(n + 1) % 2][:, 0:T],
                                            ALU.mult).then_inc(free[(n + 1) % 2], 1)
                            dve.drain()
                            dve.sem_inc(c_used, 1)
                            V.tensor_scalar(z[:, 0:SEQ], uT[:, j, 0:SEQ], cw[:, 0, bass.ds(j, 1)], None, ALU.mult)
                            V.tensor_scalar(z[:, SEQ:T], state[:, j, 0, :], cw[:, 0, bass.ds(j, 1)], None, ALU.mult)
                            dve.drain()
                            V.scalar_tensor_tensor(out=z[:, 0:SEQ], in0=uT[:, j, 1:1 + SEQ], scalar=cw[:, 1, bass.ds(j, 1)],
                                                   in1=z[:, 0:SEQ], op0=ALU.mult, op1=ALU.add)
                            V.scalar_tensor_tensor(out=z[:, SEQ:T], in0=state[:, j, 1, :], scalar=cw[:, 1, bass.ds(j, 1)],
                                                   in1=z[:, SEQ:T], op0=ALU.mult, op1=ALU.add)
                            dve.drain()
                            V.scalar_tensor_tensor(out=z, in0=uT[:, j, 2:UW], scalar=cw[:, 2, bass.ds(j, 1)],
                                                   in1=z, op0=ALU.mult, op1=ALU.add)
                            dve.drain()
                            dve.wait_ge(full, it * 6 + (n + 3))
                            V.tensor_tensor(gz[:, j, :], z, pj[(n + 2) % 2][:, 0:T], ALU.mult) \
                                .then_inc(free[(n + 2) % 2], 1)
                            dve.drain()
                            dve.sem_inc(gz_ready, 1)
                for b in range(BLOCKS):
                    n, m = BASE[f"mix{layer}"] + b, rows(b)
                    if layer == 0 and b == 0:
                        dve.wait_ge(s_h, 32)
                    dve.wait_ge(full, n + 1)
                    V.scalar_tensor_tensor(out=h[0:m, b, :], in0=h[0:m, b, :], scalar=ALPHA, in1=pj[n % 2][0:m, :],
                                           op0=ALU.mult, op1=ALU.add).then_inc(free[n % 2], 1)
                    dve.drain()
                    layer_norm(b, 2 * layer)
                dve.drain()
                with dve.Fori(0, HEADS) as hd:
                    dve.drain()
                    route_keys(hd + u0)
                    route_pairs()
                    route_top()
                    route_ids(0, hd)
                    gates(0, hd, hd + u0)
                with dve.Fori(0, TB) as b:
                    dve.drain()
                    V.tensor_copy(xcur[:], h[:, b, :]).then_inc(x_ready, 1)
                    with dve.Fori(0, HEADS) as hd:
                        dve.drain()
                        route_keys(b * HEADS + hd + (u0 + HEADS))
                        dot_group(b * 16 + hd * 2 + g0, g0 % 2, range(0, 4))
                        route_pairs()
                        dot_group(b * 16 + hd * 2 + g0, g0 % 2, range(4, 8))
                        route_top()
                        dot_group(b * 16 + hd * 2 + (1 + g0), (1 + g0) % 2, range(0, 4))
                        route_ids(b + 1, hd)
                        dot_group(b * 16 + hd * 2 + (1 + g0), (1 + g0) % 2, range(4, 8))
                        gates(b + 1, hd, b * HEADS + hd + (u0 + HEADS))
                dve.drain()
                V.tensor_copy(x_ig[0:NS, 0:P], idx[0:NS, TB, :, :].rearrange("p h k -> p (h k)"))
                V.tensor_copy(x_ig[0:NS, P:2 * P], gate[0:NS, TB, :, :].rearrange("p h k -> p (h k)")).then_inc(ig_ready, 1)
                n = BASE[f"x_spread{layer}"]
                dve.wait_ge(full, n + 1)
                V.tensor_copy(xcur[:], pj[n % 2][:]).then_inc(free[n % 2], 1)
                n = BASE[f"i_spread{layer}"]
                dve.wait_ge(full, n + 1)
                V.tensor_tensor(x_pr.rearrange("p (g k) -> p g k", k=TOPK),
                                pj[n % 2][:, 0:256].rearrange("p (g k) -> p g k", k=TOPK),
                                const("kmask").rearrange("p (g k) -> p g k", g=1).broadcast_to([P, 16, TOPK]),
                                ALU.mult).then_inc(free[n % 2], 1)
                dve.drain()
                V.tensor_reduce(x_sel, x_pr.rearrange("p (g k) -> p g k", k=TOPK), AX_X, ALU.add)
                dve.drain()
                V.tensor_copy(ixs, x_sel[:, 0:HEADS])
                V.tensor_copy(gs8, x_sel[:, HEADS:2 * HEADS]).then_inc(ixs_ready, 1)
                G = g0 + GROUPS - 1
                dot_group(G, G % 2)
                for b in range(BLOCKS):
                    dve.wait_ge(acc_free, BLOCKS * layer + b + 2)
                    layer_norm(b, 2 * layer + 1)
                    dve.drain()
                for b in range(BLOCKS):
                    n, m = BASE[f"ple{layer}"] + BLOCKS + b, rows(b)
                    y = sig[0:m, b, :]
                    dve.wait_ge(full, n + 1)
                    if b == 0:
                        all_read(dve, n)
                    V.tensor_tensor(y, y, pj[n % 2][0:m, :], ALU.mult).then_inc(free[n % 2], 1)
                    dve.drain()
                    V.tensor_tensor(h[0:m, b, :], h[0:m, b, :], y, ALU.add).then_inc(ple_done, 1)
                    dve.drain()

        @block.tensor
        def _(pe):
            mm = nc.tensor.matmul

            def features(base, first):
                with pe.Fori(0, 2) as it:
                    for f in range(8):
                        slot = (first + f // 4) % 2
                        n = base + f
                        if f % 4 == 0:
                            pe.wait_ge(s_panel[slot], it * 16 + 16 * ((first + f // 4) // 2 + 1))
                        pe.wait_ge(free[n % 2], it * 4 + freed(n))
                        w = panel[:, slot, :].rearrange("p (c n) -> p c n", c=C)[:, :, (f % 4) * P:(f % 4 + 1) * P]
                        for c in range(C):
                            mm(pj[n % 2][:, 0:SEQ], w[:, c, :], hT[:, c, 0:SEQ], start=(c == 0), stop=(c == C - 1))
                        for c in range(C):
                            m = mm(pj[n % 2][:, SEQ:T], w[:, c, :], hT[:, c, SEQ:T], start=(c == 0), stop=(c == C - 1))
                        m.then_inc(full, 1)

            def token_rows(n, b, src, first, chunks=C, width=512):
                m = rows(b)
                pe.wait_ge(free[n % 2], freed(n))
                for half in range(2):
                    slot = (first + half) % 2
                    w = panel[:, slot, :].rearrange("p (c n) -> p c n", c=C)
                    for c in range(C):
                        last = mm(pj[n % 2][0:m, half * 512:(half + 1) * 512], src[:, c, b * P:b * P + m], w[:, c, :],
                                  start=(c == 0), stop=(c == C - 1))
                last.then_inc(full, 1)

            def both_panels(first):
                for i in (first, first + 1):
                    pe.wait_ge(s_panel[i % 2], 16 * (i // 2 + 1))

            def turn_h(base, ready, count):
                for b in range(BLOCKS):
                    n, m = base + b, rows(b)
                    pe.wait_ge(ready, count + b + 1)
                    pe.wait_ge(free[n % 2], freed(n))
                    for c in range(C):
                        t = nc.tensor.transpose(pj[n % 2][:, c * P:c * P + m], h[0:m, b, c * P:(c + 1) * P],
                                                const("ident")[0:m, 0:m])
                    t.then_inc(full, 1)

            pe.wait_ge(s_hT, 16)
            features(BASE["qk"], PN_QK)
            both_panels(PN_V)
            for b in range(BLOCKS):
                token_rows(BASE["v"] + b, b, hT, PN_V)
            pe.wait_ge(s_const, 16)
            all_read(pe, BASE["v"])
            for b in range(BLOCKS):
                n, m = BASE["k_rows"] + b, rows(b)
                pe.wait_ge(free[n % 2], freed(n))
                for hd in range(HEADS):
                    t = nc.tensor.transpose(pj[n % 2][0:m, hd * P:(hd + 1) * P], qT3[:, HEADS + hd, b * P:b * P + m],
                                            const("ident"))
                t.then_inc(full, 1)
            n = BASE["q_rows"]
            pe.wait_ge(free[n % 2], freed(n))
            for hd in range(HEADS):
                t = nc.tensor.transpose(pj[n % 2][0:NS, hd * P:(hd + 1) * P], qT3[:, hd, SEQ:T], const("ident"))
            t.then_inc(full, 1)
            pe.wait_ge(s_attn_c, 16)
            all_read(pe, BASE["q_spread"])
            for b in range(NS):
                n = BASE["q_spread"] + b
                pe.wait_ge(free[n % 2], freed(n))
                for half in range(2):
                    m = mm(pj[n % 2][:, half * 512:(half + 1) * 512], aconst("pick")[0:NS, b * P:(b + 1) * P],
                           xcur[0:NS, half * 512:(half + 1) * 512], start=True, stop=True)
                m.then_inc(full, 1)
            n = BASE["s_turn"]
            pe.wait_ge(s_scores, 1)
            pe.wait_ge(free[n % 2], freed(n))
            for j in range(2):
                nc.tensor.transpose(pj[n % 2][:, j * P:(j + 1) * P], s_pos[:, j, :], const("ident"))
            nc.tensor.transpose(pj[n % 2][:, PAST:PAST + NS], s_new[0:NS, :], const("ident")[0:NS, 0:NS]).then_inc(full, 1)
            n = BASE["p_turn"]
            pe.wait_ge(s_probs, 1)
            pe.wait_ge(free[n % 2], freed(n))
            for j in range(2):
                nc.tensor.transpose(pj[n % 2][:, j * P:(j + 1) * P], yb[:, j * P:(j + 1) * P], const("ident"))
            nc.tensor.transpose(pj[n % 2][0:NS, PAST:PAST + P], yb[:, PAST:PAST + NS], const("ident")).then_inc(full, 1)
            n = BASE["s_out"]
            all_read(pe, n)
            for b in range(NS):
                pair = NS + b
                pe.wait_ge(s_pair[pair % 2], 32 * (pair // 2 + 1))
                for hd in range(HEADS):
                    col = pj[n % 2][:, hd * NS + b:hd * NS + b + 1]
                    g = b * HEADS + hd
                    for j in range(N_PAGES):
                        m = mm(col, kv_pages[:, pair % 2, j, hd * P:(hd + 1) * P],
                               diag[:, 0, j * NS * HEADS + g:j * NS * HEADS + g + 1], start=(j == 0), stop=False)
                    if hd == HEADS - 1:
                        m.then_inc(vpair_used, 1)
                    m = mm(col, v_rows[0:NS, TB, hd * P:(hd + 1) * P], diag[0:NS, 1, g:g + 1], start=False, stop=True)
            m.then_inc(full, 1)

            units = [(hd, i) for hd in range(HEADS) for i in range(TB)]
            for u in range(len(units) + 3):
                if u < len(units):
                    hd, i = units[u]
                    k = (i + 1) * P
                    n = BASE["attn"] + u
                    pe.wait_ge(free[n % 2], freed(n))
                    for c in range(2):
                        m = mm(pj[n % 2][:, c * 512:c * 512 + k], qT3[c * HD:(c + 1) * HD, hd, i * P:(i + 1) * P],
                               qT3[c * HD:(c + 1) * HD, HEADS + hd, 0:k], start=True, stop=True)
                    m.then_inc(full, 1)
                if 2 <= u <= len(units) + 1:
                    v = u - 2
                    pe.wait_ge(a_w, v + 1)
                    if v >= 2:
                        pe.wait_ge(a_wT, v - 1)
                    for kb in range(units[v][1] + 1):
                        t = nc.tensor.transpose(tp[v % 2][:, kb * P:(kb + 1) * P], wrow[:, v % 2, kb * P:(kb + 1) * P],
                                                const("ident"))
                    t.then_inc(a_wT_ps, 1)
                if u >= 3:
                    v = u - 3
                    hd, i = units[v]
                    pe.wait_ge(a_wT, v + 1)
                    pe.wait_ge(a_ofree, v + 1)
                    for kb in range(i + 1):
                        m = mm(acc[:, (v % 2) * 512:(v % 2) * 512 + P], v_rows[:, kb, hd * P:(hd + 1) * P],
                               wT[:, v % 2, kb * P:(kb + 1) * P], start=(kb == 0), stop=(kb == i))
                    m.then_inc(a_o, 1)
            for hd in range(HEADS):
                n = BASE["subln"] + hd
                pe.wait_ge(sq_ready, hd + 1)
                pe.wait_ge(free[n % 2], freed(n))
                sq = logit[:, hd % 2].rearrange("p c n -> p (c n)")
                mm(pj[n % 2][:, 0:SEQ], aconst("mean"), sq[:, 0:SEQ], start=True, stop=True)
                mm(pj[n % 2][:, SEQ:T], aconst("mean"), sq[:, SEQ:T], start=True, stop=True).then_inc(full, 1)

            def key_scores(hd, unit):
                pe.wait_ge(q_staged, unit + 1)
                pe.wait_ge(sc_read, unit + 1)
                for c in range(2):
                    m = mm(tp[0][:, c * P:(c + 1) * P], qst[:, c * P:(c + 1) * P], keys[:, bass.ds(hd * 2 + c, 1), :].rearrange("p a n -> p (a n)"),
                           start=True, stop=True)
                m.then_inc(sc_ready, 1)

            def start_tile(src, count):
                pe.wait_ge(acc_free, count)
                for half in range(2):
                    mm(acc[:, half * 512:(half + 1) * 512], const("alpha_eye"), src[:, half * 512:(half + 1) * 512],
                       start=True, stop=True, skip_group_check=True)

            def add_experts(G):
                for r in range(RING):
                    pe.wait_ge(diag_ready, G * RING + r + 1)
                    for half in range(2):
                        m = mm(acc[:, half * 512:(half + 1) * 512], diag[:, r % DIAGS, :],
                               uv[:, r, D + half * 512:D + (half + 1) * 512], start=False, stop=True,
                               skip_group_check=True)
                    m.then_inc(slot_done, 1)

            for layer in range(DEPTH):
                g0 = layer * GROUPS
                u0 = layer * BLOCKS * HEADS
                if layer == 0:
                    both_panels(PN_O)
                    pe.wait_ge(o_normed, HEADS)
                    for b in range(BLOCKS):
                        token_rows(BASE["mix0"] + b, b, oT, PN_O)
                else:
                    turn_h(BASE["turn_b0"], ple_done, 0)
                    all_read(pe, BASE["conv"])
                    with pe.Fori(0, C // 2) as it:
                        for jj in range(2):
                            slot = (PN_CONV + jj) % 2
                            pe.wait_ge(s_panel[slot], it * 16 + 16 * ((PN_CONV + jj) // 2 + 1))
                            for k in range(3):
                                n = BASE["conv"] + 3 * jj + k
                                pe.wait_ge(free[n % 2], it * 3 + freed(n))
                                w = panel[:, slot, 0:C * 384].rearrange("p (c n) -> p c n", c=C)[:, :, k * P:(k + 1) * P]
                                for c in range(C):
                                    mm(pj[n % 2][:, 0:SEQ], w[:, c, :], hT[:, c, 0:SEQ], start=(c == 0), stop=(c == C - 1))
                                for c in range(C):
                                    m = mm(pj[n % 2][:, SEQ:T], w[:, c, :], hT[:, c, SEQ:T], start=(c == 0),
                                           stop=(c == C - 1))
                                m.then_inc(full, 1)
                    both_panels(PN_COUT)
                    pe.wait_ge(gz_ready, C)
                    for b in range(BLOCKS):
                        token_rows(BASE["mix1"] + b, b, gz, PN_COUT)
                turn_h(BASE[f"turn{layer}"], ln_done, 2 * BLOCKS * layer)
                all_read(pe, BASE[f"pq{layer}"])
                features(BASE[f"pq{layer}"], (PN_PQ, PN_PQ1)[layer])
                pe.wait_ge(s_keys, 16 * (layer + 1))
                with pe.Fori(0, HEADS) as hd:
                    key_scores(hd, hd + u0)
                with pe.Fori(0, TB) as b:
                    pe.wait_ge(x_ready, b + (TB * layer + 1))
                    start_tile(xcur, b + (BLOCKS * layer + 1))
                    with pe.Fori(0, HEADS) as hd:
                        key_scores(hd, b * HEADS + hd + (u0 + HEADS))
                        for half in range(2):
                            add_experts(b * 16 + hd * 2 + (half + g0))
                n = BASE[f"x_spread{layer}"]
                pe.wait_ge(free[n % 2], freed(n))
                for half in range(2):
                    m = mm(pj[n % 2][:, half * 512:(half + 1) * 512], const("spread")[0:NS, :],
                           h[0:NS, TB, half * 512:(half + 1) * 512], start=True, stop=True)
                m.then_inc(full, 1)
                n = BASE[f"i_spread{layer}"]
                pe.wait_ge(ig_ready, layer + 1)
                pe.wait_ge(free[n % 2], freed(n))
                mm(pj[n % 2][:, 0:256], const("spread")[0:NS, :], x_ig[0:NS, :], start=True, stop=True).then_inc(full, 1)
                start_tile(h[:, TB, :], BLOCKS * layer + TB + 1)
                add_experts(g0 + GROUPS - 1)
                turn_h(BASE[f"turn_a{layer}"], ln_done, (2 * layer + 1) * BLOCKS)
                first = (PN_GATE, PN_GATE1)[layer]
                both_panels(first)
                all_read(pe, BASE[f"ple{layer}"])
                for b in range(BLOCKS):
                    token_rows(BASE[f"ple{layer}"] + b, b, hT, first)
                i = first + 2
                pe.wait_ge(s_panel[i % 2], 16 * (i // 2 + 1))
                wp = panel[:, i % 2, 0:2 * D].rearrange("p (c n) -> p c n", c=2)
                pT = panel[:, i % 2, 2 * D:2 * D + 2 * T].rearrange("p (c t) -> p c t", c=2)
                for b in range(BLOCKS):
                    n, m = BASE[f"ple{layer}"] + BLOCKS + b, rows(b)
                    pe.wait_ge(free[n % 2], freed(n))
                    for half in range(2):
                        for c in range(2):
                            last = mm(pj[n % 2][0:m, half * 512:(half + 1) * 512], pT[:, c, b * P:b * P + m],
                                      wp[:, c, half * 512:(half + 1) * 512], start=(c == 0), stop=(c == 1))
                    last.then_inc(full, 1)


def weight_panels(i):
    out = np.zeros((PANELS, P, C * 512), np.float32)

    def put(at, w):
        for k in range(w.shape[1] // 512):
            out[at + k] = w[:, k * 512:(k + 1) * 512].reshape(C, P, 512).transpose(1, 0, 2).reshape(P, C * 512)

    put(PN_QK, i["w_attn_qkv"][0])
    put(PN_O, i["w_attn_o"][0])
    put(PN_COUT, i["w_conv_out"][0])
    for layer, pq, gate, proj in ((0, PN_PQ, PN_GATE, PN_PROJ), (1, PN_PQ1, PN_GATE1, PN_PROJ1)):
        put(pq, i["w_peer_q"][layer])
        put(gate, i["w_ple_gate"][layer])
        out[proj, :, 0:2 * D] = i["w_ple_proj"][layer].reshape(2, P, D).transpose(1, 0, 2).reshape(P, 2 * D)
        for first, x in ((0, i["p_prompt"][layer, 0]), (SEQ, i["p_sample"][layer, :, 0])):
            pT = out[proj, :, 2 * D:2 * D + 2 * T].reshape(P, 2, T)
            pT[:, :, first:first + len(x)] = x.T.reshape(2, P, len(x)).transpose(1, 0, 2)
            out[proj, :, 2 * D:2 * D + 2 * T] = pT.reshape(P, 2 * T)
    w = i["w_conv_in"][0].reshape(C, P, 3, C, P)
    for j in range(C):
        out[PN_CONV + j, :, 0:C * 384] = w[:, :, [1, 2, 0], j, :].transpose(1, 0, 2, 3).reshape(P, C * 384)
    return out


def kernel(**inputs):
    import concourse.bacc as bacc
    from concourse.bass_utils import run_bass_kernel_spmd as run

    i = {k: np.asarray(v) for k, v in inputs.items()}
    h0 = np.concatenate([i["x_prompt"][0], i["x_sample"][:, 0]])
    arrays = {
        "h0": h0,
        "h0T": h0.T.reshape(C, P, T).transpose(1, 0, 2),
        "consts": constants(),
        "panels": weight_panels(i),
        "keysT": i["peer_keys"].transpose(0, 4, 1, 2, 3).reshape(DEPTH, P, 16, KEYS),
        "uv0": np.concatenate([i["peer_u"][0], i["peer_v"][0]], axis=1),
        "uv1": np.concatenate([i["peer_u"][1], i["peer_v"][1]], axis=1),
        "cache_k": i["cache_k"][0].reshape(POOL_PAGES, PAGE, D),
        "cache_v": i["cache_v"][0].reshape(POOL_PAGES, PAGE, D),
        "pages": i["page_table"].reshape(1, NS * N_PAGES),
        "wlam": i["w_attn_lambda"].reshape(1, 4 * HD),
        "subg": i["attn_subln_g"].reshape(P, 1),
        "ln": np.stack([i["ln_g"].reshape(4, D), i["ln_b"].reshape(4, D)], axis=1),
        "convw": i["conv_w"][0].reshape(3, C, P).transpose(2, 0, 1),
        "state_conv": i["state_conv"][0],
        "stateT": i["state_conv"][0].reshape(NS, 2, C, P).transpose(3, 2, 1, 0),
    }
    outs = {"y_p": (SEQ, D), "y_s": (NS, D), "nk_p": (SEQ, D), "nv_p": (SEQ, D), "nk_s": (NS, D), "nv_s": (NS, D),
            "cp": (2, D), "cs": (NS, 2, D)}
    nc = bacc.Bacc("TRN2", target_bir_lowering=False, num_devices=1)
    feed, args = {}, []
    for name, a in arrays.items():
        a = np.ascontiguousarray(a)
        feed["in_" + name] = a
        args.append(nc.dram_tensor("in_" + name, a.shape, mybir.dt.from_np(a.dtype), kind="ExternalInput").ap())
    for name, shape in outs.items():
        args.append(nc.dram_tensor("out_" + name, shape, F32, kind="ExternalOutput").ap())
    build(nc, *args)
    r = run(nc, [feed], core_ids=[0]).results[0]
    return (r["out_y_p"].reshape(1, SEQ, D), r["out_y_s"].reshape(NS, 1, D),
            r["out_nk_p"].reshape(1, 1, SEQ, HEADS, P), r["out_nv_p"].reshape(1, 1, SEQ, HEADS, P),
            r["out_nk_s"].reshape(1, NS, 1, HEADS, P), r["out_nv_s"].reshape(1, NS, 1, HEADS, P),
            r["out_cp"].reshape(1, 1, 2, D), r["out_cs"].reshape(1, NS, 2, D))
```

```python
import math
from contextlib import ExitStack

import numpy as np

import concourse.bass as bass
from concourse import mybir

ALU = mybir.AluOpType
ACT = mybir.ActivationFunctionType
F32 = mybir.dt.float32
I32 = mybir.dt.int32
U32 = mybir.dt.uint32
AX_X = mybir.AxisListType.X

P = 128
D = 1024
C = D // P
SEQ = 512
NS = 8
T = SEQ + NS
TB = SEQ // P
BLOCKS = TB + 1
HEADS = 8
HD = 64
PAGE = 128
N_PAGES = 2
PAST = PAGE * N_PAGES
POOL_PAGES = 20
TOPK = 16
KEYS = 128
EXPERTS = KEYS * KEYS
PLE = 256
DEPTH = 2
ALPHA = (2 * DEPTH) ** 0.25
LAM_INIT = 0.8 - 0.6 * math.exp(0.0)
EPS = 1e-5
NEG = -1e30
LOWEST = -3.0e38
SCALE = HD ** -0.5
SLOPES = [2.0 ** -(h + 1) for h in range(HEADS)]
RING = 8
GROUPS = TB * HEADS * 2 + 1
DIAGS = 4

GROUP_TILES = [(0, 1), (2, 3, 4)]
G_OFF = [0, 2 * P]
G_W = [2 * P, T - 2 * P]
PW = 256
SLOTS = 3
BANKS = 4

USES = [("qk", 16), ("v", 4 * BLOCKS), ("k_rows", BLOCKS), ("q_rows", 1), ("q_spread", NS), ("s_turn", 1),
        ("p_turn", 1), ("s_out", 1), ("attn", TB * HEADS), ("subln", HEADS)]
BASE = {}
_n = 0
for _name, _count in USES:
    BASE[_name] = _n
    _n += _count
PAIR_USES = _n


def group_of(b):
    return 0 if b < 2 else 1


def rows(b):
    return P if b < TB else NS


class Piece:

    def __init__(self, kind, layer=0, g=0, b=0, p=0, f=0, half=0, ready="", count=0, e=0, load=0, tiles=None,
                 i=0, j=0, k=0, first=False, hd=0, u=0):
        self.kind, self.n, self.panel, self.fence = kind, None, None, False
        self.layer, self.g, self.b = layer, g, b
        self.p, self.f, self.half = p, f, half
        self.ready, self.count = ready, count
        self.e, self.load, self.tiles = e, load, tiles
        self.i, self.j, self.k = i, j, k
        self.first, self.hd, self.u = first, hd, u


class Plan:

    def __init__(self):
        self.n = 0
        self.panels = []
        self.release = []
        self.norms = 0
        self.projs = 0
        self.routes = 0
        self.ln_loads = []
        self.embeds = []
        self.ln_of = {}
        self.ple_of = {}
        for p in range(8):
            self.add_panel("qk", 0, p, ("pair", BASE["qk"] + 2 * (p + 1)))
        for p in range(4):
            self.add_panel("v", 0, p, ("pair", BASE["v"] + BLOCKS * (p + 1)))

    def add_panel(self, name, layer, index, release=None):
        self.panels.append((name, layer, index))
        self.release.append(release)
        return len(self.panels) - 1

    def product(self, piece, panel=None):
        piece.n = self.n
        self.n += 1
        if panel is not None:
            piece.panel = panel
            self.release[panel] = ("full", self.n)
        return piece

    def mix(self, layer, g):
        out = []
        for p in range(4):
            w = self.add_panel("mix", layer, p)
            for b in GROUP_TILES[g]:
                out.append(self.product(Piece("mix", layer=layer, g=g, p=p, b=b), w))
        out[0].fence = True
        return out

    def norm(self, k, g, after_experts):
        if not self.ln_loads or self.ln_loads[-1][0] != k:
            self.ln_loads.append((k, self.norms, len(self.panels)))
        a, c = [], []
        for b in GROUP_TILES[g]:
            e = self.norms
            self.norms += 1
            a.append(Piece("norm_a", b=b, e=e, load=len(self.ln_loads),
                           tiles=self.tile_count(k // 2, b) if after_experts else None))
            c.append(Piece("norm_b", b=b, e=e))
            self.ln_of[b] = e + 1
        return a[:2] + c[:1] + a[2:] + c[1:]

    @staticmethod
    def tile_count(layer, b):
        return layer * BLOCKS + b + 2

    def turn(self, g, of, ready):
        out = []
        for b in GROUP_TILES[g]:
            for half in range(2):
                out.append(self.product(Piece("turn", b=b, g=g, half=half, ready=ready, count=of[b])))
        return out

    def features(self, kind, layer, g):
        out = []
        for p in range(8):
            w = self.add_panel(kind, layer, p)
            for f in (2 * p, 2 * p + 1):
                out.append(self.product(Piece(kind, layer=layer, g=g, f=f), w))
        out[0].fence = True
        return out

    def conv(self, g):
        out = []
        for p in range(12):
            w = self.add_panel("conv", 1, p)
            for i in (2 * p, 2 * p + 1):
                out.append(self.product(Piece("conv", g=g, j=i // 3, k=i % 3, i=i), w))
        out[0].fence = True
        return out

    def embed(self, layer, g):
        out = []
        self.embeds.append((layer, g, self.projs, len(self.panels)))
        for p in range(4):
            w = self.add_panel("gate", layer, p)
            for b in GROUP_TILES[g]:
                out.append(self.product(Piece("gate", layer=layer, g=g, p=p, b=b), w))
        out[0].fence = True
        w = self.add_panel("proj", layer, 0)
        first = len(out)
        for b in GROUP_TILES[g]:
            for p in range(4):
                self.projs += 1
                out.append(self.product(Piece("proj", layer=layer, g=g, p=p, b=b, load=len(self.embeds), first=False), w))
            self.ple_of[b] = self.projs
        out[first].first = True
        return out

    def route(self, layer, b):
        out = []
        for hd in range(HEADS):
            for i in range(4):
                out.append(Piece("route", layer=layer, b=b, hd=hd, i=i, u=self.routes))
            self.routes += 1
        return [Piece("stage", layer=layer, b=b, hd=0, u=self.routes - HEADS)] + out

    def build(self):
        steps = [("alone", 0, 0, [], self.mix(0, 0) + self.norm(0, 0, False) + self.turn(0, self.ln_of, "norm")
                  + self.features("pq", 0, 0) + self.route(0, 0))]

        def window(layer, b, *lanes):
            quarters = 4 * HEADS if b < TB else 2
            lots = [[] for _ in range(quarters)]
            for first, last, pieces in lanes:
                for i, x in enumerate(pieces):
                    lots[first + i * (last - first) // len(pieces)].append(x)
            prep = [self.product(Piece(*x)) for x in (("x_spread",), ("x_spread",), ("i_spread",))] if b == TB else []
            steps.append(("window", layer, b, prep, lots))

        r = self.route(0, 1)
        bg = self.mix(0, 1) + self.norm(0, 1, False) + self.turn(1, self.ln_of, "norm") + self.features("pq", 0, 1)
        window(0, 0, (0, 32, r), (0, 32, bg))
        window(0, 1, (0, 32, self.route(0, 2)))
        r3, rs, r0 = self.route(0, 3), self.route(0, 4), self.route(1, 0)
        bg = self.norm(1, 0, True) + self.turn(0, self.ln_of, "norm") + self.embed(0, 0) \
            + self.turn(0, dict(self.ple_of), "embedding") + self.conv(0) + self.mix(1, 0) + self.norm(2, 0, False) \
            + self.turn(0, self.ln_of, "norm") + self.features("pq", 1, 0)
        cut = len(bg) * 2 // 3
        window(0, 2, (0, 32, r3), (0, 32, bg[:cut]))
        window(0, 3, (0, 15, rs), (16, 32, r0), (0, 16, bg[cut:]))
        window(0, 4)
        r1, r2, r3, rs = (self.route(1, b) for b in (1, 2, 3, 4))
        bg = self.norm(1, 1, True) + self.turn(1, self.ln_of, "norm") + self.embed(0, 1) \
            + self.turn(1, dict(self.ple_of), "embedding") + self.conv(1) + self.mix(1, 1) \
            + self.norm(2, 1, False) + self.turn(1, self.ln_of, "norm") + self.features("pq", 1, 1)
        cut = len(bg) * 2 // 3
        window(1, 0, (0, 32, r1), (0, 32, bg[:cut]))
        window(1, 1, (16, 32, r2), (0, 16, bg[cut:]))
        bg = self.norm(3, 0, True) + self.turn(0, self.ln_of, "norm") + self.embed(1, 0)
        window(1, 2, (0, 32, r3), (0, 32, bg))
        window(1, 3, (0, 32, rs))
        window(1, 4)
        steps.append(("alone", 1, TB, [], self.norm(3, 1, True) + self.turn(1, self.ln_of, "norm") + self.embed(1, 1)))
        return steps


def window_quarters(layer, b, lots):
    first = layer * GROUPS + b * HEADS * 2
    return [(t, first + t // 2, t % 2, t // 4, lot) for t, lot in enumerate(lots)]


DRAM_PANELS = [("qk", 0, 8), ("v", 0, 4)] + [(name, layer, count) for name, count in
                                            (("mix", 4), ("pq", 8), ("gate", 4), ("proj", 1)) for layer in range(DEPTH)] \
    + [("conv", 1, 12)]
PANEL_AT = {}
for _name, _layer, _count in DRAM_PANELS:
    for _i in range(_count):
        PANEL_AT[_name, _layer, _i] = len(PANEL_AT)

CONST = [("ident", P), ("alpha_eye", P), ("group_of", P), ("spread", P), ("kmask", TOPK), ("iota", TOPK)]
ATTN_CONST = [("dist", SEQ), ("bias_s", PAST + NS), ("pick", NS * P), ("own", NS), ("mean", P), ("second", 1)]


def columns(parts):
    at, out = 0, {}
    for name, width in parts:
        out[name] = (at, at + width)
        at += width
    return out, at


CC, N_CONST = columns(CONST)
AC, N_ATTN = columns(ATTN_CONST)


def constants():
    p = np.arange(P)
    a = np.zeros((P, N_CONST + N_ATTN), np.float32)

    def put(cols, off, v):
        a[:v.shape[0], off + cols[0]:off + cols[1]] = v

    put(CC["ident"], 0, np.eye(P))
    put(CC["alpha_eye"], 0, np.eye(P) * ALPHA)
    put(CC["group_of"], 0, (p[:, None] // TOPK == p[None, :]).astype(np.float32))
    put(CC["spread"], 0, (np.arange(NS)[:, None] == p[None, :] // TOPK).astype(np.float32))
    put(CC["kmask"], 0, (p[:, None] % TOPK == np.arange(TOPK)[None, :]).astype(np.float32))
    put(CC["iota"], 0, np.tile(np.arange(TOPK), (P, 1)))
    j = np.arange(SEQ)
    dist = p[:, None] + (SEQ - P) - j[None, :]
    put(AC["dist"], N_CONST, np.where(dist >= 0, -dist, NEG))
    slope = np.array(SLOPES)[(p // 2) % HEADS] / SCALE
    bias = np.zeros((P, PAST + NS))
    bias[:, :PAST] = -slope[:, None] * (PAST - np.arange(PAST))[None, :]
    put(AC["bias_s"], N_CONST, bias)
    pick = np.zeros((NS, NS, P))
    for b in range(NS):
        pick[b, b] = 1
    put(AC["pick"], N_CONST, pick.reshape(NS, NS * P))
    put(AC["own"], N_CONST, np.where(np.eye(NS) > 0, 0, NEG))
    put(AC["mean"], N_CONST, np.full((P, P), 1 / P))
    put(AC["second"], N_CONST, (p % 2)[:, None])
    return a


def freed(n):
    return n // 2 + 1


def bank_freed(n):
    return n // BANKS + 1


def build(nc, h0, h0T, consts, panels, ple_rows, keysT, uv0, uv1, cache_k, cache_v, pages, wlam, subg, ln, convw,
          state_conv, stateT, y_p, y_s, nk_p, nv_p, nk_s, nv_s, cp, cs):
    uv_dram = [uv0, uv1]
    ctx = ExitStack()
    with ctx:
        def sb(name, shape, dt=F32):
            return ctx.enter_context(nc.sbuf_tensor(name, shape, dt))

        def sem(name):
            return ctx.enter_context(nc.semaphore(name))

        h = sb("h", [P, BLOCKS, D])
        hT = sb("hT", [P, C, G_W[1]])
        gx = sb("gx", [P, C, G_W[1] + 2])
        gxT = gx[:].rearrange("p c t -> p (c t)")[:, 0:C * G_W[1]].rearrange("p (c t) -> p c t", c=C)
        QTN = 16 * T
        qT = sb("qT", [P, QTN + P - NS])
        qT3 = qT[:, 0:QTN].rearrange("p (f t) -> p f t", t=T)
        qT4 = qT[:, 0:QTN].rearrange("p (a f t) -> p a f t", a=2, t=T)
        q_off = [0, 16 * G_W[0]]
        qTg = [qT[:, q_off[g]:q_off[g] + 16 * G_W[g]].rearrange("p (f t) -> p f t", t=G_W[g]) for g in range(2)]
        sig = [qT[:, q_off[g]:q_off[g] + len(GROUP_TILES[g]) * D].rearrange("p (b n) -> p b n", n=D) for g in range(2)]
        keys = sb("keys", [P, 16, KEYS])
        arena = sb("arena", [P, RING * 2 * D])
        uv = arena[:].rearrange("p (r n) -> p r n", r=RING)
        panel = sb("panel", [P, SLOTS, C * PW])
        pTs = sb("pTs", [P, 2, G_W[1]])
        c_st = sb("c_st", [P, 2, G_W[1]])
        z = sb("z", [P, G_W[1]])
        carry = sb("carry", [P, C, 2])
        tail = sb("tail", [P, C, 2 + NS])
        xcur = sb("xcur", [P, D])
        ya = sb("ya", [P, D])
        yb = sb("yb", [P, D])
        lng = sb("lng", [P, D])
        lnb = sb("lnb", [P, D])
        idx = sb("idx", [P, BLOCKS, HEADS, TOPK], I32)
        gate = sb("gate", [P, BLOCKS, HEADS, TOPK])
        diag = sb("diag", [P, DIAGS, P])
        qst = sb("qst", [P, 2 * P])
        cst = sb("cst", [P, N_CONST])
        ixst = sb("ixst", [P, 2, RING], I32)
        dots = sb("dots", [P, 2, RING])
        act_w = sb("act_w", [P, 3, 2, RING])
        small = sb("small", [P, 64])
        state = sb("state", [P, C, 2, NS])
        cw = sb("cw", [P, 3, C])

        def const(name):
            return cst[:, CC[name][0]:CC[name][1]]

        at = [0]

        def part(n):
            at[0] += n
            return arena[:, at[0] - n:at[0]]

        v_rows = part(BLOCKS * D).rearrange("p (b n) -> p b n", b=BLOCKS)
        oT = [part(C * G_W[0]).rearrange("p (c t) -> p c t", c=C), gxT]
        kv_pages = part(4 * D).rearrange("p (i j n) -> p i j n", i=2, j=2)
        logit = kv_pages[:, 0].rearrange("p j (c n) -> p j c n", c=2)
        wrow = kv_pages[:, 1, 0].rearrange("p (j n) -> p j n", j=2)
        wT = kv_pages[:, 1, 1].rearrange("p (j n) -> p j n", j=2)
        attn_c = part(N_ATTN)
        wl = part(4 * HD)
        s_pos = part(2 * P).rearrange("p (j n) -> p j n", j=2)
        s_new = part(P)

        def aconst(name):
            return attn_c[:, AC[name][0]:AC[name][1]]

        r_sc = yb[:, 0:256]
        r_wk = yb[:, 256:512]
        r_eq = yb[:, 512:1024]
        r_cand = ya[:, 0:256]
        r_v = ya[:, 256:288]
        r_si = ya[:, 288:320].bitcast(U32)
        r_sif = ya[:, 320:352]
        r_tv = ya[:, 352:368]
        r_ti = ya[:, 368:384].bitcast(U32)
        r_ij = ya[:, 384:416].bitcast(U32)
        r_ijf = ya[:, 416:448]
        r_e = ya[:, 448:480]
        r_nm = ya[:, 480:481]
        r_ex = ya[:, 496:512]
        r_sum = ya[:, 512:513]
        r_inv = ya[:, 513:514]
        x_ig = yb[:, 0:256]
        x_pr = yb[:, 256:512]
        x_sel = ya[:, 640:656]

        stats = small[:, 0:12].rearrange("p (a s) -> p a s", a=2)
        lam2 = small[:, 16:18]
        lam_e = small[:, 18:20]
        neglam = small[:, 20:21]
        coef = small[:, 21:22]
        gsub = small[:, 22:23]
        subg_sb = small[:, 23:24]
        mx = small[:, 24:28].rearrange("p (j c) -> p j c", j=2)
        nb = small[:, 28:32].rearrange("p (j c) -> p j c", j=2)
        lsum = small[:, 32:36].rearrange("p (j c) -> p j c", j=2)
        linv = small[:, 36:40].rearrange("p (j c) -> p j c", j=2)
        smx, snb, ssum, sinv = (small[:, 40 + i:41 + i] for i in range(4))
        ixs = small[:, 44:52].bitcast(I32)
        gs8 = small[:, 52:60]
        eps = small[:, 60:61]
        mv = sb("mv", [P, 2, 2])
        rstd = sb("rstd", [P, 2, 1])
        pg = sb("pg", [1, NS * N_PAGES], I32)

        bank = ctx.enter_context(nc.psum_tensor("bank", [P, BANKS, 512], F32))
        pj = [bank[:, 2 * i:2 * i + 2, :].rearrange("p a n -> p (a n)") for i in range(2)]
        acc = ctx.enter_context(nc.psum_tensor("acc", [P, 1024], F32))
        tp = [ctx.enter_context(nc.psum_tensor(f"tp{i}", [P, 512], F32)) for i in range(2)]

        s_const = sem("const_in")
        s_attn_c = sem("attn_const_in")
        s_h = sem("h_in")
        s_hT = sem("hT_in")
        s_keys = sem("keys_in")
        s_small = sem("small_in")
        s_pages = sem("page_ids_in")
        s_zero = sem("zeroed")
        s_panel = [sem(f"panel_in{i}") for i in range(SLOTS)]
        s_pT = sem("embedding_rows_in")
        s_ln = sem("ln_params_in")
        s_pair = [sem(f"page_pair_in{i}") for i in range(2)]
        full = sem("pair_full")
        free = [sem(f"pair_free{i}") for i in range(2)]
        bank_full = sem("bank_full")
        bank_free = [sem(f"bank_free{i}") for i in range(BANKS)]
        k_out = [sem(f"k_rows_stored{i}") for i in range(3)]
        v_out = sem("v_rows_stored")
        kpair_used = sem("k_pair_used")
        vpair_used = sem("v_pair_used")
        lam_sums = sem("lambda_sums")
        lam_exps = sem("lambda_exps")
        s_scores = sem("sample_scores")
        s_bias_done = sem("sample_logits")
        s_exp_done = sem("sample_exps")
        s_probs = sem("sample_probs")
        s_wT = sem("sample_weights_turned")
        a_logits = sem("logits_ready")
        a_exps = sem("exps_ready")
        a_w = sem("weights_ready")
        a_wT_ps = sem("weights_turned")
        a_wT = sem("turned_weights_ready")
        a_o = sem("attn_out_full")
        a_ofree = sem("attn_out_free")
        sq_ready = sem("squares_ready")
        o_normed = sem("attn_out_normed")
        var_ready = sem("variance_ready")
        std_ready = sem("deviation_ready")
        rms_ready = sem("rms_ready")
        ln_done = sem("ln_done")
        ple_done = sem("embedding")
        tail_ready = sem("conv_state_ready")
        conv_out = sem("conv_state_stored")
        conv_copy = sem("conv_state_copied")
        q_staged = sem("q_staged")
        sc_ready = sem("key_scores_ready")
        sc_read = sem("key_scores_read")
        top_ready = sem("top_ready")
        gexp_done = sem("gate_exps")
        idx_done = sem("expert_ids")
        g_done = sem("gates_ready")
        ix_ready = sem("ids_staged")
        gathered = [sem(f"gathered{r}") for r in range(RING)]
        dot_done = sem("dots_done")
        gelu_done = sem("gelu_done")
        diag_ready = sem("diag_ready")
        slot_done = sem("slots_done")
        x_ready = sem("x_staged")
        acc_free = sem("acc_free")
        ig_ready = sem("sample_ids_rows")
        ixs_ready = sem("sample_ids_spread")
        y_out = sem("y_stored")
        turn = {e: sem(f"turn_{e}") for e in ("act", "pool", "dve")}

        SEED_SLOTS = RING
        SEED_GELU = 4

        block = ctx.enter_context(nc.Block())

        def rms_buf(hd):
            return (wrow, wT)[hd % 2].rearrange("p j n -> p (j n)")[:, 0:T]

        def squares(hd):
            return logit[:, hd % 2].rearrange("p c n -> p (c n)")[:, 0:T]

        def all_read(eng, n):
            for p in range(2):
                eng.wait_ge(free[p], (n - p + 1) // 2 + 1)

        def banks_read(eng, n):
            for p in range(BANKS):
                eng.wait_ge(bank_free[p], (n - p + BANKS - 1) // BANKS + 1)

        plan = Plan()
        steps = plan.build()

        def local(b):
            return b * P - G_OFF[group_of(b)]

        @block.sync
        def _(sp):
            sp.dma_start(hT[:, :, 0:G_W[0]], h0T[:, :, 0:G_W[0]]).then_inc(s_hT, 16)

            def load_panel(i):
                if i >= SLOTS:
                    kind, count = plan.release[i - SLOTS]
                    sp.wait_ge(full if kind == "pair" else bank_full, count)
                sp.dma_start(panel[:, i % SLOTS, :], panels[PANEL_AT[plan.panels[i]]]).then_inc(s_panel[i % SLOTS], 16)

            def load_ln(k, norms):
                if k == 0:
                    for i in range(2):
                        sp.wait_ge(k_out[i], 32)
                else:
                    sp.wait_ge(ln_done, norms)
                sp.dma_start(lng[:], ln[k, 0:1, :].broadcast_to([P, D])).then_inc(s_ln, 16)
                sp.dma_start(lnb[:], ln[k, 1:2, :].broadcast_to([P, D])).then_inc(s_ln, 16)

            def load_embedding(layer, g, projs):
                if projs:
                    sp.wait_ge(ple_done, projs)
                sp.dma_start(pTs[:, :, 0:G_W[g]], ple_rows[layer, :, :, G_OFF[g]:G_OFF[g] + G_W[g]]).then_inc(s_pT, 16)

            load_panel(0)
            sp.dma_start(gxT, h0T[:, :, G_W[0]:T]).then_inc(s_hT, 16)
            load_panel(1)
            load_panel(2)
            sp.dma_start(cst[:], consts[:, 0:N_CONST]).then_inc(s_const, 16)
            sp.dma_start(attn_c, consts[:, N_CONST:N_CONST + N_ATTN]).then_inc(s_attn_c, 16)
            sp.dma_start(wl, wlam.broadcast_to([P, 4 * HD])).then_inc(s_small, 16)
            sp.dma_start(subg_sb, subg).then_inc(s_small, 16)
            sp.dma_start(cw[:], convw).then_inc(s_small, 16)
            sp.dma_start(state[:], stateT).then_inc(s_small, 16)
            sp.dma_start(h[:, 0:TB, :], h0[0:SEQ, :].rearrange("(b p) n -> p b n", p=P)).then_inc(s_h, 16)
            sp.wait_ge(s_zero, 1)
            sp.dma_start(h[0:NS, TB, :], h0[SEQ:T, :]).then_inc(s_h, 16)
            sp.dma_start(keys[:], keysT[0]).then_inc(s_keys, 16)
            for i in range(SLOTS, len(plan.panels) + 1):
                for k, norms, before in plan.ln_loads:
                    if before == i:
                        load_ln(k, norms)
                for layer, g, projs, before in plan.embeds:
                    if before == i:
                        load_embedding(layer, g, projs)
                if i < len(plan.panels):
                    load_panel(i)
            for b in range(BLOCKS):
                sp.wait_ge(ple_done, plan.ple_of[b])
                dst = y_p[b * P:(b + 1) * P, :] if b < TB else y_s
                sp.dma_start(dst, h[0:rows(b), b, :]).then_inc(y_out, 16)
            sp.wait_ge(y_out, 16 * BLOCKS)
            sp.wait_ge(v_out, 16 * BLOCKS)
            sp.wait_ge(k_out[2], 16)
            sp.wait_ge(conv_out, 16 * 2 * C)
            sp.wait_ge(conv_copy, 16)

        @block.gpsimd
        def _(pool):
            pool.dma_start(pg[:], pages).then_inc(s_pages, 16)
            nc.gpsimd.memset(h[:, TB, :], 0.0).then_inc(s_zero, 1)
            nc.gpsimd.memset(qT[:, QTN:QTN + P - NS], 0.0).then_inc(s_zero, 1)
            pool.wait_ge(s_pages, 16)

            def load_pair(i):
                cache = cache_k if i < NS else cache_v
                if i >= 2:
                    pool.wait_ge(kpair_used, min(i - 1, NS))
                    if i - 2 >= NS:
                        pool.wait_ge(vpair_used, i - 1 - NS)
                for j in range(N_PAGES):
                    k = (i % NS) * N_PAGES + j
                    page = pool.value_load(pg[0:1, k:k + 1], min_val=0, max_val=POOL_PAGES - 1)
                    pool.dma_start(kv_pages[:, i % 2, j, :], cache[bass.ds(page, 1)].rearrange("a p n -> (a p) n")) \
                        .then_inc(s_pair[i % 2], 16)

            load_pair(0)
            load_pair(1)
            for b in range(BLOCKS):
                n = BASE["v"] + 3 * BLOCKS + b
                pool.wait_ge(free[n % 2], freed(n) + 1)
                dst = nv_p[b * P:(b + 1) * P, :] if b < TB else nv_s
                pool.dma_start(dst, v_rows[0:rows(b), b, :]).then_inc(v_out, 16)
            for b in range(BLOCKS):
                n = BASE["k_rows"] + b
                pool.wait_ge(free[n % 2], freed(n) + 1)
                dst = nk_p[b * P:(b + 1) * P, :] if b < TB else nk_s
                src = (lng, lnb)[b % 2] if b < TB else ya
                pool.dma_start(dst, src[0:rows(b), :]).then_inc(k_out[b % 2 if b < TB else 2], 16)
            for i in range(2, 2 * NS):
                load_pair(i)

            def gather_group(layer, G, first, ids, ids_ready, count):
                half = first % 2
                pool.wait_ge(ids_ready, count)
                pool.sem_inc(turn["pool"], 1)
                nc.gpsimd.tensor_copy(ixst[:, half, :], ids).then_inc(ix_ready, 1)
                for r in range(RING):
                    if r == 0:
                        pool.wait_ge(ix_ready, G + 1)
                    pool.wait_ge(slot_done, G * RING + r + 1)
                    pool.sem_inc(turn["pool"], 1)
                    nc.gpsimd.indirect_dma_start(
                        uv[:, r, :], None, uv_dram[layer],
                        bass.IndirectOffsetOnAxis(ixst[:, half, r:r + 1], 0)).then_inc(gathered[r], 16)

            ids5 = idx[:].rearrange("p b h (a r) -> p b h a r", a=2)

            def gather_tiles(layer, first, last):
                with pool.Fori(first, last) as b:
                    with pool.Fori(0, HEADS) as hd:
                        for half in range(2):
                            G = layer * GROUPS + half
                            gather_group(layer, b * 16 + hd * 2 + G, G, ids5[:, b, hd, half, :],
                                         idx_done, b * HEADS + hd + (BLOCKS * layer * HEADS + 1))

            pool.wait_ge(v_out, 16 * BLOCKS)
            gather_tiles(0, 0, TB)
            gather_group(0, GROUPS - 1, GROUPS - 1, ixs, ixs_ready, 1)
            gather_tiles(1, 0, 2)
            pool.dma_start(cs[:, 0, :], state_conv[:, 1, :]).then_inc(conv_copy, 16)
            pool.wait_ge(tail_ready, 1)
            with nc.allow_non_contiguous_dma(reason="small state"):
                for j in range(C):
                    pool.dma_start(cp[:, j * P:(j + 1) * P].rearrange("s p -> p s"),
                                   tail[:, j, 0:2]).then_inc(conv_out, 16)
                    pool.dma_start(cs[:, 1, j * P:(j + 1) * P].rearrange("s p -> p s"),
                                   tail[:, j, 2:2 + NS]).then_inc(conv_out, 16)
            gather_tiles(1, 2, TB)
            gather_group(1, 2 * GROUPS - 1, 2 * GROUPS - 1, ixs, ixs_ready, 2)

        @block.scalar
        def _(act):
            act.sem_inc(slot_done, SEED_SLOTS)
            act.sem_inc(free[0], 1)
            act.sem_inc(free[1], 1)
            for i in range(BANKS):
                act.sem_inc(bank_free[i], 1)
            act.sem_inc(acc_free, 1)
            act.sem_inc(a_ofree, 2)

            with act.Fori(0, 2) as it:
                for f in range(8):
                    n = BASE["qk"] + f
                    act.wait_ge(full, it * 8 + (n + 1))
                    act.sem_inc(turn["act"], 1)
                    nc.scalar.activation(qT4[:, it, f, :], pj[n % 2][:, PW:PW + T], ACT.Copy).then_inc(free[n % 2], 1)
            for p in range(4):
                for b in range(BLOCKS):
                    n, m = BASE["v"] + p * BLOCKS + b, rows(b)
                    act.wait_ge(full, n + 1)
                    nc.scalar.activation(v_rows[0:m, b, p * PW:(p + 1) * PW], pj[n % 2][0:m, 0:PW],
                                         ACT.Copy).then_inc(free[n % 2], 1)
            act.wait_ge(lam_sums, 1)
            nc.scalar.activation(lam_e, lam2, ACT.Exp).then_inc(lam_exps, 1)
            act.wait_ge(s_bias_done, 1)
            nc.scalar.activation(yb[:, 0:PAST + NS], yb[:, 0:PAST + NS], ACT.Exp, bias=snb, scale=SCALE,
                                 accum_out=ssum).then_inc(s_exp_done, 1)
            n = BASE["s_out"]
            act.wait_ge(full, n + 1)
            nc.scalar.activation(oT[1][:, :, 2 * P:G_W[1]], pj[n % 2][:, 0:HEADS * NS].rearrange("p (h b) -> p h b", h=HEADS),
                                 ACT.Copy).then_inc(free[n % 2], 1)

            units = [(hd, i) for hd in range(HEADS) for i in range(TB)]
            for u in range(len(units) + 3):
                if u < len(units):
                    n = (units[u][1] + 1) * P
                    act.wait_ge(a_logits, u + 1)
                    for c in range(2):
                        e = nc.scalar.activation(logit[:, u % 2, c, 0:n], logit[:, u % 2, c, 0:n], ACT.Exp,
                                                 bias=nb[:, u % 2, c:c + 1], scale=SCALE,
                                                 accum_out=lsum[:, u % 2, c:c + 1])
                    e.then_inc(a_exps, 1)
                if 2 <= u <= len(units) + 1:
                    v, n = u - 2, (units[u - 2][1] + 1) * P
                    act.wait_ge(a_wT_ps, v + 1)
                    if v >= 2:
                        act.wait_ge(a_o, v - 1)
                    nc.scalar.activation(wT[:, v % 2, 0:n], tp[v % 2][:, 0:n], ACT.Copy).then_inc(a_wT, 1)
                if u >= 3:
                    v = u - 3
                    hd, i = units[v]
                    act.wait_ge(a_o, v + 1)
                    nc.scalar.activation(oT[group_of(i)][:, hd, local(i):local(i) + P], acc[:, (v % 2) * 512:(v % 2) * 512 + P],
                                         ACT.Copy).then_inc(a_ofree, 1)
            act.drain()
            for hd in range(HEADS + 1):
                if hd < HEADS:
                    if hd >= 2:
                        act.wait_ge(full, BASE["subln"] + hd - 1)
                    for g in range(2):
                        a = nc.scalar.activation(squares(hd)[:, G_OFF[g]:G_OFF[g] + G_W[g]], oT[g][:, hd, :], ACT.Square)
                    a.then_inc(sq_ready, 1)
                if hd >= 1:
                    n = BASE["subln"] + hd - 1
                    act.wait_ge(full, n + 1)
                    if hd >= 3:
                        act.wait_ge(o_normed, hd - 2)
                    nc.scalar.activation(rms_buf(hd - 1), pj[n % 2][:, PW:PW + T], ACT.Sqrt, bias=eps)
                    act.drain()
                    act.sem_inc(rms_ready, 1)
                    act.sem_inc(free[n % 2], 1)

            def stage_q(b, hd, unit):
                act.wait_ge(sc_ready, unit + 1)
                g = group_of(b)
                for c in range(2):
                    at = q_off[g] + (2 * hd + c) * G_W[g] + local(b)
                    a = nc.scalar.activation(qst[:, c * P:(c + 1) * P], qT[:, at:at + P], ACT.Copy)
                a.then_inc(q_staged, 1)

            def background(x):
                product_of = bank[:, x.n % BANKS, :] if x.n is not None else None
                if x.kind == "norm_a":
                    m, i = rows(x.b), x.e % 2
                    act.wait_ge(var_ready, x.e + 1)
                    nc.scalar.activation(rstd[0:m, i], mv[0:m, i, 1:2], ACT.Sqrt, bias=eps[0:m]).then_inc(std_ready, 1)
                elif x.kind == "turn":
                    m = rows(x.b)
                    act.wait_ge(bank_full, x.n + 1)
                    nc.scalar.activation(hT[:, 4 * x.half:4 * x.half + 4, local(x.b):local(x.b) + m],
                                         product_of.rearrange("p (c t) -> p c t", c=4)[:, :, 0:m],
                                         ACT.Copy).then_inc(bank_free[x.n % BANKS], 1)
                elif x.kind == "pq":
                    if x.fence:
                        act.drain()
                    act.wait_ge(bank_full, x.n + 1)
                    nc.scalar.activation(qTg[x.g][:, x.f, :], product_of[:, 0:G_W[x.g]],
                                         ACT.Copy).then_inc(bank_free[x.n % BANKS], 1)
                elif x.kind == "gate":
                    if x.fence:
                        act.drain()
                    m = rows(x.b)
                    act.wait_ge(bank_full, x.n + 1)
                    nc.scalar.activation(sig[x.g][0:m, local(x.b) // P, x.p * PW:(x.p + 1) * PW], product_of[0:m, 0:PW],
                                         ACT.Sigmoid).then_inc(bank_free[x.n % BANKS], 1)
                elif x.kind == "conv" and x.k == 0:
                    act.wait_ge(bank_full, x.n + 1)
                    nc.scalar.activation(c_st[:, x.j % 2, 0:G_W[x.g]], product_of[:, 0:G_W[x.g]],
                                         ACT.Copy).then_inc(bank_free[x.n % BANKS], 1)
                elif x.kind == "stage":
                    act.drain()
                    if x.layer == 1 and x.b == 0:
                        act.wait_ge(sc_ready, x.u + 1)
                        act.dma_start(keys[:], keysT[1]).then_inc(s_keys, 16)
                    if x.layer == 0 and x.b == TB:
                        act.wait_ge(s_zero, 2)
                    stage_q(x.b, 0, x.u)
                elif x.kind == "route" and x.i == 1 and x.hd < HEADS - 1:
                    stage_q(x.b, x.hd + 1, x.u + 1)
                elif x.kind == "route" and x.i == 3:
                    act.wait_ge(top_ready, x.u + 1)
                    nc.scalar.activation(r_ex, r_tv, ACT.Exp, bias=r_nm, accum_out=r_sum).then_inc(gexp_done, 1)

            def four_experts(G, q, mask):
                half, s = G % 2, slice(4 * q, 4 * q + 4)
                act.wait_ge(dot_done, G * RING + 4 * q + 4)
                nc.scalar.activation(act_w[:, 1, half, s], dots[:, half, s], ACT.Gelu).then_inc(gelu_done, 1)
                act.drain()
                for r in range(4 * q, 4 * q + 4):
                    nc.scalar.activation(act_w[:, 2, half, r:r + 1], act_w[:, 1, half, r:r + 1], ACT.Copy,
                                         scale=act_w[:, 0, half, r:r + 1])
                act.drain()
                for r in range(4 * q, 4 * q + 4):
                    act.wait_ge(slot_done, G * RING + r + 1 + SEED_SLOTS - DIAGS)
                    nc.scalar.activation(diag[:, r % DIAGS, :], mask, ACT.Copy,
                                         scale=act_w[:, 2, half, r:r + 1]).then_inc(diag_ready, 1)

            gates5 = gate[:].rearrange("p b h (a r) -> p b h a r", a=2)
            for kind, layer, b, prep, lots in steps:
                if kind == "alone":
                    for x in lots:
                        background(x)
                    continue
                later = []
                for t, G, q, hd, lot in window_quarters(layer, b, lots):
                    for x in later:
                        background(x)
                    later = lot
                    if q == 0 and b < TB:
                        act.wait_ge(g_done, (layer * BLOCKS + b) * HEADS + hd + 1)
                        nc.scalar.activation(act_w[:, 0, G % 2, :], gates5[:, b, hd, t // 2 % 2, :], ACT.Copy)
                    elif q == 0:
                        act.wait_ge(ixs_ready, layer + 1)
                        nc.scalar.activation(act_w[:, 0, G % 2, :], gs8, ACT.Copy)
                    four_experts(G, q, const("ident" if b < TB else "group_of"))
                for x in later:
                    background(x)
                act.wait_ge(slot_done, (G + 1) * RING + SEED_SLOTS)
                nc.scalar.activation(h[0:rows(b), b, :], acc[0:rows(b), :], ACT.Copy).then_inc(acc_free, 1)

        @block.vector
        def _(dve):
            V = nc.vector
            V.memset(eps, EPS)
            dve.sem_inc(gelu_done, SEED_GELU)
            dve.sem_inc(sc_read, 1)
            dve.sem_inc(sc_ready, 1)

            dve.wait_ge(s_small, 64)
            dve.wait_ge(s_attn_c, 16)
            w4 = wl.rearrange("p (a b d) -> p a b d", a=2, b=2)
            V.tensor_tensor(w4[:, :, 0, :], w4[:, :, 0, :], w4[:, :, 1, :], ALU.mult)
            dve.drain()
            V.tensor_reduce(lam2, w4[:, :, 0, :], AX_X, ALU.add).then_inc(lam_sums, 1)
            V.tensor_scalar(gsub, subg_sb, 1.0 - LAM_INIT, None, ALU.mult)
            for b in range(BLOCKS):
                n, m = BASE["k_rows"] + b, rows(b)
                dve.wait_ge(full, n + 1)
                if b in (2, 3):
                    dve.wait_ge(k_out[b % 2], 16)
                V.tensor_copy(((lng, lnb)[b % 2] if b < TB else ya)[0:m, :], pj[n % 2][0:m, :]).then_inc(free[n % 2], 1)
            n = BASE["q_rows"]
            dve.wait_ge(full, n + 1)
            V.tensor_copy(xcur[0:NS, :], pj[n % 2][0:NS, :]).then_inc(free[n % 2], 1)
            dve.wait_ge(lam_exps, 1)
            V.tensor_tensor(neglam, lam_e[:, 1:2], lam_e[:, 0:1], ALU.subtract)
            dve.drain()
            V.tensor_scalar(neglam, neglam, LAM_INIT, None, ALU.subtract)
            dve.drain()
            V.tensor_scalar(coef, neglam, 1.0, None, ALU.subtract)
            dve.drain()
            V.tensor_scalar(coef, coef, aconst("second"), 1.0, ALU.mult, ALU.add)
            for b in range(NS):
                n = BASE["q_spread"] + b
                dve.wait_ge(full, n + 1)
                for j in range(N_PAGES):
                    dve.wait_ge(s_pair[b % 2], 32 * (b // 2 + 1))
                    dve.drain()
                    t = V.tensor_tensor(yb[:], kv_pages[:, b % 2, j, :], pj[n % 2], ALU.mult)
                    if j == N_PAGES - 1:
                        t.then_inc(free[n % 2], 1)
                    dve.drain()
                    t = V.tensor_reduce(s_pos[:, j, b * 16:(b + 1) * 16], yb[:].rearrange("p (g d) -> p g d", d=HD), AX_X,
                                        ALU.add)
                    if j == N_PAGES - 1:
                        t.then_inc(kpair_used, 1)
            dve.drain()
            V.tensor_tensor(yb[0:NS, :], xcur[0:NS, :], ya[0:NS, :], ALU.mult)
            dve.drain()
            V.tensor_reduce(yb[0:NS, 0:16], yb[0:NS, :].rearrange("p (g d) -> p g d", d=HD), AX_X, ALU.add)
            dve.drain()
            V.tensor_tensor(s_new[0:NS, :].rearrange("p (b g) -> p b g", b=NS),
                            yb[0:NS, 0:16].rearrange("p (b g) -> p b g", b=1).broadcast_to([NS, NS, 16]),
                            aconst("own")[0:NS, :].rearrange("p (b g) -> p b g", g=1).broadcast_to([NS, NS, 16]),
                            ALU.add).then_inc(s_scores, 1)
            n = BASE["s_turn"]
            lg = yb[:, 0:PAST + NS]
            dve.wait_ge(full, n + 1)
            dve.drain()
            V.tensor_tensor(lg, pj[n % 2][:, 0:PAST + NS], aconst("bias_s"), ALU.add).then_inc(free[n % 2], 1)
            dve.drain()
            V.tensor_reduce(smx, lg, AX_X, ALU.max)
            dve.drain()
            V.tensor_scalar(snb, smx, -SCALE, None, ALU.mult).then_inc(s_bias_done, 1)
            dve.wait_ge(s_exp_done, 1)
            V.reciprocal(sinv, ssum)
            dve.drain()
            V.tensor_scalar(lg, lg, sinv, coef, ALU.mult, ALU.mult).then_inc(s_probs, 1)
            n = BASE["p_turn"]
            dve.wait_ge(full, n + 1)
            V.tensor_reduce(diag[:, 0, :], pj[n % 2][:, 0:PAST].rearrange("p (g c) -> p g c", c=2), AX_X, ALU.add)
            V.tensor_reduce(diag[0:NS, 1, 0:NS * HEADS],
                            pj[n % 2][0:NS, PAST:PAST + P].rearrange("p (g c) -> p g c", c=2), AX_X,
                            ALU.add).then_inc(free[n % 2], 1)

            units = [(hd, i) for hd in range(HEADS) for i in range(TB)]
            dve.wait_ge(vpair_used, NS)
            for u in range(len(units) + 1):
                if u < len(units):
                    hd, i = units[u]
                    k = (i + 1) * P
                    n = BASE["attn"] + u
                    dve.wait_ge(full, n + 1)
                    V.scalar_tensor_tensor(out=logit[:, u % 2, :, 0:k],
                                           in0=aconst("dist")[:, SEQ - k:SEQ].rearrange("p (a k) -> p a k", a=1)
                                           .broadcast_to([P, 2, k]),
                                           scalar=SLOPES[hd] / SCALE,
                                           in1=pj[n % 2].rearrange("p (c k) -> p c k", c=2)[:, :, 0:k],
                                           op0=ALU.mult, op1=ALU.add).then_inc(free[n % 2], 1)
                    dve.drain()
                    V.tensor_reduce(mx[:, u % 2, :], logit[:, u % 2, :, 0:k], AX_X, ALU.max)
                    dve.drain()
                    V.tensor_scalar(nb[:, u % 2, :], mx[:, u % 2, :], -SCALE, None, ALU.mult).then_inc(a_logits, 1)
                if u >= 1:
                    v = u - 1
                    k = (units[v][1] + 1) * P
                    dve.wait_ge(a_exps, v + 1)
                    V.reciprocal(linv[:, v % 2, :], lsum[:, v % 2, :])
                    dve.drain()
                    V.tensor_scalar(linv[:, v % 2, 1:2], linv[:, v % 2, 1:2], neglam, None, ALU.mult)
                    if v >= 2:
                        dve.wait_ge(a_wT_ps, v - 1)
                    V.tensor_scalar(wrow[:, v % 2, 0:k], logit[:, v % 2, 0, 0:k], linv[:, v % 2, 0:1], None, ALU.mult)
                    dve.drain()
                    V.scalar_tensor_tensor(out=wrow[:, v % 2, 0:k], in0=logit[:, v % 2, 1, 0:k],
                                           scalar=linv[:, v % 2, 1:2], in1=wrow[:, v % 2, 0:k],
                                           op0=ALU.mult, op1=ALU.add).then_inc(a_w, 1)
                    dve.drain()
            for hd in range(HEADS):
                n = BASE["subln"] + hd
                rr = rms_buf(hd)
                dve.wait_ge(rms_ready, hd + 1)
                V.reciprocal(rr, rr)
                dve.drain()
                for g in range(2):
                    o = V.scalar_tensor_tensor(out=oT[g][:, hd, :], in0=oT[g][:, hd, :], scalar=gsub,
                                               in1=rr[:, G_OFF[g]:G_OFF[g] + G_W[g]], op0=ALU.mult, op1=ALU.mult)
                o.then_inc(o_normed, 1)
                dve.drain()

            def norm_a(x):
                m, i = rows(x.b), x.e % 2
                row = h[0:m, x.b, :]
                if x.tiles is not None:
                    dve.wait_ge(acc_free, x.tiles)
                for a in range(2):
                    V.bn_stats(stats[0:m, a, :], row[:, a * 512:(a + 1) * 512])
                dve.drain()
                V.bn_aggr(mv[0:m, i, :], stats[0:m].rearrange("p a s -> p (a s)"))
                dve.drain()
                dve.sem_inc(var_ready, 1)
                dve.wait_ge(s_ln, 32 * x.load)
                V.scalar_tensor_tensor(out=row, in0=row, scalar=mv[0:m, i, 0:1], in1=lng[0:m, :],
                                       op0=ALU.subtract, op1=ALU.mult)

            def norm_b(x):
                m, i = rows(x.b), x.e % 2
                row = h[0:m, x.b, :]
                dve.wait_ge(std_ready, x.e + 1)
                V.reciprocal(rstd[0:m, i], rstd[0:m, i])
                dve.drain()
                V.scalar_tensor_tensor(out=row, in0=row, scalar=rstd[0:m, i], in1=lnb[0:m, :],
                                       op0=ALU.mult, op1=ALU.add).then_inc(ln_done, 1)

            def convolve(x):
                g, j, n, w = x.g, x.j, x.n, G_W[x.g]
                last = 2 * P + 2
                dve.wait_ge(bank_free[(n - 1) % BANKS], bank_freed(n - 1) + 1)
                dve.wait_ge(bank_full, n + 1)
                if j == 0 and g == 0:
                    V.memset(gx[:, :, 0:2], 0.0)
                elif j == 0:
                    V.tensor_copy(gx[:, :, 0:2], carry[:])
                V.tensor_tensor(gx[:, j, 2:2 + w], c_st[:, j % 2, 0:w], bank[:, n % BANKS, 0:w],
                                ALU.mult).then_inc(bank_free[n % BANKS], 1)
                dve.drain()
                V.tensor_scalar(z[:, 0:2 * P], gx[:, j, 0:2 * P], cw[:, 0, j:j + 1], None, ALU.mult)
                if g == 0:
                    V.tensor_copy(carry[:, j, :], gx[:, j, last - 2:last])
                else:
                    V.tensor_scalar(z[:, 2 * P:w], state[:, j, 0, :], cw[:, 0, j:j + 1], None, ALU.mult)
                    V.tensor_copy(tail[:, j, :], gx[:, j, last - 2:last + NS])
                dve.drain()
                V.scalar_tensor_tensor(out=z[:, 0:2 * P], in0=gx[:, j, 1:1 + 2 * P], scalar=cw[:, 1, j:j + 1],
                                       in1=z[:, 0:2 * P], op0=ALU.mult, op1=ALU.add)
                if g == 1:
                    V.scalar_tensor_tensor(out=z[:, 2 * P:w], in0=state[:, j, 1, :], scalar=cw[:, 1, j:j + 1],
                                           in1=z[:, 2 * P:w], op0=ALU.mult, op1=ALU.add)
                dve.drain()
                V.scalar_tensor_tensor(out=z[:, 0:w], in0=gx[:, j, 2:2 + w], scalar=cw[:, 2, j:j + 1],
                                       in1=z[:, 0:w], op0=ALU.mult, op1=ALU.add)
                if g == 1 and j == C - 1:
                    dve.sem_inc(tail_ready, 1)

            def route_keys(unit):
                dve.wait_ge(sc_ready, unit + 2)
                V.tensor_copy(r_sc, tp[0][:, 0:256]).then_inc(sc_read, 1)
                dve.drain()
                for c in range(2):
                    V.max(r_v[:, c * 16:c * 16 + 8], r_sc[:, c * P:(c + 1) * P])
                dve.drain()
                for c in range(2):
                    V.max_index(r_si[:, c * 16:c * 16 + 8], r_v[:, c * 16:c * 16 + 8], r_sc[:, c * P:(c + 1) * P])
                    V.match_replace(r_wk[:, c * P:(c + 1) * P], r_v[:, c * 16:c * 16 + 8], r_sc[:, c * P:(c + 1) * P],
                                    LOWEST)

            def route_pairs():
                dve.drain()
                for c in range(2):
                    V.max(r_v[:, c * 16 + 8:c * 16 + 16], r_wk[:, c * P:(c + 1) * P])
                dve.drain()
                for c in range(2):
                    V.max_index(r_si[:, c * 16 + 8:c * 16 + 16], r_v[:, c * 16 + 8:c * 16 + 16],
                                r_wk[:, c * P:(c + 1) * P])
                V.tensor_tensor(r_cand.rearrange("p (i j) -> p i j", j=16),
                                r_v[:, 0:16].rearrange("p (i j) -> p i j", j=1).broadcast_to([P, 16, 16]),
                                r_v[:, 16:32].rearrange("p (i j) -> p i j", i=1).broadcast_to([P, 16, 16]), ALU.add)
                dve.drain()
                V.tensor_copy(r_sif, r_si)
                V.max(r_tv[:, 0:8], r_cand)

            def route_top():
                dve.drain()
                V.max_index(r_ti[:, 0:8], r_tv[:, 0:8], r_cand)
                V.match_replace(r_wk, r_tv[:, 0:8], r_cand, LOWEST)
                dve.drain()
                V.max(r_tv[:, 8:16], r_wk)
                V.tensor_scalar(r_nm, r_tv[:, 0:1], -1.0, None, ALU.mult).then_inc(top_ready, 1)
                dve.drain()
                V.max_index(r_ti[:, 8:16], r_tv[:, 8:16], r_wk)
                dve.drain()
                V.tensor_scalar(r_ij[:, 0:16], r_ti, 4, None, ALU.logical_shift_right)
                V.tensor_scalar(r_ij[:, 16:32], r_ti, 15, None, ALU.bitwise_and)
                dve.drain()
                V.tensor_copy(r_ijf, r_ij)

            def route_ids(b, hd):
                dve.drain()
                V.tensor_tensor(r_eq.rearrange("p (k i) -> p k i", i=16),
                                r_ijf.rearrange("p (k i) -> p k i", i=1).broadcast_to([P, 32, 16]),
                                const("iota").rearrange("p (k i) -> p k i", k=1).broadcast_to([P, 32, 16]),
                                ALU.is_equal)
                dve.drain()
                eq4 = r_eq.rearrange("p (c k i) -> p c k i", c=2, i=16)
                V.tensor_tensor(eq4, eq4, r_sif.rearrange("p (c k i) -> p c k i", c=2, k=1).broadcast_to([P, 2, 16, 16]),
                                ALU.mult)
                dve.drain()
                V.tensor_reduce(r_e, r_eq.rearrange("p (k i) -> p k i", i=16), AX_X, ALU.add)
                dve.drain()
                V.scalar_tensor_tensor(out=idx[:, b, hd, :], in0=r_e[:, 0:16], scalar=float(KEYS), in1=r_e[:, 16:32],
                                       op0=ALU.mult, op1=ALU.add).then_inc(idx_done, 1)

            def gates(b, hd, unit):
                dve.wait_ge(gexp_done, unit + 1)
                V.reciprocal(r_inv, r_sum)
                dve.drain()
                V.tensor_scalar(gate[:, b, hd, :], r_ex, r_inv, None, ALU.mult).then_inc(g_done, 1)

            def background(x):
                n = x.n
                if x.kind in ("mix", "norm_a", "norm_b", "proj", "route") or x.kind == "conv" and x.k > 0:
                    dve.drain()
                if x.kind == "mix":
                    m = rows(x.b)
                    part_of_h = h[0:m, x.b, x.p * PW:(x.p + 1) * PW]
                    if n == 0:
                        dve.wait_ge(s_h, 32)
                    dve.wait_ge(bank_full, n + 1)
                    V.scalar_tensor_tensor(out=part_of_h, in0=part_of_h, scalar=ALPHA, in1=bank[0:m, n % BANKS, 0:PW],
                                           op0=ALU.mult, op1=ALU.add).then_inc(bank_free[n % BANKS], 1)
                elif x.kind == "norm_a":
                    norm_a(x)
                elif x.kind == "norm_b":
                    norm_b(x)
                elif x.kind == "proj":
                    m, cols = rows(x.b), slice(x.p * PW, (x.p + 1) * PW)
                    y = sig[x.g][0:m, local(x.b) // P, cols]
                    if x.first:
                        banks_read(dve, n)
                    dve.wait_ge(bank_full, n + 1)
                    V.tensor_tensor(y, y, bank[0:m, n % BANKS, 0:PW], ALU.mult).then_inc(bank_free[n % BANKS], 1)
                    dve.drain()
                    V.tensor_tensor(h[0:m, x.b, cols], h[0:m, x.b, cols], y, ALU.add).then_inc(ple_done, 1)
                elif x.kind == "conv" and x.k == 1:
                    convolve(x)
                elif x.kind == "conv" and x.k == 2:
                    w = G_W[x.g]
                    dve.wait_ge(bank_full, n + 1)
                    V.tensor_tensor(gx[:, x.j, 2:2 + w], z[:, 0:w], bank[:, n % BANKS, 0:w],
                                    ALU.mult).then_inc(bank_free[n % BANKS], 1)
                elif x.kind == "route":
                    if x.i == 0:
                        route_keys(x.u)
                    elif x.i == 1:
                        route_pairs()
                    elif x.i == 2:
                        route_top()
                    else:
                        route_ids(x.b, x.hd)
                        gates(x.b, x.hd, x.u)

            def four_dots(G, q):
                for r in range(4 * q, 4 * q + 4):
                    dve.wait_ge(gathered[r], G * 16 + 16)
                    if r == 0:
                        dve.wait_ge(gelu_done, G * 2 + 2)
                    V.tensor_tensor_reduce(uv[:, r, 0:D], uv[:, r, 0:D], xcur[:], 1.0, 0.0, ALU.mult, ALU.add,
                                           dots[:, G % 2, r:r + 1]).then_inc(dot_done, 1)

            def spread_sample(prep):
                V.tensor_copy(x_ig[0:NS, 0:P], idx[0:NS, TB, :, :].rearrange("p h k -> p (h k)"))
                V.tensor_copy(x_ig[0:NS, P:2 * P], gate[0:NS, TB, :, :].rearrange("p h k -> p (h k)")).then_inc(ig_ready, 1)
                for half in range(2):
                    n = prep[half].n
                    dve.wait_ge(bank_full, n + 1)
                    V.tensor_copy(xcur[:, half * 512:(half + 1) * 512], bank[:, n % BANKS, :]) \
                        .then_inc(bank_free[n % BANKS], 1)
                n = prep[2].n
                dve.wait_ge(bank_full, n + 1)
                V.tensor_tensor(x_pr.rearrange("p (g k) -> p g k", k=TOPK),
                                bank[:, n % BANKS, 0:256].rearrange("p (g k) -> p g k", k=TOPK),
                                const("kmask").rearrange("p (g k) -> p g k", g=1).broadcast_to([P, 16, TOPK]),
                                ALU.mult).then_inc(bank_free[n % BANKS], 1)
                dve.drain()
                V.tensor_reduce(x_sel, x_pr.rearrange("p (g k) -> p g k", k=TOPK), AX_X, ALU.add)
                dve.drain()
                V.tensor_copy(ixs, x_sel[:, 0:HEADS])
                V.tensor_copy(gs8, x_sel[:, HEADS:2 * HEADS]).then_inc(ixs_ready, 1)
                dve.drain()

            later = []
            for kind, layer, b, prep, lots in steps:
                if kind == "alone":
                    for x in later + lots:
                        background(x)
                    later = []
                    continue
                for t, G, q, hd, lot in window_quarters(layer, b, lots):
                    for x in later:
                        background(x)
                    later = lot
                    if t == 0 and b < TB:
                        dve.drain()
                        V.tensor_copy(xcur[:], h[:, b, :]).then_inc(x_ready, 1)
                        dve.drain()
                    elif t == 0:
                        dve.drain()
                        spread_sample(prep)
                    four_dots(G, q)

        @block.tensor
        def _(pe):
            mm = nc.tensor.matmul

            pe.wait_ge(s_hT, 16)
            src = [hT, gxT]
            for f in range(2 * HEADS):
                n, slot = BASE["qk"] + f, f // 2 % SLOTS
                if f % 2 == 0:
                    pe.wait_ge(s_panel[slot], 16 * (f // 2 // SLOTS + 1))
                pe.wait_ge(free[n % 2], freed(n))
                w = panel[:, slot, :].rearrange("p (c n) -> p c n", c=C)[:, :, (f % 2) * P:(f % 2 + 1) * P]
                for g in range(2):
                    if f == 0 and g == 1:
                        pe.wait_ge(s_hT, 32)
                    for c in range(C):
                        m = mm(pj[n % 2][:, PW + G_OFF[g]:PW + G_OFF[g] + G_W[g]], w[:, c, :], src[g][:, c, 0:G_W[g]],
                               start=(c == 0), stop=(c == C - 1))
                m.then_inc(full, 1)
            for p in range(4):
                slot = (8 + p) % SLOTS
                pe.wait_ge(s_panel[slot], 16 * ((8 + p) // SLOTS + 1))
                w = panel[:, slot, :].rearrange("p (c n) -> p c n", c=C)
                for b in range(BLOCKS):
                    n, m = BASE["v"] + p * BLOCKS + b, rows(b)
                    pe.wait_ge(free[n % 2], freed(n))
                    for c in range(C):
                        last = mm(pj[n % 2][0:m, 0:PW], src[group_of(b)][:, c, local(b):local(b) + m], w[:, c, :],
                                  start=(c == 0), stop=(c == C - 1))
                    last.then_inc(full, 1)
            pe.wait_ge(s_const, 16)
            all_read(pe, BASE["v"])
            for b in range(BLOCKS):
                n, m = BASE["k_rows"] + b, rows(b)
                pe.wait_ge(free[n % 2], freed(n))
                for hd in range(HEADS):
                    t = nc.tensor.transpose(pj[n % 2][0:m, hd * P:(hd + 1) * P], qT3[:, HEADS + hd, b * P:b * P + m],
                                            const("ident"))
                t.then_inc(full, 1)
            n = BASE["q_rows"]
            pe.wait_ge(free[n % 2], freed(n))
            for hd in range(HEADS):
                t = nc.tensor.transpose(pj[n % 2][0:NS, hd * P:(hd + 1) * P], qT3[:, hd, SEQ:T], const("ident"))
            t.then_inc(full, 1)
            pe.wait_ge(s_attn_c, 16)
            all_read(pe, BASE["q_spread"])
            for b in range(NS):
                n = BASE["q_spread"] + b
                pe.wait_ge(free[n % 2], freed(n))
                for half in range(2):
                    m = mm(pj[n % 2][:, half * 512:(half + 1) * 512], aconst("pick")[0:NS, b * P:(b + 1) * P],
                           xcur[0:NS, half * 512:(half + 1) * 512], start=True, stop=True)
                m.then_inc(full, 1)
            n = BASE["s_turn"]
            pe.wait_ge(s_scores, 1)
            pe.wait_ge(free[n % 2], freed(n))
            for j in range(2):
                nc.tensor.transpose(pj[n % 2][:, j * P:(j + 1) * P], s_pos[:, j, :], const("ident"))
            nc.tensor.transpose(pj[n % 2][:, PAST:PAST + NS], s_new[0:NS, :], const("ident")[0:NS, 0:NS]).then_inc(full, 1)
            n = BASE["p_turn"]
            pe.wait_ge(s_probs, 1)
            pe.wait_ge(free[n % 2], freed(n))
            for j in range(2):
                nc.tensor.transpose(pj[n % 2][:, j * P:(j + 1) * P], yb[:, j * P:(j + 1) * P], const("ident"))
            nc.tensor.transpose(pj[n % 2][0:NS, PAST:PAST + P], yb[:, PAST:PAST + NS], const("ident")).then_inc(full, 1)
            n = BASE["s_out"]
            all_read(pe, n)
            for b in range(NS):
                pair = NS + b
                pe.wait_ge(s_pair[pair % 2], 32 * (pair // 2 + 1))
                for hd in range(HEADS):
                    col = pj[n % 2][:, hd * NS + b:hd * NS + b + 1]
                    g = b * HEADS + hd
                    for j in range(N_PAGES):
                        m = mm(col, kv_pages[:, pair % 2, j, hd * P:(hd + 1) * P],
                               diag[:, 0, j * NS * HEADS + g:j * NS * HEADS + g + 1], start=(j == 0), stop=False)
                    if hd == HEADS - 1:
                        m.then_inc(vpair_used, 1)
                    m = mm(col, v_rows[0:NS, TB, hd * P:(hd + 1) * P], diag[0:NS, 1, g:g + 1], start=False, stop=True)
            m.then_inc(full, 1)

            units = [(hd, i) for hd in range(HEADS) for i in range(TB)]
            for u in range(len(units) + 3):
                if u < len(units):
                    hd, i = units[u]
                    k = (i + 1) * P
                    n = BASE["attn"] + u
                    pe.wait_ge(free[n % 2], freed(n))
                    for c in range(2):
                        m = mm(pj[n % 2][:, c * 512:c * 512 + k], qT3[c * HD:(c + 1) * HD, hd, i * P:(i + 1) * P],
                               qT3[c * HD:(c + 1) * HD, HEADS + hd, 0:k], start=True, stop=True)
                    m.then_inc(full, 1)
                if 2 <= u <= len(units) + 1:
                    v = u - 2
                    pe.wait_ge(a_w, v + 1)
                    if v >= 2:
                        pe.wait_ge(a_wT, v - 1)
                    for kb in range(units[v][1] + 1):
                        t = nc.tensor.transpose(tp[v % 2][:, kb * P:(kb + 1) * P], wrow[:, v % 2, kb * P:(kb + 1) * P],
                                                const("ident"))
                    t.then_inc(a_wT_ps, 1)
                if u >= 3:
                    v = u - 3
                    hd, i = units[v]
                    pe.wait_ge(a_wT, v + 1)
                    pe.wait_ge(a_ofree, v + 1)
                    for kb in range(i + 1):
                        m = mm(acc[:, (v % 2) * 512:(v % 2) * 512 + P], v_rows[:, kb, hd * P:(hd + 1) * P],
                               wT[:, v % 2, kb * P:(kb + 1) * P], start=(kb == 0), stop=(kb == i))
                    m.then_inc(a_o, 1)
            for hd in range(HEADS):
                n = BASE["subln"] + hd
                pe.wait_ge(sq_ready, hd + 1)
                pe.wait_ge(free[n % 2], freed(n))
                for g in range(2):
                    m = mm(pj[n % 2][:, PW + G_OFF[g]:PW + G_OFF[g] + G_W[g]], aconst("mean"),
                           squares(hd)[:, G_OFF[g]:G_OFF[g] + G_W[g]], start=True, stop=True)
                m.then_inc(full, 1)

            def key_scores(hd, unit):
                pe.wait_ge(q_staged, unit + 1)
                pe.wait_ge(sc_read, unit + 1)
                for c in range(2):
                    m = mm(tp[0][:, c * P:(c + 1) * P], qst[:, c * P:(c + 1) * P], keys[:, hd * 2 + c, :],
                           start=True, stop=True)
                m.then_inc(sc_ready, 1)

            def start_tile(src, count):
                pe.wait_ge(acc_free, count)
                for half in range(2):
                    mm(acc[:, half * 512:(half + 1) * 512], const("alpha_eye"), src[:, half * 512:(half + 1) * 512],
                       start=True, stop=True, skip_group_check=True)

            def add_four(G, q):
                for r in range(4 * q, 4 * q + 4):
                    pe.wait_ge(diag_ready, G * RING + r + 1)
                    for half in range(2):
                        m = mm(acc[:, half * 512:(half + 1) * 512], diag[:, r % DIAGS, :],
                               uv[:, r, D + half * 512:D + (half + 1) * 512], start=False, stop=True,
                               skip_group_check=True)
                    m.then_inc(slot_done, 1)

            def open_product(x):
                if x.panel is not None:
                    pe.wait_ge(s_panel[x.panel % SLOTS], 16 * (x.panel // SLOTS + 1))
                if x.fence:
                    banks_read(pe, x.n)
                pe.wait_ge(bank_free[x.n % BANKS], bank_freed(x.n))

            def token_major(x, src, chunks, weights):
                m = rows(x.b)
                for c in range(chunks):
                    last = mm(bank[0:m, x.n % BANKS, 0:PW], src[:, c, local(x.b):local(x.b) + m], weights[:, c, :],
                              start=(c == 0), stop=(c == chunks - 1))
                last.then_inc(bank_full, 1)

            def feature_major(x, columns_of):
                w = panel[:, x.panel % SLOTS, :].rearrange("p (c n) -> p c n", c=C)[:, :, columns_of * P:(columns_of + 1) * P]
                for c in range(C):
                    last = mm(bank[:, x.n % BANKS, 0:G_W[x.g]], w[:, c, :], hT[:, c, 0:G_W[x.g]],
                              start=(c == 0), stop=(c == C - 1))
                last.then_inc(bank_full, 1)

            def background(x):
                if x.n is not None:
                    open_product(x)
                    weights = panel[:, (x.panel or 0) % SLOTS, :].rearrange("p (c n) -> p c n", c=C)
                if x.kind == "mix" and x.layer == 0:
                    if x.n == 0:
                        pe.wait_ge(o_normed, HEADS)
                    token_major(x, oT[x.g], C, weights)
                elif x.kind == "mix":
                    token_major(x, gx[:, :, 2:2 + G_W[x.g]], C, weights)
                elif x.kind == "turn":
                    if x.ready == "norm":
                        pe.wait_ge(ln_done, x.count)
                    else:
                        pe.wait_ge(ple_done, x.count)
                    m = rows(x.b)
                    for q in range(4):
                        c = 4 * x.half + q
                        last = nc.tensor.transpose(bank[:, x.n % BANKS, q * P:q * P + m], h[0:m, x.b, c * P:(c + 1) * P],
                                                   const("ident")[0:m, 0:m])
                    last.then_inc(bank_full, 1)
                elif x.kind == "pq":
                    feature_major(x, x.f % 2)
                elif x.kind == "conv":
                    feature_major(x, x.i % 2)
                elif x.kind == "gate":
                    token_major(x, hT, C, weights)
                elif x.kind == "proj":
                    pe.wait_ge(s_pT, 16 * x.load)
                    wp = panel[:, x.panel % SLOTS, :].rearrange("p (c n) -> p c n", c=2)
                    token_major(x, pTs, 2, wp[:, :, x.p * PW:(x.p + 1) * PW])
                elif x.kind == "route" and x.i == 0:
                    if x.b == 0 and x.hd == 0:
                        pe.wait_ge(s_keys, 16 * (x.layer + 1))
                    key_scores(x.hd, x.u)

            for kind, layer, b, prep, lots in steps:
                if kind == "alone":
                    for x in lots:
                        background(x)
                    continue
                for i, x in enumerate(prep):
                    open_product(x)
                    if i < 2:
                        last = mm(bank[:, x.n % BANKS, :], const("spread")[0:NS, :], h[0:NS, TB, i * 512:(i + 1) * 512],
                                  start=True, stop=True)
                    else:
                        pe.wait_ge(ig_ready, layer + 1)
                        last = mm(bank[:, x.n % BANKS, 0:256], const("spread")[0:NS, :], x_ig[0:NS, :],
                                  start=True, stop=True)
                    last.then_inc(bank_full, 1)
                if b < TB:
                    pe.wait_ge(x_ready, layer * TB + b + 1)
                    start_tile(xcur, layer * BLOCKS + b + 1)
                else:
                    start_tile(h[:, TB, :], layer * BLOCKS + b + 1)
                for t, G, q, hd, lot in window_quarters(layer, b, lots):
                    for x in lot:
                        background(x)
                    add_four(G, q)


def weight_panels(i):
    out = np.zeros((len(PANEL_AT), P, C * PW), np.float32)

    def put(name, layer, w):
        for k in range(w.shape[1] // PW):
            if (name, layer, k) in PANEL_AT:
                out[PANEL_AT[name, layer, k]] = w[:, k * PW:(k + 1) * PW].reshape(C, P, PW).transpose(1, 0, 2) \
                    .reshape(P, C * PW)

    qkv = i["w_attn_qkv"][0]
    put("qk", 0, qkv[:, 0:2 * D])
    put("v", 0, qkv[:, 2 * D:3 * D])
    put("mix", 0, i["w_attn_o"][0])
    put("mix", 1, i["w_conv_out"][0])
    for layer in range(DEPTH):
        put("pq", layer, i["w_peer_q"][layer])
        put("gate", layer, i["w_ple_gate"][layer])
        out[PANEL_AT["proj", layer, 0]] = i["w_ple_proj"][layer].reshape(2, P, D).transpose(1, 0, 2).reshape(P, 2 * D)
    w = i["w_conv_in"][0].reshape(D, 3, C, P)[:, [1, 2, 0]].transpose(0, 2, 1, 3).reshape(D, 3 * D)
    put("conv", 1, w)
    return out


def embedding_rows(i):
    p = np.concatenate([i["p_prompt"][:, 0], i["p_sample"][:, :, 0]], axis=1)
    return p.reshape(DEPTH, T, 2, P).transpose(0, 3, 2, 1)


def kernel(**inputs):
    import concourse.bacc as bacc
    from concourse.bass_utils import run_bass_kernel_spmd as run

    i = {k: np.asarray(v) for k, v in inputs.items()}
    h0 = np.concatenate([i["x_prompt"][0], i["x_sample"][:, 0]])
    arrays = {
        "h0": h0,
        "h0T": h0.T.reshape(C, P, T).transpose(1, 0, 2),
        "consts": constants(),
        "panels": weight_panels(i),
        "ple_rows": embedding_rows(i),
        "keysT": i["peer_keys"].transpose(0, 4, 1, 2, 3).reshape(DEPTH, P, 16, KEYS),
        "uv0": np.concatenate([i["peer_u"][0], i["peer_v"][0]], axis=1),
        "uv1": np.concatenate([i["peer_u"][1], i["peer_v"][1]], axis=1),
        "cache_k": i["cache_k"][0].reshape(POOL_PAGES, PAGE, D),
        "cache_v": i["cache_v"][0].reshape(POOL_PAGES, PAGE, D),
        "pages": i["page_table"].reshape(1, NS * N_PAGES),
        "wlam": i["w_attn_lambda"].reshape(1, 4 * HD),
        "subg": i["attn_subln_g"].reshape(P, 1),
        "ln": np.stack([i["ln_g"].reshape(4, D), i["ln_b"].reshape(4, D)], axis=1),
        "convw": i["conv_w"][0].reshape(3, C, P).transpose(2, 0, 1),
        "state_conv": i["state_conv"][0],
        "stateT": i["state_conv"][0].reshape(NS, 2, C, P).transpose(3, 2, 1, 0),
    }
    outs = {"y_p": (SEQ, D), "y_s": (NS, D), "nk_p": (SEQ, D), "nv_p": (SEQ, D), "nk_s": (NS, D), "nv_s": (NS, D),
            "cp": (2, D), "cs": (NS, 2, D)}
    nc = bacc.Bacc("TRN2", target_bir_lowering=False, num_devices=1)
    feed, args = {}, []
    for name, a in arrays.items():
        a = np.ascontiguousarray(a)
        feed["in_" + name] = a
        args.append(nc.dram_tensor("in_" + name, a.shape, mybir.dt.from_np(a.dtype), kind="ExternalInput").ap())
    for name, shape in outs.items():
        args.append(nc.dram_tensor("out_" + name, shape, F32, kind="ExternalOutput").ap())
    build(nc, *args)
    r = run(nc, [feed], core_ids=[0]).results[0]
    return (r["out_y_p"].reshape(1, SEQ, D), r["out_y_s"].reshape(NS, 1, D),
            r["out_nk_p"].reshape(1, 1, SEQ, HEADS, P), r["out_nv_p"].reshape(1, 1, SEQ, HEADS, P),
            r["out_nk_s"].reshape(1, NS, 1, HEADS, P), r["out_nv_s"].reshape(1, NS, 1, HEADS, P),
            r["out_cp"].reshape(1, 1, 2, D), r["out_cs"].reshape(1, NS, 2, D))
```

```python
import math
from contextlib import ExitStack

import numpy as np

import concourse.bass as bass
from concourse import mybir

ALU = mybir.AluOpType
ACT = mybir.ActivationFunctionType
F32 = mybir.dt.float32
I32 = mybir.dt.int32
U32 = mybir.dt.uint32
AX_X = mybir.AxisListType.X

P = 128
D = 1024
C = D // P
SEQ = 512
NS = 8
T = SEQ + NS
TB = SEQ // P
BLOCKS = TB + 1
HEADS = 8
HD = 64
PAGE = 128
N_PAGES = 2
PAST = PAGE * N_PAGES
POOL_PAGES = 20
TOPK = 16
KEYS = 128
EXPERTS = KEYS * KEYS
PLE = 256
DEPTH = 2
ALPHA = (2 * DEPTH) ** 0.25
LAM_INIT = 0.8 - 0.6 * math.exp(0.0)
EPS = 1e-5
NEG = -1e30
LOWEST = -3.0e38
SCALE = HD ** -0.5
SLOPES = [2.0 ** -(h + 1) for h in range(HEADS)]
RING = 8
GROUPS = TB * HEADS * 2 + 1
DIAGS = 4

GROUP_TILES = [(0, 1), (2, 3, 4)]
TILE_ORDER = [(0, 1, 2, 3, TB), (0, 1, 2, TB, 3)]
G_OFF = [0, 2 * P]
G_W = [2 * P, T - 2 * P]
PW = 256
SLOTS = 3
BANKS = 4

ORDER = [("qk", f) for f in range(2 * HEADS)] + [("k_rows", b) for b in range(BLOCKS)] + [("q_rows", 0)] \
    + [("v", i) for i in range(4)]
for _b in range(NS):
    ORDER += [("q_spread", _b), ("v", 4 + 2 * _b), ("v", 5 + 2 * _b)]
S_TURN, P_TURN, O_TURN = 3, 6, 15
S_OUT = {8: 0, 12: 1}
for _u in range(TB * HEADS):
    ORDER += [("s_turn", 0)] * (_u == S_TURN) + [("p_turn", 0)] * (_u == P_TURN)
    ORDER += [("s_out", S_OUT.get(_u))] * (_u in S_OUT) + [("o_turn", 0)] * (_u == O_TURN) + [("attn", _u)]
ORDER += [("subln", hd) for hd in range(HEADS)]
USE = {name: n for n, name in enumerate(ORDER)}


def group_of(b):
    return 0 if b < 2 else 1


def place(layer, b):
    return layer * BLOCKS + TILE_ORDER[layer].index(b)


def rows(b):
    return P if b < TB else NS


class Piece:

    def __init__(self, kind, layer=0, g=0, b=0, p=0, f=0, half=0, ready="", count=0, e=0, load=0, tiles=None,
                 i=0, j=0, k=0, first=False, hd=0, u=0):
        self.kind, self.product, self.n, self.panel, self.fence = kind, False, None, None, False
        self.layer, self.g, self.b = layer, g, b
        self.p, self.f, self.half = p, f, half
        self.ready, self.count = ready, count
        self.e, self.load, self.tiles = e, load, tiles
        self.i, self.j, self.k = i, j, k
        self.first, self.hd, self.u = first, hd, u


COST = {"mix": 8, "gate": 8, "conv": 8, "pq": 8, "proj": 2, "turn": 2, "norm_a": 4, "norm_b": 3, "route": 1,
        "stage": 1, "side": 1, "i_spread": 1, "x_spread": 1}


class Plan:

    def __init__(self):
        self.panels = []
        self.release = []
        self.norms = 0
        self.projs = 0
        self.routes = 0
        self.ln_loads = []
        self.embeds = []
        self.ln_of = {}
        self.ple_of = {}
        for p in range(8):
            self.add_panel("qk", 0, p, ("pair", USE["qk", 2 * p + 1] + 1))
        for p in range(4):
            self.add_panel("v", 0, p, ("pair", USE["v", BLOCKS * (p + 1) - 1] + 1))

    def add_panel(self, name, layer, index, release=None):
        self.panels.append((name, layer, index))
        self.release.append(release)
        return len(self.panels) - 1

    def product(self, piece, panel=None):
        piece.product, piece.panel = True, panel
        return piece

    def number(self, steps):
        n = 0
        for kind, layer, b, lots in steps:
            for lot in lots:
                for x in lot:
                    if x.product:
                        x.n = n
                        n += 1
                        if x.panel is not None:
                            self.release[x.panel] = ("bank", n)

    def mix(self, layer, g):
        out = []
        for p in range(4):
            w = self.add_panel("mix", layer, p)
            for b in GROUP_TILES[g]:
                out.append(self.product(Piece("mix", layer=layer, g=g, p=p, b=b), w))
        out[0].fence = True
        return out

    def norm(self, k, tiles, after_experts):
        if not self.ln_loads or self.ln_loads[-1][0] != k:
            self.ln_loads.append((k, self.norms, len(self.panels)))
        a, c = [], []
        for b in tiles:
            e = self.norms
            self.norms += 1
            a.append(Piece("norm_a", b=b, e=e, load=len(self.ln_loads),
                           tiles=self.tile_count(k // 2, b) if after_experts else None))
            c.append(Piece("norm_b", b=b, e=e))
            self.ln_of[b] = e + 1
        return a[:2] + c[:1] + a[2:] + c[1:]

    @staticmethod
    def tile_count(layer, b):
        return place(layer, b) + 2

    def turn(self, tiles, of, ready):
        out = []
        for b in tiles:
            for half in range(2):
                out.append(self.product(Piece("turn", b=b, half=half, ready=ready, count=of[b])))
        return out

    def features(self, kind, layer, g):
        out = []
        for p in range(8):
            w = self.add_panel(kind, layer, p)
            for f in (2 * p, 2 * p + 1):
                out.append(self.product(Piece(kind, layer=layer, g=g, f=f), w))
        out[0].fence = True
        return out

    def conv(self, g):
        out = []
        for p in range(12):
            w = self.add_panel("conv", 1, p)
            for i in (2 * p, 2 * p + 1):
                out.append(self.product(Piece("conv", g=g, j=i // 3, k=i % 3, i=i), w))
        out[0].fence = True
        return out

    def embed(self, layer, tiles):
        g = group_of(tiles[0])
        out = []
        self.embeds.append((layer, g, self.projs, len(self.panels)))
        for p in range(4):
            w = self.add_panel("gate", layer, p)
            for b in tiles:
                out.append(self.product(Piece("gate", layer=layer, g=g, p=p, b=b), w))
        out[0].fence = True
        w = self.add_panel("proj", layer, 0)
        first = len(out)
        for b in tiles:
            for p in range(4):
                self.projs += 1
                out.append(self.product(Piece("proj", layer=layer, g=g, p=p, b=b, load=len(self.embeds), first=False), w))
            self.ple_of[b] = self.projs
        out[first].first = True
        return out

    def route(self, layer, b):
        out = []
        for hd in range(HEADS):
            for i in range(4):
                out.append(Piece("route", layer=layer, b=b, hd=hd, i=i, u=self.routes))
            self.routes += 1
        return [Piece("stage", layer=layer, b=b, hd=0, u=self.routes - HEADS)] + out

    def sample_rows(self, layer):
        return [Piece("side", layer=layer)], \
            [self.product(Piece("i_spread", layer=layer))] + [self.product(Piece("x_spread", half=i)) for i in range(2)]

    def next_layer(self, g):
        tiles = GROUP_TILES[g]
        out = self.norm(1, tiles, True) + self.turn(tiles, self.ln_of, "norm") + self.embed(0, tiles)
        out += self.turn(tiles, dict(self.ple_of), "embedding") + self.conv(g) + self.mix(1, g)
        return out + self.norm(2, tiles, False) + self.turn(tiles, self.ln_of, "norm") + self.features("pq", 1, g)

    def build(self):

        def window(layer, b, *lanes):
            lots = [[] for _ in range(4 * HEADS if b < TB else 2)]
            for first, last, pieces in lanes:
                total, so_far = sum(COST[x.kind] for x in pieces), 0
                at, before = first, None
                for x in pieces:
                    if before and (x.fence or x.kind == "turn" and before != "turn" or before == "stage"):
                        at = min(at + 1, last - 1)
                    at = max(at, first + int(so_far * (last - first) / total))
                    lots[at].append(x)
                    so_far += COST[x.kind]
                    before = x.kind
            steps.append(("window", layer, b, lots))

        def cut_at(pieces, share):
            total, so_far = sum(COST[x.kind] for x in pieces), 0
            for i, x in enumerate(pieces):
                if so_far >= share * total:
                    return pieces[:i], pieces[i:]
                so_far += COST[x.kind]
            return pieces, []

        first = self.mix(0, 0) + self.norm(0, GROUP_TILES[0], False) + self.turn(GROUP_TILES[0], self.ln_of, "norm")
        q, r = self.features("pq", 0, 0), self.route(0, 0)
        steps = [("alone", 0, 0, [first + q[:2] + r[:1] + q[2:4] + r[1:5] + q[4:6] + r[5:9]])]
        rest = []
        for hd in range(2, HEADS):
            rest += q[2 * hd + 2:2 * hd + 4] + r[1 + 4 * hd:5 + 4 * hd]
        bg = self.mix(0, 1) + self.norm(0, GROUP_TILES[1], False) + self.turn(GROUP_TILES[1], self.ln_of, "norm")
        r1 = self.route(0, 1)
        window(0, 0, (0, 16, rest), (16, 32, r1[:21]), (16, 32, bg))
        bg, r2 = self.features("pq", 0, 1), self.route(0, 2)
        window(0, 1, (0, 8, r1[21:]), (17, 32, r2[:21]), (0, 17, bg))
        r3, rs = self.route(0, 3), self.route(0, 4)
        bg = self.next_layer(0)
        early, late = cut_at(bg, 0.56)
        window(0, 2, (0, 6, r2[21:]), (6, 32, r3), (0, 32, early))
        side, spread = self.sample_rows(0)
        r0 = self.route(1, 0)
        window(0, 3, (0, 14, rs), (14, 15, side), (16, 17, spread), (19, 32, r0[:25]), (0, 28, late))
        window(0, 4)
        r1, r2, rs, r3 = (self.route(1, b) for b in TILE_ORDER[1][1:])
        bg = self.next_layer(1)
        early, late = cut_at(bg, 0.53)
        window(1, 0, (0, 5, r0[25:]), (5, 32, r1), (1, 32, early))
        window(1, 1, (19, 32, r2[:25]), (0, 29, late))
        bg = self.norm(3, GROUP_TILES[0], True) + self.turn(GROUP_TILES[0], self.ln_of, "norm") + self.embed(1, GROUP_TILES[0])
        side, spread = self.sample_rows(1)
        window(1, 2, (0, 5, r2[25:]), (5, 18, rs), (18, 19, side), (20, 21, spread), (21, 32, r3[:21]), (0, 32, bg))
        window(1, TB)

        def end(tiles):
            return self.norm(3, tiles, True) + self.turn(tiles, self.ln_of, "norm") + self.embed(1, tiles)

        window(1, 3, (0, 8, r3[21:]), (2, 30, end((2, TB))))
        steps.append(("alone", 1, 3, [end((3,))]))
        self.number(steps)
        return steps


def first_group(layer, b):
    before = TILE_ORDER[layer][:TILE_ORDER[layer].index(b)]
    return layer * GROUPS + sum(HEADS * 2 if x < TB else 1 for x in before)


def window_quarters(layer, b, lots):
    first = first_group(layer, b)
    return [(t, first + t // 2, t % 2, t // 4, lot) for t, lot in enumerate(lots)]


DRAM_PANELS = [("qk", 0, 8), ("v", 0, 4)] + [(name, layer, count) for name, count in
                                            (("mix", 4), ("pq", 8), ("gate", 4), ("proj", 1)) for layer in range(DEPTH)] \
    + [("conv", 1, 12)]
PANEL_AT = {}
for _name, _layer, _count in DRAM_PANELS:
    for _i in range(_count):
        PANEL_AT[_name, _layer, _i] = len(PANEL_AT)

CONST = [("ident", P), ("alpha_eye", P), ("group_of", P), ("spread", P), ("kmask", TOPK), ("iota", TOPK)]
ATTN_CONST = [("dist", SEQ), ("bias_s", PAST + NS), ("pick", NS * P), ("own", NS), ("mean", P), ("second", 1)]


def columns(parts):
    at, out = 0, {}
    for name, width in parts:
        out[name] = (at, at + width)
        at += width
    return out, at


CC, N_CONST = columns(CONST)
AC, N_ATTN = columns(ATTN_CONST)


def constants():
    p = np.arange(P)
    a = np.zeros((P, N_CONST + N_ATTN), np.float32)

    def put(cols, off, v):
        a[:v.shape[0], off + cols[0]:off + cols[1]] = v

    put(CC["ident"], 0, np.eye(P))
    put(CC["alpha_eye"], 0, np.eye(P) * ALPHA)
    put(CC["group_of"], 0, (p[:, None] // TOPK == p[None, :]).astype(np.float32))
    put(CC["spread"], 0, (np.arange(NS)[:, None] == p[None, :] // TOPK).astype(np.float32))
    put(CC["kmask"], 0, (p[:, None] % TOPK == np.arange(TOPK)[None, :]).astype(np.float32))
    put(CC["iota"], 0, np.tile(np.arange(TOPK), (P, 1)))
    j = np.arange(SEQ)
    dist = p[:, None] + (SEQ - P) - j[None, :]
    put(AC["dist"], N_CONST, np.where(dist >= 0, -dist, NEG))
    slope = np.array(SLOPES)[(p // 2) % HEADS] / SCALE
    bias = np.zeros((P, PAST + NS))
    bias[:, :PAST] = -slope[:, None] * (PAST - np.arange(PAST))[None, :]
    put(AC["bias_s"], N_CONST, bias)
    pick = np.zeros((NS, NS, P))
    for b in range(NS):
        pick[b, b] = 1
    put(AC["pick"], N_CONST, pick.reshape(NS, NS * P))
    put(AC["own"], N_CONST, np.where(np.eye(NS) > 0, 0, NEG))
    put(AC["mean"], N_CONST, np.full((P, P), 1 / P))
    put(AC["second"], N_CONST, (p % 2)[:, None])
    return a


def freed(n):
    return n // 2 + 1


def bank_freed(n):
    return n // BANKS + 1


def build(nc, h0, h0T, consts, panels, ple_rows, keysT, uv0, uv1, cache_k, cache_v, pages, wlam, subg, ln, convw,
          state_conv, stateT, y_p, y_s, nk_p, nv_p, nk_s, nv_s, cp, cs):
    uv_dram = [uv0, uv1]
    ctx = ExitStack()
    with ctx:
        def sb(name, shape, dt=F32):
            return ctx.enter_context(nc.sbuf_tensor(name, shape, dt))

        def sem(name):
            return ctx.enter_context(nc.semaphore(name))

        h = sb("h", [P, BLOCKS, D])
        hT = sb("hT", [P, C, G_W[1]])
        gx = sb("gx", [P, C, G_W[1] + 2])
        gxT = gx[:].rearrange("p c t -> p (c t)")[:, 0:C * G_W[1]].rearrange("p (c t) -> p c t", c=C)
        QTN = 16 * T
        qT = sb("qT", [P, QTN + P - NS])
        qT3 = qT[:, 0:QTN].rearrange("p (f t) -> p f t", t=T)
        qT4 = qT[:, 0:QTN].rearrange("p (a f t) -> p a f t", a=2, t=T)
        q_off = [0, 16 * G_W[0]]
        qTg = [qT[:, q_off[g]:q_off[g] + 16 * G_W[g]].rearrange("p (f t) -> p f t", t=G_W[g]) for g in range(2)]
        sig = [qT[:, q_off[g]:q_off[g] + len(GROUP_TILES[g]) * D].rearrange("p (b n) -> p b n", n=D) for g in range(2)]
        keys = sb("keys", [P, 16, KEYS])
        arena = sb("arena", [P, RING * 2 * D])
        uv = arena[:].rearrange("p (r n) -> p r n", r=RING)
        panel = sb("panel", [P, SLOTS, C * PW])
        pTs = sb("pTs", [P, 2, G_W[1]])
        c_st = sb("c_st", [P, 2, G_W[1]])
        z = sb("z", [P, G_W[1]])
        carry = sb("carry", [P, C, 2])
        tail = sb("tail", [P, C, 2 + NS])
        xcur = sb("xcur", [P, D])
        x_sample = sb("x_sample", [P, D])
        ya = sb("ya", [P, D])
        yb = sb("yb", [P, D])
        lng = sb("lng", [P, D])
        lnb = sb("lnb", [P, D])
        idx = sb("idx", [P, BLOCKS, HEADS, TOPK], I32)
        gate = sb("gate", [P, BLOCKS, HEADS, TOPK])
        diag = sb("diag", [P, DIAGS, P])
        qst = sb("qst", [P, 2 * P])
        cst = sb("cst", [P, N_CONST])
        ixst = sb("ixst", [P, 2, RING], I32)
        dots = sb("dots", [P, 2, RING])
        act_w = sb("act_w", [P, 3, 2, RING])
        small = sb("small", [P, 64])
        state = sb("state", [P, C, 2, NS])
        cw = sb("cw", [P, 3, C])

        def const(name):
            return cst[:, CC[name][0]:CC[name][1]]

        at = [0]

        def part(n):
            at[0] += n
            return arena[:, at[0] - n:at[0]]

        v_rows = part(BLOCKS * D).rearrange("p (b n) -> p b n", b=BLOCKS)
        oT = [part(C * G_W[0]).rearrange("p (c t) -> p c t", c=C), gxT]
        kv_pages = part(4 * D).rearrange("p (i j n) -> p i j n", i=2, j=2)
        logit = hT[:].rearrange("p c t -> p (c t)")[:, 0:4 * SEQ].rearrange("p (j c n) -> p j c n", j=2, c=2)
        pair_of_rows = part(4 * SEQ)
        wrow, wT = (pair_of_rows[:, i * 2 * SEQ:(i + 1) * 2 * SEQ].rearrange("p (j n) -> p j n", j=2) for i in range(2))
        rms = [pair_of_rows[:, 0:HEADS * G_W[0]].rearrange("p (h t) -> p h t", h=HEADS),
               kv_pages.rearrange("p i j n -> p (i j n)")[:, 0:HEADS * G_W[1]].rearrange("p (h t) -> p h t", h=HEADS)]
        head_bias = [buffer[:].rearrange("p a n -> p (a n)")[:, 0:SEQ] for buffer in (c_st, pTs)]
        s_weight = x_sample[:].rearrange("p (j b g) -> p j b g", j=2, b=NS)
        attn_c = part(N_ATTN)
        wl = part(4 * HD)
        s_pos = part(2 * P).rearrange("p (j n) -> p j n", j=2)
        s_new = part(P)

        def aconst(name):
            return attn_c[:, AC[name][0]:AC[name][1]]

        r_sc = yb[:, 0:256]
        r_wk = yb[:, 256:512]
        r_eq = yb[:, 512:1024]
        r_cand = ya[:, 0:256]
        r_v = ya[:, 256:288]
        r_si = ya[:, 288:320].bitcast(U32)
        r_sif = ya[:, 320:352]
        r_tv = ya[:, 352:368]
        r_ti = ya[:, 368:384].bitcast(U32)
        r_ij = ya[:, 384:416].bitcast(U32)
        r_ijf = ya[:, 416:448]
        r_e = ya[:, 448:480]
        r_nm = ya[:, 480:481]
        r_ex = ya[:, 496:512]
        r_sum = ya[:, 512:513]
        r_inv = ya[:, 513:514]
        x_ig = yb[:, 0:256]
        x_pr = yb[:, 256:512]
        x_sel = ya[:, 640:656]

        stats = small[:, 0:12].rearrange("p (a s) -> p a s", a=2)
        lam2 = small[:, 16:18]
        lam_e = small[:, 18:20]
        neglam = small[:, 20:21]
        coef = small[:, 21:22]
        gsub = small[:, 22:23]
        subg_sb = small[:, 23:24]
        mx = small[:, 24:28].rearrange("p (j c) -> p j c", j=2)
        nb = small[:, 28:32].rearrange("p (j c) -> p j c", j=2)
        lsum = small[:, 32:36].rearrange("p (j c) -> p j c", j=2)
        linv = small[:, 36:40].rearrange("p (j c) -> p j c", j=2)
        smx, snb, ssum, sinv = (small[:, 40 + i:41 + i] for i in range(4))
        ixs = small[:, 44:52].bitcast(I32)
        gs8 = small[:, 52:60]
        eps = small[:, 60:61]
        mv = sb("mv", [P, 2, 2])
        rstd = sb("rstd", [P, 2, 1])
        pg = sb("pg", [1, NS * N_PAGES], I32)

        bank = ctx.enter_context(nc.psum_tensor("bank", [P, BANKS, 512], F32))
        pj = [bank[:, 2 * i:2 * i + 2, :].rearrange("p a n -> p (a n)") for i in range(2)]
        acc = ctx.enter_context(nc.psum_tensor("acc", [P, 1024], F32))
        tp = [ctx.enter_context(nc.psum_tensor(f"tp{i}", [P, 512], F32)) for i in range(2)]

        s_const = sem("const_in")
        s_attn_c = sem("attn_const_in")
        s_h = sem("h_in")
        s_hT = sem("hT_in")
        s_keys = sem("keys_in")
        s_small = sem("small_in")
        s_pages = sem("page_ids_in")
        s_zero = sem("zeroed")
        s_panel = [sem(f"panel_in{i}") for i in range(SLOTS)]
        s_pT = sem("embedding_rows_in")
        s_ln = sem("ln_params_in")
        s_pair = [sem(f"page_pair_in{i}") for i in range(2)]
        full = sem("pair_full")
        free = [sem(f"pair_free{i}") for i in range(2)]
        bank_full = sem("bank_full")
        bank_free = [sem(f"bank_free{i}") for i in range(BANKS)]
        k_out = [sem(f"k_rows_stored{i}") for i in range(3)]
        v_out = sem("v_rows_stored")
        kpair_used = sem("k_pair_used")
        vpair_used = sem("v_pair_used")
        lam_sums = sem("lambda_sums")
        lam_exps = sem("lambda_exps")
        s_scores = sem("sample_scores")
        s_bias_done = sem("sample_logits")
        s_exp_done = sem("sample_exps")
        s_probs = sem("sample_probs")
        s_weighted = sem("sample_weights")
        a_logits = sem("logits_ready")
        a_exps = sem("exps_ready")
        a_w = sem("weights_ready")
        a_wT_ps = sem("weights_turned")
        a_wT = sem("turned_weights_ready")
        a_o = sem("attn_out_full")
        a_ofree = sem("attn_out_free")
        sq_ready = sem("squares_ready")
        o_normed = sem("attn_out_normed")
        var_ready = sem("variance_ready")
        std_ready = sem("deviation_ready")
        rms_ready = sem("rms_ready")
        ln_done = sem("ln_done")
        ple_done = sem("embedding")
        tail_ready = sem("conv_state_ready")
        conv_out = sem("conv_state_stored")
        conv_copy = sem("conv_state_copied")
        q_staged = sem("q_staged")
        sc_ready = sem("key_scores_ready")
        sc_read = sem("key_scores_read")
        top_ready = sem("top_ready")
        gexp_done = sem("gate_exps")
        idx_done = sem("expert_ids")
        g_done = sem("gates_ready")
        ix_ready = sem("ids_staged")
        gathered = [sem(f"gathered{r}") for r in range(RING)]
        dot_done = sem("dots_done")
        gelu_done = sem("gelu_done")
        diag_ready = sem("diag_ready")
        slot_done = sem("slots_done")
        x_ready = sem("x_staged")
        acc_free = sem("acc_free")
        ig_ready = sem("sample_ids_rows")
        ixs_ready = sem("sample_ids_spread")
        y_out = sem("y_stored")
        turn = {e: sem(f"turn_{e}") for e in ("act", "pool", "dve")}

        SEED_SLOTS = RING
        SEED_GELU = 4

        block = ctx.enter_context(nc.Block())

        def squares(hd):
            return logit[:, hd % 2].rearrange("p c n -> p (c n)")[:, 0:T]

        def all_read(eng, n):
            for p in range(2):
                eng.wait_ge(free[p], (n - p + 1) // 2 + 1)

        def banks_read(eng, n):
            for p in range(BANKS):
                eng.wait_ge(bank_free[p], (n - p + BANKS - 1) // BANKS + 1)

        plan = Plan()
        steps = plan.build()

        def local(b):
            return b * P - G_OFF[group_of(b)]

        @block.sync
        def _(sp):
            sp.dma_start(hT[:, :, 0:G_W[0]], h0T[:, :, 0:G_W[0]]).then_inc(s_hT, 16)

            def load_panel(i):
                if i >= SLOTS:
                    kind, count = plan.release[i - SLOTS]
                    sp.wait_ge(full if kind == "pair" else bank_full, count)
                sp.dma_start(panel[:, i % SLOTS, :], panels[PANEL_AT[plan.panels[i]]]).then_inc(s_panel[i % SLOTS], 16)

            def load_ln(k, norms):
                if k == 0:
                    for i in range(2):
                        sp.wait_ge(k_out[i], 32)
                else:
                    sp.wait_ge(ln_done, norms)
                sp.dma_start(lng[:], ln[k, 0:1, :].broadcast_to([P, D])).then_inc(s_ln, 16)
                sp.dma_start(lnb[:], ln[k, 1:2, :].broadcast_to([P, D])).then_inc(s_ln, 16)

            def load_embedding(layer, g, projs):
                if projs:
                    sp.wait_ge(ple_done, projs)
                sp.dma_start(pTs[:, :, 0:G_W[g]], ple_rows[layer, :, :, G_OFF[g]:G_OFF[g] + G_W[g]]).then_inc(s_pT, 16)

            load_panel(0)
            sp.dma_start(gxT, h0T[:, :, G_W[0]:T]).then_inc(s_hT, 16)
            load_panel(1)
            load_panel(2)
            sp.dma_start(cst[:], consts[:, 0:N_CONST]).then_inc(s_const, 16)
            sp.dma_start(attn_c, consts[:, N_CONST:N_CONST + N_ATTN]).then_inc(s_attn_c, 16)
            sp.dma_start(wl, wlam.broadcast_to([P, 4 * HD])).then_inc(s_small, 16)
            sp.dma_start(subg_sb, subg).then_inc(s_small, 16)
            sp.dma_start(cw[:], convw).then_inc(s_small, 16)
            sp.dma_start(state[:], stateT).then_inc(s_small, 16)
            sp.dma_start(h[:, 0:TB, :], h0[0:SEQ, :].rearrange("(b p) n -> p b n", p=P)).then_inc(s_h, 16)
            sp.wait_ge(s_zero, 1)
            sp.dma_start(h[0:NS, TB, :], h0[SEQ:T, :]).then_inc(s_h, 16)
            sp.dma_start(keys[:], keysT[0]).then_inc(s_keys, 16)
            for i in range(SLOTS, len(plan.panels) + 1):
                for k, norms, before in plan.ln_loads:
                    if before == i:
                        load_ln(k, norms)
                for layer, g, projs, before in plan.embeds:
                    if before == i:
                        load_embedding(layer, g, projs)
                if i < len(plan.panels):
                    load_panel(i)
            for b in TILE_ORDER[1]:
                sp.wait_ge(ple_done, plan.ple_of[b])
                dst = y_p[b * P:(b + 1) * P, :] if b < TB else y_s
                sp.dma_start(dst, h[0:rows(b), b, :]).then_inc(y_out, 16)
            sp.wait_ge(y_out, 16 * BLOCKS)
            sp.wait_ge(v_out, 16 * BLOCKS)
            sp.wait_ge(k_out[2], 16)
            sp.wait_ge(conv_out, 16 * 2 * C)
            sp.wait_ge(conv_copy, 16)

        @block.gpsimd
        def _(pool):
            pool.dma_start(pg[:], pages).then_inc(s_pages, 16)
            nc.gpsimd.memset(h[:, TB, :], 0.0).then_inc(s_zero, 1)
            nc.gpsimd.memset(qT[:, QTN:QTN + P - NS], 0.0).then_inc(s_zero, 1)
            pool.wait_ge(s_pages, 16)

            def load_pair(i):
                cache = cache_k if i < NS else cache_v
                if i >= 2:
                    pool.wait_ge(kpair_used, min(i - 1, NS))
                    if i - 2 >= NS:
                        pool.wait_ge(vpair_used, i - 1 - NS)
                for j in range(N_PAGES):
                    k = (i % NS) * N_PAGES + j
                    page = pool.value_load(pg[0:1, k:k + 1], min_val=0, max_val=POOL_PAGES - 1)
                    pool.dma_start(kv_pages[:, i % 2, j, :], cache[bass.ds(page, 1)].rearrange("a p n -> (a p) n")) \
                        .then_inc(s_pair[i % 2], 16)

            load_pair(0)
            load_pair(1)
            for b in range(BLOCKS):
                n = USE["k_rows", b]
                pool.wait_ge(free[n % 2], freed(n) + 1)
                dst = nk_p[b * P:(b + 1) * P, :] if b < TB else nk_s
                src = (lng, lnb)[b % 2] if b < TB else ya
                pool.dma_start(dst, src[0:rows(b), :]).then_inc(k_out[b % 2 if b < TB else 2], 16)
            for i in range(2, NS + 2):
                load_pair(i)
            for b in range(BLOCKS):
                n = USE["v", 3 * BLOCKS + b]
                pool.wait_ge(free[n % 2], freed(n) + 1)
                dst = nv_p[b * P:(b + 1) * P, :] if b < TB else nv_s
                pool.dma_start(dst, v_rows[0:rows(b), b, :]).then_inc(v_out, 16)
            for i in range(NS + 2, 2 * NS):
                load_pair(i)

            def gather_group(layer, G, first, ids, ids_ready, count):
                half = first % 2
                pool.wait_ge(ids_ready, count)
                pool.sem_inc(turn["pool"], 1)
                nc.gpsimd.tensor_copy(ixst[:, half, :], ids).then_inc(ix_ready, 1)
                for r in range(RING):
                    if r == 0:
                        pool.wait_ge(ix_ready, G + 1)
                    pool.wait_ge(slot_done, G * RING + r + 1)
                    pool.sem_inc(turn["pool"], 1)
                    nc.gpsimd.indirect_dma_start(
                        uv[:, r, :], None, uv_dram[layer],
                        bass.IndirectOffsetOnAxis(ixst[:, half, r:r + 1], 0)).then_inc(gathered[r], 16)

            ids5 = idx[:].rearrange("p b h (a r) -> p b h a r", a=2)

            def gather_tiles(layer, first, last):
                G0 = first_group(layer, first) - first * HEADS * 2
                routed = (place(layer, first) - first) * HEADS
                with pool.Fori(first, last) as b:
                    with pool.Fori(0, HEADS) as hd:
                        for half in range(2):
                            G = G0 + half
                            gather_group(layer, b * 16 + hd * 2 + G, G, ids5[:, b, hd, half, :],
                                         idx_done, b * HEADS + hd + (routed + 1))

            def gather_sample(layer):
                G = first_group(layer, TB)
                gather_group(layer, G, G, ixs, ixs_ready, layer + 1)

            pool.wait_ge(v_out, 16 * BLOCKS)
            gather_tiles(0, 0, TB)
            gather_sample(0)
            gather_tiles(1, 0, 2)
            pool.dma_start(cs[:, 0, :], state_conv[:, 1, :]).then_inc(conv_copy, 16)
            pool.wait_ge(tail_ready, 1)
            with nc.allow_non_contiguous_dma(reason="small state"):
                for j in range(C):
                    pool.dma_start(cp[:, j * P:(j + 1) * P].rearrange("s p -> p s"),
                                   tail[:, j, 0:2]).then_inc(conv_out, 16)
                    pool.dma_start(cs[:, 1, j * P:(j + 1) * P].rearrange("s p -> p s"),
                                   tail[:, j, 2:2 + NS]).then_inc(conv_out, 16)
            gather_tiles(1, 2, 3)
            gather_sample(1)
            gather_tiles(1, 3, TB)

        @block.scalar
        def _(act):
            act.sem_inc(slot_done, SEED_SLOTS)
            act.sem_inc(free[0], 1)
            act.sem_inc(free[1], 1)
            for i in range(BANKS):
                act.sem_inc(bank_free[i], 1)
            act.sem_inc(acc_free, 1)
            act.sem_inc(a_ofree, 2)

            with act.Fori(0, 2) as it:
                for f in range(8):
                    n = USE["qk", f]
                    act.wait_ge(full, it * 8 + (n + 1))
                    act.sem_inc(turn["act"], 1)
                    nc.scalar.activation(qT4[:, it, f, :], pj[n % 2][:, PW:PW + T], ACT.Copy).then_inc(free[n % 2], 1)
            act.wait_ge(lam_sums, 1)
            nc.scalar.activation(lam_e, lam2, ACT.Exp).then_inc(lam_exps, 1)
            for p in range(4):
                for b in range(BLOCKS):
                    n, m = USE["v", p * BLOCKS + b], rows(b)
                    act.wait_ge(full, n + 1)
                    nc.scalar.activation(v_rows[0:m, b, p * PW:(p + 1) * PW], pj[n % 2][0:m, 0:PW],
                                         ACT.Copy).then_inc(free[n % 2], 1)
            units = [(hd, i) for hd in range(HEADS) for i in range(TB)]
            for u in range(len(units) + 3):
                if u == S_TURN + 1:
                    act.wait_ge(s_bias_done, 1)
                    nc.scalar.activation(yb[:, 0:PAST + NS], yb[:, 0:PAST + NS], ACT.Exp, bias=snb, scale=SCALE,
                                         accum_out=ssum).then_inc(s_exp_done, 1)
                if u in S_OUT:
                    n = USE["s_out", S_OUT[u]]
                    own = slice(S_OUT[u] * NS * HEADS // 2, (S_OUT[u] + 1) * NS * HEADS // 2)
                    act.wait_ge(full, n + 1)
                    nc.scalar.activation(xcur[own, :], pj[n % 2][own, :], ACT.Copy) \
                        .then_inc(free[n % 2], 1)
                if u == O_TURN:
                    n = USE["o_turn", 0]
                    act.wait_ge(full, n + 1)
                    own = pj[n % 2][:, 0:HEADS * (NS * HEADS + 1)].rearrange("p (h x) -> p h x", h=HEADS)
                    own = own[:, :, 0:NS * HEADS:HEADS]
                    nc.scalar.activation(oT[1][:, :, 2 * P:G_W[1]], own, ACT.Copy).then_inc(free[n % 2], 1)
                if u < len(units):
                    n = (units[u][1] + 1) * P
                    act.wait_ge(a_logits, u + 1)
                    for c in range(2):
                        e = nc.scalar.activation(logit[:, u % 2, c, 0:n], logit[:, u % 2, c, 0:n], ACT.Exp,
                                                 bias=nb[:, u % 2, c:c + 1], scale=SCALE,
                                                 accum_out=lsum[:, u % 2, c:c + 1])
                    e.then_inc(a_exps, 1)
                if 2 <= u <= len(units) + 1:
                    v, n = u - 2, (units[u - 2][1] + 1) * P
                    act.wait_ge(a_wT_ps, v + 1)
                    if v >= 2:
                        act.wait_ge(a_o, v - 1)
                    nc.scalar.activation(wT[:, v % 2, 0:n], tp[v % 2][:, 0:n], ACT.Copy).then_inc(a_wT, 1)
                if u >= 3:
                    v = u - 3
                    hd, i = units[v]
                    act.wait_ge(a_o, v + 1)
                    nc.scalar.activation(oT[group_of(i)][:, hd, local(i):local(i) + P], acc[:, (v % 2) * 512:(v % 2) * 512 + P],
                                         ACT.Copy).then_inc(a_ofree, 1)
            act.drain()
            for hd in range(HEADS + 1):
                if hd < HEADS:
                    if hd >= 2:
                        act.wait_ge(full, USE["subln", hd - 2] + 1)
                    for g in range(2):
                        a = nc.scalar.activation(squares(hd)[:, G_OFF[g]:G_OFF[g] + G_W[g]], oT[g][:, hd, :], ACT.Square)
                    a.then_inc(sq_ready, 1)
                if hd >= 1:
                    n = USE["subln", hd - 1]
                    act.wait_ge(full, n + 1)
                    for g in range(2):
                        nc.scalar.activation(rms[g][:, hd - 1, :],
                                             pj[n % 2][:, PW + G_OFF[g]:PW + G_OFF[g] + G_W[g]], ACT.Sqrt, bias=eps)
                    act.drain()
                    act.sem_inc(rms_ready, 1)
                    act.sem_inc(free[n % 2], 1)

            def stage_q(b, hd, unit):
                act.wait_ge(sc_ready, unit + 1)
                g = group_of(b)
                for c in range(2):
                    at = q_off[g] + (2 * hd + c) * G_W[g] + local(b)
                    a = nc.scalar.activation(qst[:, c * P:(c + 1) * P], qT[:, at:at + P], ACT.Copy)
                a.then_inc(q_staged, 1)

            def background(x):
                product_of = bank[:, x.n % BANKS, :] if x.n is not None else None
                if x.kind == "norm_a":
                    m, i = rows(x.b), x.e % 2
                    act.wait_ge(var_ready, x.e + 1)
                    nc.scalar.activation(rstd[0:m, i], mv[0:m, i, 1:2], ACT.Sqrt, bias=eps[0:m]).then_inc(std_ready, 1)
                elif x.kind == "turn":
                    m = rows(x.b)
                    act.wait_ge(bank_full, x.n + 1)
                    nc.scalar.activation(hT[:, 4 * x.half:4 * x.half + 4, local(x.b):local(x.b) + m],
                                         product_of.rearrange("p (c t) -> p c t", c=4)[:, :, 0:m],
                                         ACT.Copy).then_inc(bank_free[x.n % BANKS], 1)
                elif x.kind == "pq":
                    if x.fence:
                        act.drain()
                    act.wait_ge(bank_full, x.n + 1)
                    nc.scalar.activation(qTg[x.g][:, x.f, :], product_of[:, 0:G_W[x.g]],
                                         ACT.Copy).then_inc(bank_free[x.n % BANKS], 1)
                elif x.kind == "gate":
                    if x.fence:
                        act.drain()
                    m = rows(x.b)
                    act.wait_ge(bank_full, x.n + 1)
                    nc.scalar.activation(sig[x.g][0:m, local(x.b) // P, x.p * PW:(x.p + 1) * PW], product_of[0:m, 0:PW],
                                         ACT.Sigmoid).then_inc(bank_free[x.n % BANKS], 1)
                elif x.kind == "conv" and x.k == 0:
                    act.wait_ge(bank_full, x.n + 1)
                    nc.scalar.activation(c_st[:, x.j % 2, 0:G_W[x.g]], product_of[:, 0:G_W[x.g]],
                                         ACT.Copy).then_inc(bank_free[x.n % BANKS], 1)
                elif x.kind == "stage":
                    act.drain()
                    if x.layer == 1 and x.b == 0:
                        act.wait_ge(sc_ready, x.u + 1)
                        act.dma_start(keys[:], keysT[1]).then_inc(s_keys, 16)
                    if x.layer == 0 and x.b == TB:
                        act.wait_ge(s_zero, 2)
                    stage_q(x.b, 0, x.u)
                elif x.kind == "route" and x.i == 1 and x.hd < HEADS - 1:
                    act.drain()
                    stage_q(x.b, x.hd + 1, x.u + 1)
                elif x.kind == "route" and x.i == 3:
                    act.wait_ge(top_ready, x.u + 1)
                    nc.scalar.activation(r_ex, r_tv, ACT.Exp, bias=r_nm, accum_out=r_sum).then_inc(gexp_done, 1)

            def four_experts(G, q, mask):
                half, s = G % 2, slice(4 * q, 4 * q + 4)
                act.wait_ge(dot_done, G * RING + 4 * q + 4)
                nc.scalar.activation(act_w[:, 1, half, s], dots[:, half, s], ACT.Gelu).then_inc(gelu_done, 1)
                act.drain()
                for r in range(4 * q, 4 * q + 4):
                    nc.scalar.activation(act_w[:, 2, half, r:r + 1], act_w[:, 1, half, r:r + 1], ACT.Copy,
                                         scale=act_w[:, 0, half, r:r + 1])
                act.drain()
                for r in range(4 * q, 4 * q + 4):
                    act.wait_ge(slot_done, G * RING + r + 1 + SEED_SLOTS - DIAGS)
                    nc.scalar.activation(diag[:, r % DIAGS, :], mask, ACT.Copy,
                                         scale=act_w[:, 2, half, r:r + 1]).then_inc(diag_ready, 1)

            gates5 = gate[:].rearrange("p b h (a r) -> p b h a r", a=2)
            for kind, layer, b, lots in steps:
                if kind == "alone":
                    for x in lots[0]:
                        background(x)
                    continue
                later = []
                for t, G, q, hd, lot in window_quarters(layer, b, lots):
                    for x in later:
                        background(x)
                    later = lot
                    if q == 0 and b < TB:
                        act.wait_ge(g_done, place(layer, b) * HEADS + hd + 1)
                        nc.scalar.activation(act_w[:, 0, G % 2, :], gates5[:, b, hd, t // 2 % 2, :], ACT.Copy)
                    elif q == 0:
                        act.wait_ge(ixs_ready, layer + 1)
                        nc.scalar.activation(act_w[:, 0, G % 2, :], gs8, ACT.Copy)
                    four_experts(G, q, const("ident" if b < TB else "group_of"))
                for x in later:
                    background(x)
                act.wait_ge(slot_done, (G + 1) * RING + SEED_SLOTS)
                nc.scalar.activation(h[0:rows(b), b, :], acc[0:rows(b), :], ACT.Copy).then_inc(acc_free, 1)

        @block.vector
        def _(dve):
            V = nc.vector
            V.memset(eps, EPS)
            dve.sem_inc(gelu_done, SEED_GELU)
            dve.sem_inc(sc_read, 1)
            dve.sem_inc(sc_ready, 1)

            dve.wait_ge(s_small, 64)
            dve.wait_ge(s_attn_c, 16)
            w4 = wl.rearrange("p (a b d) -> p a b d", a=2, b=2)
            V.tensor_tensor(w4[:, :, 0, :], w4[:, :, 0, :], w4[:, :, 1, :], ALU.mult)
            dve.drain()
            V.tensor_reduce(lam2, w4[:, :, 0, :], AX_X, ALU.add).then_inc(lam_sums, 1)
            V.tensor_scalar(gsub, subg_sb, 1.0 - LAM_INIT, None, ALU.mult)
            for b in range(BLOCKS):
                n, m = USE["k_rows", b], rows(b)
                dve.wait_ge(full, n + 1)
                if b in (2, 3):
                    dve.wait_ge(k_out[b % 2], 16)
                V.tensor_copy(((lng, lnb)[b % 2] if b < TB else ya)[0:m, :], pj[n % 2][0:m, :]).then_inc(free[n % 2], 1)
            n = USE["q_rows", 0]
            dve.wait_ge(full, n + 1)
            V.tensor_copy(xcur[0:NS, :], pj[n % 2][0:NS, :]).then_inc(free[n % 2], 1)
            dve.wait_ge(lam_exps, 1)
            V.tensor_tensor(neglam, lam_e[:, 1:2], lam_e[:, 0:1], ALU.subtract)
            dve.drain()
            V.tensor_scalar(neglam, neglam, LAM_INIT, None, ALU.subtract)
            dve.drain()
            V.tensor_scalar(coef, neglam, 1.0, None, ALU.subtract)
            dve.drain()
            V.tensor_scalar(coef, coef, aconst("second"), 1.0, ALU.mult, ALU.add)
            for b in range(NS):
                n = USE["q_spread", b]
                dve.wait_ge(full, n + 1)
                for j in range(N_PAGES):
                    dve.wait_ge(s_pair[b % 2], 32 * (b // 2 + 1))
                    dve.drain()
                    t = V.tensor_tensor(yb[:], kv_pages[:, b % 2, j, :], pj[n % 2], ALU.mult)
                    if j == N_PAGES - 1:
                        t.then_inc(free[n % 2], 1)
                    dve.drain()
                    t = V.tensor_reduce(s_pos[:, j, b * 16:(b + 1) * 16], yb[:].rearrange("p (g d) -> p g d", d=HD), AX_X,
                                        ALU.add)
                    if j == N_PAGES - 1:
                        t.then_inc(kpair_used, 1)
            dve.drain()
            V.tensor_tensor(yb[0:NS, :], xcur[0:NS, :], ya[0:NS, :], ALU.mult)
            dve.drain()
            V.tensor_reduce(yb[0:NS, 0:16], yb[0:NS, :].rearrange("p (g d) -> p g d", d=HD), AX_X, ALU.add)
            dve.drain()
            V.tensor_tensor(s_new[0:NS, :].rearrange("p (b g) -> p b g", b=NS),
                            yb[0:NS, 0:16].rearrange("p (b g) -> p b g", b=1).broadcast_to([NS, NS, 16]),
                            aconst("own")[0:NS, :].rearrange("p (b g) -> p b g", g=1).broadcast_to([NS, NS, 16]),
                            ALU.add).then_inc(s_scores, 1)
            lg = yb[:, 0:PAST + NS]

            def sample_logits():
                n = USE["s_turn", 0]
                dve.wait_ge(full, n + 1)
                dve.drain()
                V.tensor_tensor(lg, pj[n % 2][:, 0:PAST + NS], aconst("bias_s"), ALU.add).then_inc(free[n % 2], 1)
                dve.drain()
                V.tensor_reduce(smx, lg, AX_X, ALU.max)
                dve.drain()
                V.tensor_scalar(snb, smx, -SCALE, None, ALU.mult).then_inc(s_bias_done, 1)

            def sample_probs():
                dve.wait_ge(s_exp_done, 1)
                V.reciprocal(sinv, ssum)
                dve.drain()
                V.tensor_scalar(lg, lg, sinv, coef, ALU.mult, ALU.mult).then_inc(s_probs, 1)

            def sample_weights():
                n = USE["p_turn", 0]
                dve.wait_ge(full, n + 1)
                V.memset(x_sample[:], 0.0)
                V.tensor_reduce(diag[:, 0, :], pj[n % 2][:, 0:PAST].rearrange("p (g c) -> p g c", c=2), AX_X, ALU.add)
                V.tensor_reduce(diag[0:NS, 1, 0:NS * HEADS],
                                pj[n % 2][0:NS, PAST:PAST + P].rearrange("p (g c) -> p g c", c=2), AX_X,
                                ALU.add).then_inc(free[n % 2], 1)
                dve.drain()
                turned = diag[:, 0, :].rearrange("p (j b h) -> p j b h", j=2, b=NS)
                for b in range(NS):
                    w = V.tensor_copy(s_weight[:, :, b, b * HEADS:(b + 1) * HEADS], turned[:, :, b, :])
                w.then_inc(s_weighted, 1)

            units = [(hd, i) for hd in range(HEADS) for i in range(TB)]
            for u in range(len(units) + 1):
                if u == S_TURN:
                    sample_logits()
                if u == P_TURN - 1:
                    sample_probs()
                if u == P_TURN:
                    sample_weights()
                if u < len(units):
                    hd, i = units[u]
                    k = (i + 1) * P
                    n = USE["attn", u]
                    if i == 0:
                        V.tensor_scalar(head_bias[hd % 2], aconst("dist"), SLOPES[hd] / SCALE, None, ALU.mult)
                        dve.drain()
                    dve.wait_ge(full, n + 1)
                    bias = head_bias[hd % 2]
                    for c in range(2):
                        m = V.tensor_tensor_reduce(logit[:, u % 2, c, 0:k], pj[n % 2][:, c * SEQ:c * SEQ + k],
                                                   bias[:, SEQ - k:SEQ], 1.0, LOWEST, ALU.add, ALU.max,
                                                   mx[:, u % 2, c:c + 1])
                    m.then_inc(free[n % 2], 1)
                    dve.drain()
                    V.tensor_scalar(nb[:, u % 2, :], mx[:, u % 2, :], -SCALE, None, ALU.mult).then_inc(a_logits, 1)
                if u >= 1:
                    v = u - 1
                    k = (units[v][1] + 1) * P
                    dve.wait_ge(a_exps, v + 1)
                    V.reciprocal(linv[:, v % 2, :], lsum[:, v % 2, :])
                    dve.drain()
                    V.tensor_scalar(linv[:, v % 2, 1:2], linv[:, v % 2, 1:2], neglam, None, ALU.mult)
                    if v >= 2:
                        dve.wait_ge(a_wT_ps, v - 1)
                    V.tensor_scalar(wrow[:, v % 2, 0:k], logit[:, v % 2, 0, 0:k], linv[:, v % 2, 0:1], None, ALU.mult)
                    dve.drain()
                    V.scalar_tensor_tensor(out=wrow[:, v % 2, 0:k], in0=logit[:, v % 2, 1, 0:k],
                                           scalar=linv[:, v % 2, 1:2], in1=wrow[:, v % 2, 0:k],
                                           op0=ALU.mult, op1=ALU.add).then_inc(a_w, 1)
                    dve.drain()
            def norm_values(g, hd):
                rr = rms[g][:, hd, :]
                dve.wait_ge(rms_ready, hd + 1)
                V.reciprocal(rr, rr)
                dve.drain()
                V.scalar_tensor_tensor(out=oT[g][:, hd, :], in0=oT[g][:, hd, :], scalar=gsub, in1=rr,
                                       op0=ALU.mult, op1=ALU.mult).then_inc(o_normed, 1)

            for hd in range(HEADS):
                norm_values(0, hd)

            def norm_a(x):
                m, i = rows(x.b), x.e % 2
                row = h[0:m, x.b, :]
                if x.tiles is not None:
                    dve.wait_ge(acc_free, x.tiles)
                for a in range(2):
                    V.bn_stats(stats[0:m, a, :], row[:, a * 512:(a + 1) * 512])
                dve.drain()
                V.bn_aggr(mv[0:m, i, :], stats[0:m].rearrange("p a s -> p (a s)"))
                dve.drain()
                dve.sem_inc(var_ready, 1)
                dve.wait_ge(s_ln, 32 * x.load)
                V.scalar_tensor_tensor(out=row, in0=row, scalar=mv[0:m, i, 0:1], in1=lng[0:m, :],
                                       op0=ALU.subtract, op1=ALU.mult)

            def norm_b(x):
                m, i = rows(x.b), x.e % 2
                row = h[0:m, x.b, :]
                dve.wait_ge(std_ready, x.e + 1)
                V.reciprocal(rstd[0:m, i], rstd[0:m, i])
                dve.drain()
                V.scalar_tensor_tensor(out=row, in0=row, scalar=rstd[0:m, i], in1=lnb[0:m, :],
                                       op0=ALU.mult, op1=ALU.add).then_inc(ln_done, 1)

            def convolve(x):
                g, j, n, w = x.g, x.j, x.n, G_W[x.g]
                last = 2 * P + 2
                dve.wait_ge(bank_free[(n - 1) % BANKS], bank_freed(n - 1) + 1)
                dve.wait_ge(bank_full, n + 1)
                if j == 0 and g == 0:
                    V.memset(gx[:, :, 0:2], 0.0)
                elif j == 0:
                    V.tensor_copy(gx[:, :, 0:2], carry[:])
                V.tensor_tensor(gx[:, j, 2:2 + w], c_st[:, j % 2, 0:w], bank[:, n % BANKS, 0:w],
                                ALU.mult).then_inc(bank_free[n % BANKS], 1)
                dve.drain()
                V.tensor_scalar(z[:, 0:2 * P], gx[:, j, 0:2 * P], cw[:, 0, j:j + 1], None, ALU.mult)
                if g == 0:
                    V.tensor_copy(carry[:, j, :], gx[:, j, last - 2:last])
                else:
                    V.tensor_scalar(z[:, 2 * P:w], state[:, j, 0, :], cw[:, 0, j:j + 1], None, ALU.mult)
                    V.tensor_copy(tail[:, j, :], gx[:, j, last - 2:last + NS])
                dve.drain()
                V.scalar_tensor_tensor(out=z[:, 0:2 * P], in0=gx[:, j, 1:1 + 2 * P], scalar=cw[:, 1, j:j + 1],
                                       in1=z[:, 0:2 * P], op0=ALU.mult, op1=ALU.add)
                if g == 1:
                    V.scalar_tensor_tensor(out=z[:, 2 * P:w], in0=state[:, j, 1, :], scalar=cw[:, 1, j:j + 1],
                                           in1=z[:, 2 * P:w], op0=ALU.mult, op1=ALU.add)
                dve.drain()
                V.scalar_tensor_tensor(out=z[:, 0:w], in0=gx[:, j, 2:2 + w], scalar=cw[:, 2, j:j + 1],
                                       in1=z[:, 0:w], op0=ALU.mult, op1=ALU.add)
                if g == 1 and j == C - 1:
                    dve.sem_inc(tail_ready, 1)

            def route_keys(unit):
                dve.wait_ge(sc_ready, unit + 2)
                V.tensor_copy(r_sc, tp[0][:, 0:256]).then_inc(sc_read, 1)
                dve.drain()
                for c in range(2):
                    V.max(r_v[:, c * 16:c * 16 + 8], r_sc[:, c * P:(c + 1) * P])
                dve.drain()
                for c in range(2):
                    V.max_index(r_si[:, c * 16:c * 16 + 8], r_v[:, c * 16:c * 16 + 8], r_sc[:, c * P:(c + 1) * P])
                    V.match_replace(r_wk[:, c * P:(c + 1) * P], r_v[:, c * 16:c * 16 + 8], r_sc[:, c * P:(c + 1) * P],
                                    LOWEST)

            def route_pairs():
                dve.drain()
                for c in range(2):
                    V.max(r_v[:, c * 16 + 8:c * 16 + 16], r_wk[:, c * P:(c + 1) * P])
                dve.drain()
                for c in range(2):
                    V.max_index(r_si[:, c * 16 + 8:c * 16 + 16], r_v[:, c * 16 + 8:c * 16 + 16],
                                r_wk[:, c * P:(c + 1) * P])
                V.tensor_tensor(r_cand.rearrange("p (i j) -> p i j", j=16),
                                r_v[:, 0:16].rearrange("p (i j) -> p i j", j=1).broadcast_to([P, 16, 16]),
                                r_v[:, 16:32].rearrange("p (i j) -> p i j", i=1).broadcast_to([P, 16, 16]), ALU.add)
                dve.drain()
                V.tensor_copy(r_sif, r_si)
                V.max(r_tv[:, 0:8], r_cand)

            def route_top():
                dve.drain()
                V.max_index(r_ti[:, 0:8], r_tv[:, 0:8], r_cand)
                V.match_replace(r_wk, r_tv[:, 0:8], r_cand, LOWEST)
                dve.drain()
                V.max(r_tv[:, 8:16], r_wk)
                V.tensor_scalar(r_nm, r_tv[:, 0:1], -1.0, None, ALU.mult).then_inc(top_ready, 1)
                dve.drain()
                V.max_index(r_ti[:, 8:16], r_tv[:, 8:16], r_wk)
                dve.drain()
                V.tensor_scalar(r_ij[:, 0:16], r_ti, 4, None, ALU.logical_shift_right)
                V.tensor_scalar(r_ij[:, 16:32], r_ti, 15, None, ALU.bitwise_and)
                dve.drain()
                V.tensor_copy(r_ijf, r_ij)

            def route_ids(b, hd):
                dve.drain()
                V.tensor_tensor(r_eq.rearrange("p (k i) -> p k i", i=16),
                                r_ijf.rearrange("p (k i) -> p k i", i=1).broadcast_to([P, 32, 16]),
                                const("iota").rearrange("p (k i) -> p k i", k=1).broadcast_to([P, 32, 16]),
                                ALU.is_equal)
                dve.drain()
                eq4 = r_eq.rearrange("p (c k i) -> p c k i", c=2, i=16)
                V.tensor_tensor(eq4, eq4, r_sif.rearrange("p (c k i) -> p c k i", c=2, k=1).broadcast_to([P, 2, 16, 16]),
                                ALU.mult)
                dve.drain()
                V.tensor_reduce(r_e, r_eq.rearrange("p (k i) -> p k i", i=16), AX_X, ALU.add)
                dve.drain()
                V.scalar_tensor_tensor(out=idx[:, b, hd, :], in0=r_e[:, 0:16], scalar=float(KEYS), in1=r_e[:, 16:32],
                                       op0=ALU.mult, op1=ALU.add).then_inc(idx_done, 1)

            def gates(b, hd, unit):
                dve.wait_ge(gexp_done, unit + 1)
                V.reciprocal(r_inv, r_sum)
                dve.drain()
                V.tensor_scalar(gate[:, b, hd, :], r_ex, r_inv, None, ALU.mult).then_inc(g_done, 1)

            def background(x):
                n = x.n
                if x.kind in ("mix", "norm_a", "norm_b", "proj", "route", "side", "i_spread") or x.kind == "conv" and x.k > 0:
                    dve.drain()
                if x.kind == "mix":
                    m = rows(x.b)
                    part_of_h = h[0:m, x.b, x.p * PW:(x.p + 1) * PW]
                    if n == 0:
                        dve.wait_ge(s_h, 32)
                    dve.wait_ge(bank_full, n + 1)
                    V.scalar_tensor_tensor(out=part_of_h, in0=part_of_h, scalar=ALPHA, in1=bank[0:m, n % BANKS, 0:PW],
                                           op0=ALU.mult, op1=ALU.add).then_inc(bank_free[n % BANKS], 1)
                    if n < HEADS:
                        norm_values(1, n)
                elif x.kind == "norm_a":
                    norm_a(x)
                elif x.kind == "norm_b":
                    norm_b(x)
                elif x.kind == "proj":
                    m, cols = rows(x.b), slice(x.p * PW, (x.p + 1) * PW)
                    y = sig[x.g][0:m, local(x.b) // P, cols]
                    if x.first:
                        banks_read(dve, n)
                    dve.wait_ge(bank_full, n + 1)
                    V.tensor_tensor(y, y, bank[0:m, n % BANKS, 0:PW], ALU.mult).then_inc(bank_free[n % BANKS], 1)
                    dve.drain()
                    V.tensor_tensor(h[0:m, x.b, cols], h[0:m, x.b, cols], y, ALU.add).then_inc(ple_done, 1)
                elif x.kind == "conv" and x.k == 1:
                    convolve(x)
                elif x.kind == "conv" and x.k == 2:
                    w = G_W[x.g]
                    dve.wait_ge(bank_full, n + 1)
                    V.tensor_tensor(gx[:, x.j, 2:2 + w], z[:, 0:w], bank[:, n % BANKS, 0:w],
                                    ALU.mult).then_inc(bank_free[n % BANKS], 1)
                elif x.kind == "side":
                    V.tensor_copy(x_ig[0:NS, 0:P], idx[0:NS, TB, :, :].rearrange("p h k -> p (h k)"))
                    V.tensor_copy(x_ig[0:NS, P:2 * P], gate[0:NS, TB, :, :].rearrange("p h k -> p (h k)")) \
                        .then_inc(ig_ready, 1)
                elif x.kind == "x_spread":
                    dve.wait_ge(bank_full, n + 1)
                    V.tensor_copy(x_sample[:, x.half * 512:(x.half + 1) * 512], bank[:, n % BANKS, :]) \
                        .then_inc(bank_free[n % BANKS], 1)
                elif x.kind == "i_spread":
                    dve.wait_ge(bank_full, n + 1)
                    V.tensor_tensor(x_pr.rearrange("p (g k) -> p g k", k=TOPK),
                                    bank[:, n % BANKS, 0:256].rearrange("p (g k) -> p g k", k=TOPK),
                                    const("kmask").rearrange("p (g k) -> p g k", g=1).broadcast_to([P, 16, TOPK]),
                                    ALU.mult).then_inc(bank_free[n % BANKS], 1)
                    dve.drain()
                    V.tensor_reduce(x_sel, x_pr.rearrange("p (g k) -> p g k", k=TOPK), AX_X, ALU.add)
                    dve.drain()
                    V.tensor_copy(ixs, x_sel[:, 0:HEADS])
                    V.tensor_copy(gs8, x_sel[:, HEADS:2 * HEADS]).then_inc(ixs_ready, 1)
                elif x.kind == "route":
                    if x.i == 0:
                        route_keys(x.u)
                    elif x.i == 1:
                        route_pairs()
                    elif x.i == 2:
                        route_top()
                    else:
                        route_ids(x.b, x.hd)
                        gates(x.b, x.hd, x.u)

            def four_dots(G, q, x_rows):
                for r in range(4 * q, 4 * q + 4):
                    dve.wait_ge(gathered[r], G * 16 + 16)
                    if r == 0:
                        dve.wait_ge(gelu_done, G * 2 + 2)
                    V.tensor_tensor_reduce(uv[:, r, 0:D], uv[:, r, 0:D], x_rows[:], 1.0, 0.0, ALU.mult, ALU.add,
                                           dots[:, G % 2, r:r + 1]).then_inc(dot_done, 1)

            later = []
            for kind, layer, b, lots in steps:
                if kind == "alone":
                    for x in later + lots[0]:
                        background(x)
                    later = []
                    continue
                for t, G, q, hd, lot in window_quarters(layer, b, lots):
                    for x in later:
                        background(x)
                    later = lot
                    if t == 0 and b < TB:
                        dve.drain()
                        V.tensor_copy(xcur[:], h[:, b, :]).then_inc(x_ready, 1)
                        dve.drain()
                    four_dots(G, q, xcur if b < TB else x_sample)

        @block.tensor
        def _(pe):
            mm = nc.tensor.matmul

            pe.wait_ge(s_hT, 16)
            src = [hT, gxT]
            for f in range(2 * HEADS):
                n, slot = USE["qk", f], f // 2 % SLOTS
                if f % 2 == 0:
                    pe.wait_ge(s_panel[slot], 16 * (f // 2 // SLOTS + 1))
                pe.wait_ge(free[n % 2], freed(n))
                w = panel[:, slot, :].rearrange("p (c n) -> p c n", c=C)[:, :, (f % 2) * P:(f % 2 + 1) * P]
                for g in range(2):
                    if f == 0 and g == 1:
                        pe.wait_ge(s_hT, 32)
                    for c in range(C):
                        m = mm(pj[n % 2][:, PW + G_OFF[g]:PW + G_OFF[g] + G_W[g]], w[:, c, :], src[g][:, c, 0:G_W[g]],
                               start=(c == 0), stop=(c == C - 1))
                m.then_inc(full, 1)
            pe.wait_ge(s_const, 16)
            all_read(pe, USE["k_rows", 0])
            for b in range(BLOCKS):
                n, m = USE["k_rows", b], rows(b)
                pe.wait_ge(free[n % 2], freed(n))
                for hd in range(HEADS):
                    t = nc.tensor.transpose(pj[n % 2][0:m, hd * P:(hd + 1) * P], qT3[:, HEADS + hd, b * P:b * P + m],
                                            const("ident"))
                t.then_inc(full, 1)
            n = USE["q_rows", 0]
            pe.wait_ge(free[n % 2], freed(n))
            for hd in range(HEADS):
                t = nc.tensor.transpose(pj[n % 2][0:NS, hd * P:(hd + 1) * P], qT3[:, hd, SEQ:T], const("ident"))
            t.then_inc(full, 1)

            def values(i):
                n, p, b = USE["v", i], i // BLOCKS, i % BLOCKS
                m, slot = rows(b), (8 + p) % SLOTS
                pe.wait_ge(s_panel[slot], 16 * ((8 + p) // SLOTS + 1))
                pe.wait_ge(free[n % 2], freed(n))
                w = panel[:, slot, :].rearrange("p (c n) -> p c n", c=C)
                for c in range(C):
                    last = mm(pj[n % 2][0:m, 0:PW], src[group_of(b)][:, c, local(b):local(b) + m], w[:, c, :],
                              start=(c == 0), stop=(c == C - 1))
                last.then_inc(full, 1)

            for i in range(4):
                values(i)
            pe.wait_ge(s_attn_c, 16)
            pe.wait_ge(free[n % 2], freed(n) + 1)
            for b in range(NS):
                n = USE["q_spread", b]
                pe.wait_ge(free[n % 2], freed(n))
                for half in range(2):
                    m = mm(pj[n % 2][:, half * 512:(half + 1) * 512], aconst("pick")[0:NS, b * P:(b + 1) * P],
                           xcur[0:NS, half * 512:(half + 1) * 512], start=True, stop=True)
                m.then_inc(full, 1)
                values(4 + 2 * b)
                values(5 + 2 * b)

            def turn_scores():
                n = USE["s_turn", 0]
                pe.wait_ge(s_scores, 1)
                pe.wait_ge(free[n % 2], freed(n))
                for j in range(2):
                    nc.tensor.transpose(pj[n % 2][:, j * P:(j + 1) * P], s_pos[:, j, :], const("ident"))
                nc.tensor.transpose(pj[n % 2][:, PAST:PAST + NS], s_new[0:NS, :],
                                    const("ident")[0:NS, 0:NS]).then_inc(full, 1)

            def turn_probs():
                n = USE["p_turn", 0]
                pe.wait_ge(s_probs, 1)
                pe.wait_ge(free[n % 2], freed(n))
                for j in range(2):
                    nc.tensor.transpose(pj[n % 2][:, j * P:(j + 1) * P], yb[:, j * P:(j + 1) * P], const("ident"))
                nc.tensor.transpose(pj[n % 2][0:NS, PAST:PAST + P], yb[:, PAST:PAST + NS], const("ident")).then_inc(full, 1)

            def sample_out(part):
                n = USE["s_out", part]
                pe.wait_ge(s_weighted, 1)
                pe.wait_ge(free[n % 2], freed(n))
                for b in range(part * NS // 2, (part + 1) * NS // 2):
                    pair = NS + b
                    pe.wait_ge(s_pair[pair % 2], 32 * (pair // 2 + 1))
                    for j in range(N_PAGES):
                        for half in range(2):
                            m = mm(pj[n % 2][0:NS * HEADS, half * 512:(half + 1) * 512], s_weight[:, j, b, :],
                                   kv_pages[:, pair % 2, j, half * 512:(half + 1) * 512],
                                   start=(b == part * NS // 2 and j == 0), stop=False)
                    m.then_inc(vpair_used, 1)
                for half in range(2):
                    m = mm(pj[n % 2][0:NS * HEADS, half * 512:(half + 1) * 512], diag[0:NS, 1, 0:NS * HEADS],
                           v_rows[0:NS, TB, half * 512:(half + 1) * 512], start=False, stop=True)
                m.then_inc(full, 1)

            def turn_out():
                n, before = USE["o_turn", 0], USE["s_out", 1]
                pe.wait_ge(free[before % 2], freed(before) + 1)
                pe.wait_ge(free[n % 2], freed(n))
                for hd in range(HEADS):
                    t = nc.tensor.transpose(pj[n % 2][:, hd * NS * HEADS:(hd + 1) * NS * HEADS],
                                            xcur[0:NS * HEADS, hd * P:(hd + 1) * P],
                                            const("ident")[0:NS * HEADS, 0:NS * HEADS])
                t.then_inc(full, 1)

            units = [(hd, i) for hd in range(HEADS) for i in range(TB)]
            last_v = USE["v", 4 * BLOCKS - 1]
            all_read(pe, last_v + 1)
            for u in range(len(units) + 3):
                if u == S_TURN:
                    turn_scores()
                if u == P_TURN:
                    turn_probs()
                if u in S_OUT:
                    sample_out(S_OUT[u])
                if u == O_TURN:
                    turn_out()
                if u < len(units):
                    hd, i = units[u]
                    k = (i + 1) * P
                    n = USE["attn", u]
                    pe.wait_ge(free[n % 2], freed(n))
                    for c in range(2):
                        m = mm(pj[n % 2][:, c * 512:c * 512 + k], qT3[c * HD:(c + 1) * HD, hd, i * P:(i + 1) * P],
                               qT3[c * HD:(c + 1) * HD, HEADS + hd, 0:k], start=True, stop=True)
                    m.then_inc(full, 1)
                if 2 <= u <= len(units) + 1:
                    v = u - 2
                    pe.wait_ge(a_w, v + 1)
                    if v >= 2:
                        pe.wait_ge(a_wT, v - 1)
                    for kb in range(units[v][1] + 1):
                        t = nc.tensor.transpose(tp[v % 2][:, kb * P:(kb + 1) * P], wrow[:, v % 2, kb * P:(kb + 1) * P],
                                                const("ident"))
                    t.then_inc(a_wT_ps, 1)
                if u >= 3:
                    v = u - 3
                    hd, i = units[v]
                    pe.wait_ge(a_wT, v + 1)
                    pe.wait_ge(a_ofree, v + 1)
                    for kb in range(i + 1):
                        m = mm(acc[:, (v % 2) * 512:(v % 2) * 512 + P], v_rows[:, kb, hd * P:(hd + 1) * P],
                               wT[:, v % 2, kb * P:(kb + 1) * P], start=(kb == 0), stop=(kb == i))
                    m.then_inc(a_o, 1)
            for hd in range(HEADS):
                n = USE["subln", hd]
                pe.wait_ge(sq_ready, hd + 1)
                pe.wait_ge(free[n % 2], freed(n))
                for g in range(2):
                    m = mm(pj[n % 2][:, PW + G_OFF[g]:PW + G_OFF[g] + G_W[g]], aconst("mean"),
                           squares(hd)[:, G_OFF[g]:G_OFF[g] + G_W[g]], start=True, stop=True)
                m.then_inc(full, 1)

            def key_scores(hd, unit):
                pe.wait_ge(q_staged, unit + 1)
                pe.wait_ge(sc_read, unit + 1)
                for c in range(2):
                    m = mm(tp[0][:, c * P:(c + 1) * P], qst[:, c * P:(c + 1) * P], keys[:, hd * 2 + c, :],
                           start=True, stop=True)
                m.then_inc(sc_ready, 1)

            def start_tile(src, count):
                pe.wait_ge(acc_free, count)
                for half in range(2):
                    mm(acc[:, half * 512:(half + 1) * 512], const("alpha_eye"), src[:, half * 512:(half + 1) * 512],
                       start=True, stop=True, skip_group_check=True)

            def add_four(G, q):
                for r in range(4 * q, 4 * q + 4):
                    pe.wait_ge(diag_ready, G * RING + r + 1)
                    for half in range(2):
                        m = mm(acc[:, half * 512:(half + 1) * 512], diag[:, r % DIAGS, :],
                               uv[:, r, D + half * 512:D + (half + 1) * 512], start=False, stop=True,
                               skip_group_check=True)
                    m.then_inc(slot_done, 1)

            def open_product(x):
                if x.panel is not None:
                    pe.wait_ge(s_panel[x.panel % SLOTS], 16 * (x.panel // SLOTS + 1))
                if x.fence:
                    banks_read(pe, x.n)
                pe.wait_ge(bank_free[x.n % BANKS], bank_freed(x.n))

            def token_major(x, src, chunks, weights):
                m = rows(x.b)
                for c in range(chunks):
                    last = mm(bank[0:m, x.n % BANKS, 0:PW], src[:, c, local(x.b):local(x.b) + m], weights[:, c, :],
                              start=(c == 0), stop=(c == chunks - 1))
                last.then_inc(bank_full, 1)

            def feature_major(x, columns_of):
                w = panel[:, x.panel % SLOTS, :].rearrange("p (c n) -> p c n", c=C)[:, :, columns_of * P:(columns_of + 1) * P]
                for c in range(C):
                    last = mm(bank[:, x.n % BANKS, 0:G_W[x.g]], w[:, c, :], hT[:, c, 0:G_W[x.g]],
                              start=(c == 0), stop=(c == C - 1))
                last.then_inc(bank_full, 1)

            def background(x):
                if x.n is not None:
                    open_product(x)
                    weights = panel[:, (x.panel or 0) % SLOTS, :].rearrange("p (c n) -> p c n", c=C)
                if x.kind == "mix" and x.layer == 0:
                    if x.fence:
                        pe.wait_ge(o_normed, HEADS * (x.g + 1))
                        all_read(pe, len(ORDER))
                    token_major(x, oT[x.g], C, weights)
                elif x.kind == "mix":
                    token_major(x, gx[:, :, 2:2 + G_W[x.g]], C, weights)
                elif x.kind == "turn":
                    if x.ready == "norm":
                        pe.wait_ge(ln_done, x.count)
                    else:
                        pe.wait_ge(ple_done, x.count)
                    m = rows(x.b)
                    for q in range(4):
                        c = 4 * x.half + q
                        last = nc.tensor.transpose(bank[:, x.n % BANKS, q * P:q * P + m], h[0:m, x.b, c * P:(c + 1) * P],
                                                   const("ident")[0:m, 0:m])
                    last.then_inc(bank_full, 1)
                elif x.kind == "pq":
                    feature_major(x, x.f % 2)
                elif x.kind == "conv":
                    feature_major(x, x.i % 2)
                elif x.kind == "gate":
                    token_major(x, hT, C, weights)
                elif x.kind == "proj":
                    pe.wait_ge(s_pT, 16 * x.load)
                    wp = panel[:, x.panel % SLOTS, :].rearrange("p (c n) -> p c n", c=2)
                    token_major(x, pTs, 2, wp[:, :, x.p * PW:(x.p + 1) * PW])
                elif x.kind == "x_spread":
                    mm(bank[:, x.n % BANKS, :], const("spread")[0:NS, :], h[0:NS, TB, x.half * 512:(x.half + 1) * 512],
                       start=True, stop=True).then_inc(bank_full, 1)
                elif x.kind == "i_spread":
                    pe.wait_ge(ig_ready, x.layer + 1)
                    mm(bank[:, x.n % BANKS, 0:256], const("spread")[0:NS, :], x_ig[0:NS, :],
                       start=True, stop=True).then_inc(bank_full, 1)
                elif x.kind == "route" and x.i == 0:
                    if x.b == 0 and x.hd == 0:
                        pe.wait_ge(s_keys, 16 * (x.layer + 1))
                    key_scores(x.hd, x.u)

            for kind, layer, b, lots in steps:
                if kind == "alone":
                    for x in lots[0]:
                        background(x)
                    continue
                if b < TB:
                    pe.wait_ge(x_ready, layer * TB + b + 1)
                    start_tile(xcur, place(layer, b) + 1)
                else:
                    start_tile(h[:, TB, :], place(layer, b) + 1)
                for t, G, q, hd, lot in window_quarters(layer, b, lots):
                    for x in lot:
                        background(x)
                    add_four(G, q)


def weight_panels(i):
    out = np.zeros((len(PANEL_AT), P, C * PW), np.float32)

    def put(name, layer, w):
        for k in range(w.shape[1] // PW):
            if (name, layer, k) in PANEL_AT:
                out[PANEL_AT[name, layer, k]] = w[:, k * PW:(k + 1) * PW].reshape(C, P, PW).transpose(1, 0, 2) \
                    .reshape(P, C * PW)

    qkv = i["w_attn_qkv"][0]
    put("qk", 0, qkv[:, 0:2 * D])
    put("v", 0, qkv[:, 2 * D:3 * D])
    put("mix", 0, i["w_attn_o"][0])
    put("mix", 1, i["w_conv_out"][0])
    for layer in range(DEPTH):
        put("pq", layer, i["w_peer_q"][layer])
        put("gate", layer, i["w_ple_gate"][layer])
        out[PANEL_AT["proj", layer, 0]] = i["w_ple_proj"][layer].reshape(2, P, D).transpose(1, 0, 2).reshape(P, 2 * D)
    w = i["w_conv_in"][0].reshape(D, 3, C, P)[:, [1, 2, 0]].transpose(0, 2, 1, 3).reshape(D, 3 * D)
    put("conv", 1, w)
    return out


def embedding_rows(i):
    p = np.concatenate([i["p_prompt"][:, 0], i["p_sample"][:, :, 0]], axis=1)
    return p.reshape(DEPTH, T, 2, P).transpose(0, 3, 2, 1)


def kernel(**inputs):
    import concourse.bacc as bacc
    from concourse.bass_utils import run_bass_kernel_spmd as run

    i = {k: np.asarray(v) for k, v in inputs.items()}
    h0 = np.concatenate([i["x_prompt"][0], i["x_sample"][:, 0]])
    arrays = {
        "h0": h0,
        "h0T": h0.T.reshape(C, P, T).transpose(1, 0, 2),
        "consts": constants(),
        "panels": weight_panels(i),
        "ple_rows": embedding_rows(i),
        "keysT": i["peer_keys"].transpose(0, 4, 1, 2, 3).reshape(DEPTH, P, 16, KEYS),
        "uv0": np.concatenate([i["peer_u"][0], i["peer_v"][0]], axis=1),
        "uv1": np.concatenate([i["peer_u"][1], i["peer_v"][1]], axis=1),
        "cache_k": i["cache_k"][0].reshape(POOL_PAGES, PAGE, D),
        "cache_v": i["cache_v"][0].reshape(POOL_PAGES, PAGE, D),
        "pages": i["page_table"].reshape(1, NS * N_PAGES),
        "wlam": i["w_attn_lambda"].reshape(1, 4 * HD),
        "subg": i["attn_subln_g"].reshape(P, 1),
        "ln": np.stack([i["ln_g"].reshape(4, D), i["ln_b"].reshape(4, D)], axis=1),
        "convw": i["conv_w"][0].reshape(3, C, P).transpose(2, 0, 1),
        "state_conv": i["state_conv"][0],
        "stateT": i["state_conv"][0].reshape(NS, 2, C, P).transpose(3, 2, 1, 0),
    }
    outs = {"y_p": (SEQ, D), "y_s": (NS, D), "nk_p": (SEQ, D), "nv_p": (SEQ, D), "nk_s": (NS, D), "nv_s": (NS, D),
            "cp": (2, D), "cs": (NS, 2, D)}
    nc = bacc.Bacc("TRN2", target_bir_lowering=False, num_devices=1)
    feed, args = {}, []
    for name, a in arrays.items():
        a = np.ascontiguousarray(a)
        feed["in_" + name] = a
        args.append(nc.dram_tensor("in_" + name, a.shape, mybir.dt.from_np(a.dtype), kind="ExternalInput").ap())
    for name, shape in outs.items():
        args.append(nc.dram_tensor("out_" + name, shape, F32, kind="ExternalOutput").ap())
    build(nc, *args)
    r = run(nc, [feed], core_ids=[0]).results[0]
    return (r["out_y_p"].reshape(1, SEQ, D), r["out_y_s"].reshape(NS, 1, D),
            r["out_nk_p"].reshape(1, 1, SEQ, HEADS, P), r["out_nv_p"].reshape(1, 1, SEQ, HEADS, P),
            r["out_nk_s"].reshape(1, NS, 1, HEADS, P), r["out_nv_s"].reshape(1, NS, 1, HEADS, P),
            r["out_cp"].reshape(1, 1, 2, D), r["out_cs"].reshape(1, NS, 2, D))
```
